# Optimizing a Trainium2 kernel written in Bass

```python
import math
import jax
import jax.numpy as jnp
from jax import lax
import numpy as np

D_MODEL = 1024
BATCH = 1
SEQ = 512
DEPTH = 1
DEC_BATCH = 1
DEC_SEQ = 1024
PAST_LEN = 128

GRID_W = 64
N_ATTN_HEADS = 8
HEAD_DIM = 64
ATTN_WIDTH = N_ATTN_HEADS * HEAD_DIM
WIN_ROWS_MAX = 8
WIN_COLS = 16
CONV_WIDTH = D_MODEL - ATTN_WIDTH
CONV_GROUPS = 8
CONV_K = 31
IN_COLS = 3 * ATTN_WIDTH + 2 * CONV_WIDTH
N_EXPERTS = 16
EC_FACTOR = 2
D_EXPERT = 2816
N_MOD = 6
EPS = 1e-6

kernel_name = "hymba_na_conformer_ec_encoder"

def rms_norm(x, g):
    xf = x.astype(jnp.float32)
    y = xf * lax.rsqrt(jnp.mean(xf * xf, axis=-1, keepdims=True) + EPS)
    return (y * g.astype(jnp.float32)).astype(x.dtype)

def neighbourhood_attention(q, k, v, rpb):
    B, L, H, dh = q.shape
    rows = L // GRID_W
    wr = min(WIN_ROWS_MAX, rows)
    qg = q.reshape(B, rows, GRID_W, H, dh)
    kg = k.reshape(B, rows, GRID_W, H, dh)
    vg = v.reshape(B, rows, GRID_W, H, dh)
    cols = jnp.arange(GRID_W)
    col_start = jnp.clip(cols - WIN_COLS // 2, 0, GRID_W - WIN_COLS)
    col_idx = col_start[:, None] + jnp.arange(WIN_COLS)[None, :]
    col_off = col_idx - cols[:, None] + (WIN_COLS - 1)
    scale = HEAD_DIM ** -0.5

    def one_row(args):
        q_r, r = args
        rs = jnp.clip(r - wr // 2, 0, rows - wr)
        k_blk = lax.dynamic_slice_in_dim(kg, rs, wr, axis=1)
        v_blk = lax.dynamic_slice_in_dim(vg, rs, wr, axis=1)
        k_win = k_blk[:, :, col_idx]
        v_win = v_blk[:, :, col_idx]
        row_off = rs + jnp.arange(wr) - r + (WIN_ROWS_MAX - 1)
        bias = rpb[:, row_off[:, None, None], col_off[None, :, :]]
        bias = jnp.transpose(bias, (0, 2, 1, 3)).astype(jnp.float32)
        s = jnp.einsum('bqhd,brqchd->bhqrc', q_r, k_win).astype(jnp.float32) * scale + bias[None]
        p = jax.nn.softmax(s.reshape(B, H, GRID_W, wr * WIN_COLS), axis=-1)
        p = p.reshape(B, H, GRID_W, wr, WIN_COLS).astype(v.dtype)
        return jnp.einsum('bhqrc,brqchd->bqhd', p, v_win)

    out = lax.map(one_row, (jnp.transpose(qg, (1, 0, 2, 3, 4)), jnp.arange(rows)))
    return jnp.transpose(out, (1, 0, 2, 3, 4)).reshape(B, L, H * dh)

def conformer_conv(a, gt, conv_w, conv_b, conv_ln_g, conv_ln_b):
    B, L, C = a.shape
    u = a * jax.nn.sigmoid(gt)
    u = lax.conv_general_dilated(
        u, conv_w[:, None, :].astype(u.dtype), window_strides=(1,),
        padding=[(CONV_K // 2, CONV_K // 2)], dimension_numbers=('NWC', 'WIO', 'NWC'),
        feature_group_count=C) + conv_b
    uf = u.astype(jnp.float32).reshape(B, L, CONV_GROUPS, C // CONV_GROUPS)
    mu = jnp.mean(uf, axis=-1, keepdims=True)
    var = jnp.mean(jnp.square(uf - mu), axis=-1, keepdims=True)
    un = ((uf - mu) * lax.rsqrt(var + EPS)).reshape(B, L, C)
    un = (un * conv_ln_g.astype(jnp.float32) + conv_ln_b.astype(jnp.float32)).astype(a.dtype)
    return jax.nn.silu(un)

def expert_choice_ffn(h, w_router, w_gate, w_up, w_down):
    B, L, D = h.shape
    n = B * L
    cap = max(1, EC_FACTOR * n // N_EXPERTS)
    hf = h.reshape(n, D)
    aff = jax.nn.softmax((hf @ w_router).astype(jnp.float32), axis=-1)
    g, idx = lax.top_k(aff.T, cap)
    xe = hf[idx]
    hid = jax.nn.silu(jnp.einsum('ecd,edf->ecf', xe, w_gate)) * jnp.einsum('ecd,edf->ecf', xe, w_up)
    ye = jnp.einsum('ecf,efd->ecd', hid, w_down) * g[..., None].astype(h.dtype)
    y = jnp.zeros((n, D), h.dtype).at[idx.reshape(-1)].add(ye.reshape(-1, D))
    return y.reshape(B, L, D)

def encoder_layer(x, c, ada_w, ada_b, norm1_g, w_in, q_norm_g, k_norm_g, rpb,
                  conv_w, conv_b, conv_ln_g, conv_ln_b, w_out, norm2_g,
                  w_router, w_gate, w_up, w_down):
    B, L, D = x.shape
    ada = jax.nn.silu(c) @ ada_w + ada_b
    shift1, scale1, gate1, shift2, scale2, gate2 = [m[:, None, :] for m in jnp.split(ada, N_MOD, axis=-1)]

    h = rms_norm(x, norm1_g) * (1 + scale1) + shift1
    z = h @ w_in
    q, k, v, ca, cg = jnp.split(
        z, [ATTN_WIDTH, 2 * ATTN_WIDTH, 3 * ATTN_WIDTH, 3 * ATTN_WIDTH + CONV_WIDTH], axis=-1)
    q = rms_norm(q.reshape(B, L, N_ATTN_HEADS, HEAD_DIM), q_norm_g)
    k = rms_norm(k.reshape(B, L, N_ATTN_HEADS, HEAD_DIM), k_norm_g)
    v = v.reshape(B, L, N_ATTN_HEADS, HEAD_DIM)
    attn_out = neighbourhood_attention(q, k, v, rpb)
    conv_out = conformer_conv(ca, cg, conv_w, conv_b, conv_ln_g, conv_ln_b)
    mix = jnp.concatenate([attn_out, conv_out], axis=-1) @ w_out
    x = x + gate1 * mix

    h2 = rms_norm(x, norm2_g) * (1 + scale2) + shift2
    x = x + gate2 * expert_choice_ffn(h2, w_router, w_gate, w_up, w_down)
    return x

def setup_inputs(seed: int = 0) -> dict:
    key = jax.random.key(seed)
    ks = jax.random.split(key, 24)
    f32 = jnp.float32
    nrm = lambda k, shape, s: (jax.random.normal(k, shape, f32) * s).astype(f32)
    return {
        "x_prompt": nrm(ks[0], (BATCH, SEQ, D_MODEL), 1.0),
        "x_sample": nrm(ks[1], (DEC_BATCH, DEC_SEQ, D_MODEL), 1.0),
        "c_prompt": nrm(ks[2], (BATCH, D_MODEL), 1.0),
        "c_sample": nrm(ks[3], (DEC_BATCH, D_MODEL), 1.0),
        "ada_w": nrm(ks[4], (D_MODEL, N_MOD * D_MODEL), 0.5 * D_MODEL ** -0.5),
        "ada_b": nrm(ks[5], (N_MOD * D_MODEL,), 0.01),
        "norm1_g": 1.0 + nrm(ks[6], (D_MODEL,), 0.01),
        "w_in": nrm(ks[7], (D_MODEL, IN_COLS), D_MODEL ** -0.5),
        "q_norm_g": 1.0 + nrm(ks[8], (HEAD_DIM,), 0.01),
        "k_norm_g": 1.0 + nrm(ks[9], (HEAD_DIM,), 0.01),
        "rpb": nrm(ks[10], (N_ATTN_HEADS, 2 * WIN_ROWS_MAX - 1, 2 * WIN_COLS - 1), 0.1),
        "conv_w": nrm(ks[11], (CONV_K, CONV_WIDTH), CONV_K ** -0.5),
        "conv_b": nrm(ks[12], (CONV_WIDTH,), 0.01),
        "conv_ln_g": 1.0 + nrm(ks[13], (CONV_WIDTH,), 0.01),
        "conv_ln_b": nrm(ks[14], (CONV_WIDTH,), 0.01),
        "w_out": nrm(ks[15], (D_MODEL, D_MODEL), D_MODEL ** -0.5),
        "norm2_g": 1.0 + nrm(ks[16], (D_MODEL,), 0.01),
        "w_router": nrm(ks[17], (D_MODEL, N_EXPERTS), D_MODEL ** -0.5),
        "w_gate": nrm(ks[18], (N_EXPERTS, D_MODEL, D_EXPERT), D_MODEL ** -0.5),
        "w_up": nrm(ks[19], (N_EXPERTS, D_MODEL, D_EXPERT), D_MODEL ** -0.5),
        "w_down": nrm(ks[20], (N_EXPERTS, D_EXPERT, D_MODEL), D_EXPERT ** -0.5),
    }

def reference(x_prompt, x_sample, c_prompt, c_sample, ada_w, ada_b, norm1_g, w_in,
              q_norm_g, k_norm_g, rpb, conv_w, conv_b, conv_ln_g, conv_ln_b, w_out,
              norm2_g, w_router, w_gate, w_up, w_down):
    y_prompt = x_prompt
    y_sample = x_sample
    for _ in range(DEPTH):
        y_prompt = encoder_layer(y_prompt, c_prompt, ada_w, ada_b, norm1_g, w_in, q_norm_g, k_norm_g, rpb,
                                 conv_w, conv_b, conv_ln_g, conv_ln_b, w_out, norm2_g,
                                 w_router, w_gate, w_up, w_down)
        y_sample = encoder_layer(y_sample, c_sample, ada_w, ada_b, norm1_g, w_in, q_norm_g, k_norm_g, rpb,
                                 conv_w, conv_b, conv_ln_g, conv_ln_b, w_out, norm2_g,
                                 w_router, w_gate, w_up, w_down)
    return (y_prompt, y_sample)


_drawn_inputs = setup_inputs


def setup_inputs(seed=0):
    import zlib

    import numpy as np

    out = dict(_drawn_inputs(seed))
    spreads = {}
    factors = {'ada_b': 6.957,
     'norm1_g': 8.0,
     'q_norm_g': 8.0,
     'k_norm_g': 8.0,
     'rpb': 8.0,
     'conv_b': 8.0,
     'conv_ln_g': 8.0,
     'conv_ln_b': 29.766,
     'norm2_g': 8.0}
    for name, (base, spread) in spreads.items():
        noise = np.random.default_rng([zlib.crc32(name.encode()), seed]).standard_normal(out[name].shape)
        drawn = base * np.exp(spread * noise) if base else spread * noise
        out[name] = jnp.asarray(drawn.astype(out[name].dtype))
    for name, factor in factors.items():
        out[name] = (out[name] * factor).astype(out[name].dtype)
    return out
```

```python
from contextlib import ExitStack

import numpy as np

import concourse.bass as bass
from concourse import mybir

F32 = mybir.dt.float32
F32R = mybir.dt.float32r
U32 = mybir.dt.uint32
ALU = mybir.AluOpType
ACT = mybir.ActivationFunctionType
AX = mybir.AxisListType

P = 128
D = 1024
KD = D // P
PROMPT, SAMPLE = 512, 1024
TOKENS = PROMPT + SAMPLE
TILES = TOKENS // P
NCH = TOKENS // 512
MODS = 6
HEADS, DH = 8, 64
WA = HEADS * DH
WC = D - WA
IN_COLS = 3 * WA + 2 * WC
GRID_W, WIN_ROWS, WIN_COLS = 64, 8, 16
CONV_K = 31
PAD = CONV_K // 2
EXPERTS, FACTOR, FF = 16, 2, 2816
EPS = 1e-6
CAP_P = FACTOR * PROMPT // EXPERTS
CAP_S = FACTOR * SAMPLE // EXPERTS
CAP = CAP_P + CAP_S
FT = FF // P
CHUNKS = FT // 2
NEG = -1e30

Q_COLS, K_COLS = 16, 32
COL_BLOCKS = GRID_W // Q_COLS
KEY_COL0 = [min(max(Q_COLS * j - WIN_COLS // 2, 0), GRID_W - K_COLS) for j in range(COL_BLOCKS)]
ROW_SETS = [(0, 0, 0, 8, 8, 0), (PROMPT, 0, 0, 12, 16, 256), (PROMPT, 8, 4, 12, 16, 640)]
PATTERN = [0, 1, 1, 2]
BIAS_COLS = 1024
BLOCKS = [(s, j) for s in range(3) for j in range(COL_BLOCKS)]
V_ROWS = [(0, 0), (0, 4), (PROMPT, 0), (PROMPT, 4), (PROMPT, 8), (PROMPT, 12)]


def group(tile):
    return 0 if tile * P < PROMPT else 1


def program(nc, A, outs):
    g = ExitStack()
    sems = {}

    def sem(name):
        if name not in sems:
            sems[name] = g.enter_context(nc.semaphore(name))
        return sems[name]

    def dram(name, shape):
        return nc.dram_tensor(name, shape, F32, kind="Internal").ap()

    ada_d = dram("ada_d", [2, MODS * D])
    qk_d = dram("qk_d", [8, P, TOKENS])
    conv_d = dram("conv_d", [4, P, TOKENS])
    v_d = dram("v_d", [TOKENS, WA])
    xhat_d = dram("xhat_d", [TOKENS, D])
    y_d = [outs[0].rearrange("b l d -> (b l) d"), outs[1].rearrange("b l d -> (b l) d")]
    x_d = [A["x_prompt"].rearrange("b l d -> (b l) d"), A["x_sample"].rearrange("b l d -> (b l) d")]

    def rows_of(pair, t):
        r = t * P if group(t) == 0 else t * P - PROMPT
        return pair[group(t)][r:r + P, :]

    def sb(ctx, name, shape, dt=F32):
        return ctx.enter_context(nc.sbuf_tensor(name, shape, dt))

    def ps(ctx, name, shape):
        return ctx.enter_context(nc.psum_tensor(name, shape, F32))

    with g:
        ident = sb(g, "ident", [P, P])
        ones64 = sb(g, "ones64", [P, P])
        eps_col = sb(g, "eps_col", [P, 1])
        vecs = sb(g, "vecs", [P, 32])
        convp = sb(g, "convp", [P, 4, CONV_K + 3])
        qkg = sb(g, "qkg", [P, 2])
        modv = sb(g, "modv", [P, 2, 4, KD])
        a1 = sb(g, "a1", [P, 2, KD])
        a2 = sb(g, "a2", [P, 2, KD])
        rstd1 = sb(g, "rstd1", [P, TILES])

        condition(nc, A, g, sem, sb, ps, ada_d, rows_of, x_d,
                  ident, ones64, eps_col, vecs, convp, qkg, modv, a1, a2, rstd1)
        project(nc, A, sem, sb, ps, rows_of, x_d, qk_d, conv_d, v_d,
                ident, ones64, eps_col, convp, qkg, modv, a1, rstd1)
        affT = sb(g, "affT", [48, SAMPLE])
        o_ctx = ExitStack()
        with o_ctx:
            o_nat = sb(o_ctx, "o_nat", [P, len(BLOCKS), WA])
            attend(nc, A, sem, sb, ps, qk_d, v_d, ident, o_nat)
            mix(nc, A, sem, sb, ps, rows_of, x_d, y_d, ada_d, conv_d, xhat_d, ident, eps_col, modv, a2, affT, o_nat)
        experts(nc, A, sem, sb, ps, y_d, ada_d, xhat_d, ident, modv, a2, affT)


def condition(nc, A, g, sem, sb, ps, ada_d, rows_of, x_d,
              ident, ones64, eps_col, vecs, convp, qkg, modv, a1, a2, rstd1):
    NJ = MODS * D // 512
    RING, XR = 3, 3
    consts = sem("consts_loaded")
    c_loaded, cs_ready = sem("c_loaded"), sem("cs_ready")
    w_loaded = [sem(f"ada_w_loaded{i}") for i in range(RING)]
    x_loaded = [sem(f"x_loaded{i}") for i in range(XR)]
    mm_done, ada_row, ada_stored, mod_loaded = sem("ada_mm"), sem("ada_row"), sem("ada_stored"), sem("mod_loaded")
    sq_done, ms_done, rt_done, rstd_done, a_ready = (
        sem("x_sq"), sem("x_ms"), sem("x_rt"), sem("rstd1_done"), sem("a_ready"))
    eps_set = sem("eps_set")
    with ExitStack() as c:
        cT = sb(c, "cT", [P, 2, KD])
        cs = sb(c, "cs", [P, 2, KD])
        aw = sb(c, "aw", [P, RING, KD, 512])
        ada_b2 = sb(c, "ada_b2", [2, MODS * D])
        ada_sb = sb(c, "ada_sb", [2, MODS * D])
        xt = sb(c, "xt0", [P, XR, D])
        junk = sb(c, "junk0", [P, 2, D])
        ss = sb(c, "ss", [P, TILES])
        psA = ps(c, "psA", [P, 2, 512])
        w_v = A["ada_w"].rearrange("(p k) n -> p k n", k=KD)
        CONSTS = 16 * 8

        with nc.Block() as block:
            @block.sync
            def _(sp):
                for i, name in enumerate(("c_prompt", "c_sample")):
                    sp.dma_start(cT[:, i, :], A[name].rearrange("b (p k) -> (b p) k", k=KD)).then_inc(c_loaded, 16)
                for j in range(NJ):
                    if j >= RING:
                        sp.wait_ge(mm_done, j - RING + 1)
                    sp.dma_start(aw[:, j % RING], w_v[:, :, j * 512:(j + 1) * 512]).then_inc(w_loaded[j % RING], 16)
                sp.wait_ge(ada_row, NJ)
                sp.dma_start(ada_d, ada_sb[:, :]).then_inc(ada_stored, 16)
                sp.wait_ge(ada_stored, 16)
                for grp in range(2):
                    for v, m in enumerate((0, 1, 3, 4)):
                        sp.dma_start(modv[:, grp, v, :],
                                     ada_d[grp, m * D:(m + 1) * D].rearrange("(p k) -> p k", k=KD)).then_inc(mod_loaded, 16)
                sp.wait_ge(mod_loaded, 16 * 8)

            @block.gpsimd
            def _(pool):
                pool.memset(eps_col[:, :], EPS).then_inc(eps_set, 1)

            def square(act, t):
                act.wait_ge(x_loaded[t % XR], 16 * (t // XR + 1))
                if t >= 2:
                    act.wait_ge(sq_done, t - 1)
                act.activation(junk[:, t % 2, :], xt[:, t % XR, :], ACT.Square,
                               accum_out=ss[:, t:t + 1]).then_inc(sq_done, 1)

            @block.scalar
            def _(act):
                act.dma_start(ident[:, :], A["ident"]).then_inc(consts, 16)
                act.dma_start(ones64[:, :], A["ones64"]).then_inc(consts, 16)
                act.dma_start(vecs[:, 0:KD], A["norm1_g"].rearrange("(p k) -> p k", k=KD)).then_inc(consts, 16)
                act.dma_start(vecs[:, KD:2 * KD], A["norm2_g"].rearrange("(p k) -> p k", k=KD)).then_inc(consts, 16)
                act.dma_start(convp[:, :, :], A["conv_pack"]).then_inc(consts, 16)
                act.dma_start(qkg[:, :], A["qk_gain"]).then_inc(consts, 16)
                act.dma_start(ada_b2[0:1, :], A["ada_b"].rearrange("(a n) -> a n", a=1)).then_inc(consts, 16)
                act.dma_start(ada_b2[1:2, :], A["ada_b"].rearrange("(a n) -> a n", a=1)).then_inc(consts, 16)
                act.wait_ge(c_loaded, 32)
                act.activation(cs[:, :, :], cT[:, :, :], ACT.Silu).then_inc(cs_ready, 1)
                for t in range(TILES):
                    if t >= XR:
                        act.wait_ge(sq_done, t - XR + 1)
                    act.dma_start(xt[:, t % XR, :], rows_of(x_d, t)).then_inc(x_loaded[t % XR], 16)
                    if t >= 1:
                        square(act, t - 1)
                square(act, TILES - 1)
                act.wait_ge(ms_done, 1)
                act.activation(ss[:, :], ss[:, :], ACT.Sqrt).then_inc(rt_done, 1)

            @block.tensor
            def _(pe):
                pe.wait_ge(cs_ready, 1)
                for j in range(NJ):
                    pe.wait_ge(w_loaded[j % RING], 16 * (j // RING + 1))
                    if j >= 2:
                        pe.wait_ge(ada_row, j - 1)
                    for k in range(KD):
                        mm = pe.matmul(psA[0:2, j % 2, :], cs[:, :, k], aw[:, j % RING, k, :],
                                       start=(k == 0), stop=(k == KD - 1))
                    mm.then_inc(mm_done, 1)

            @block.vector
            def _(dve):
                dve.wait_ge(consts, CONSTS)
                for j in range(NJ):
                    dve.wait_ge(mm_done, j + 1)
                    dve.tensor_tensor(ada_sb[:, j * 512:(j + 1) * 512], psA[0:2, j % 2, :],
                                      ada_b2[:, j * 512:(j + 1) * 512], ALU.add).then_inc(ada_row, 1)
                dve.wait_ge(sq_done, TILES)
                dve.tensor_scalar(ss[:, :], ss[:, :], 1.0 / D, EPS, ALU.mult, ALU.add).then_inc(ms_done, 1)
                dve.wait_ge(rt_done, 1)
                dve.reciprocal(rstd1[:, :], ss[:, :]).then_inc(rstd_done, 1)
                dve.wait_ge(mod_loaded, 16 * 8)
                for grp in range(2):
                    dve.scalar_tensor_tensor(out=a1[:, grp, :], in0=modv[:, grp, 1, :], scalar=1.0,
                                             in1=vecs[:, 0:KD], op0=ALU.add, op1=ALU.mult).then_inc(a_ready, 1)
                    dve.scalar_tensor_tensor(out=a2[:, grp, :], in0=modv[:, grp, 3, :], scalar=1.0,
                                             in1=vecs[:, KD:2 * KD], op0=ALU.add, op1=ALU.mult).then_inc(a_ready, 1)


Z_TILES = ([("gate", j) if s == 0 else ("value", j) for j in range(4) for s in range(2)]
           + [("q", j) for j in range(4)] + [("k", j) for j in range(4)] + [("v", j) for j in range(4)])
Z_COL0 = {"q": 0, "k": WA, "v": 2 * WA, "value": 3 * WA, "gate": 3 * WA + WC}
NZ = len(Z_TILES)
TAPS_STEP = 9
CONV_DONE = [2 + (CONV_K * (j + 1) - 1) // TAPS_STEP for j in range(4)]


def side_jobs():
    jobs = {s: [] for s in range(NZ + 3)}
    for i, (kind, j) in enumerate(Z_TILES):
        if kind in "qkv":
            jobs[i + 1] += [("turn" if kind == "v" else "ss", i, n) for n in range(NCH)]
    for j in range(4):
        m = CONV_DONE[j] + 1
        jobs[m] += [("mean", j, n) for n in range(NCH)]
        jobs[m + 1] += [("var", j, n) for n in range(NCH)]
    return jobs


def project(nc, A, sem, sb, ps, rows_of, x_d, qk_d, conv_d, v_d,
            ident, ones64, eps_col, convp, qkg, modv, a1, rstd1):
    XR, WR = 2, 3
    jobs = side_jobs()
    flat = [(s, job) for s in sorted(jobs) for job in jobs[s]]
    index = {job: i for i, (s, job) in enumerate(flat)}
    x_loaded = [sem(f"x1_loaded{i}") for i in range(XR)]
    xn_ready, xT_done, h_hi_ready, h_lo_ready = sem("xn_ready"), sem("xT_done"), sem("h_hi_ready"), sem("h_lo_ready")
    h_mod = sem("h_mod")
    w_loaded = [sem(f"w_in_loaded{i}") for i in range(WR)]
    w_hi_ready, w_lo_ready, z_done = sem("w_in_hi"), sem("w_in_lo"), sem("z_done")
    z_act, z_dve = sem("z_out_act"), sem("z_out_dve")
    side_done = sem("side_done")
    side_act = sem("side_out_act")
    pads_set, conv_s, conv_p = sem("pads_set"), sem("conv_sample_taps"), sem("conv_prompt_taps")
    ln_cent, ln_sq, ln_r, ln_norm, ln_out = sem("ln_centred"), sem("ln_square"), sem("ln_rstd"), sem("ln_normed"), sem("ln_out")
    ln_log, qk_log, qk_r, qk_out, v_out = sem("ln_log"), sem("qk_log"), sem("qk_rstd"), sem("qk_out"), sem("v_out")
    stored = [sem(f"z_stored{i}") for i in range(3)]
    conv_mul = sem("conv_prompt_products")

    acts = [1 if kind in ("gate", "q", "k", "v") else 0 for kind, _ in Z_TILES]
    dves = [1 if kind in ("value", "q", "k") else 0 for kind, _ in Z_TILES]
    s_act = [1 if job[0] in ("var", "ss") else 0 for _, job in flat]
    stores = []
    for s in range(NZ + 3):
        if s - 1 < NZ and s >= 1 and Z_TILES[s - 1][0] in "qk":
            stores.append((s, "qk", s - 1))
        if s - 1 < NZ and s >= 1 and Z_TILES[s - 1][0] == "v":
            stores.append((s, "v", s - 1))
        for j in range(4):
            if s == CONV_DONE[j] + 2:
                stores.append((s, "conv", j))
    store_no = {(what, i): n for n, (_, what, i) in enumerate(stores)}

    with ExitStack() as c:
        h_hi = sb(c, "h_hi", [P, KD, TOKENS], F32R)
        h_lo = sb(c, "h_lo", [P, KD, TOKENS], F32R)
        psZ = ps(c, "psZ", [P, 6, 512])
        psS = ps(c, "psS", [P, 2, 512])
        with ExitStack() as c2:
            xt = sb(c2, "xt1", [P, XR, D])
            xn = sb(c2, "xn", [P, 2, D])
            hm = sb(c2, "hm", [P, 2, KD, P])
            with nc.Block() as block:
                @block.sync
                def _(sp):
                    for t in range(TILES):
                        if t >= XR:
                            sp.wait_ge(xn_ready, t - XR + 1)
                        sp.dma_start(xt[:, t % XR, :], rows_of(x_d, t)).then_inc(x_loaded[t % XR], 16)

                @block.vector
                def _(dve):
                    for t in range(TILES + 1):
                        if t < TILES:
                            dve.wait_ge(x_loaded[t % XR], 16 * (t // XR + 1))
                            if t >= 2:
                                dve.wait_ge(xT_done, t - 1)
                            dve.tensor_scalar(xn[:, t % 2, :], xt[:, t % XR, :], rstd1[:, t:t + 1], None,
                                              ALU.mult).then_inc(xn_ready, 1)
                        if t >= 1:
                            u = t - 1
                            dve.wait_ge(h_hi_ready, u + 1)
                            dve.tensor_tensor(h_lo[:, :, u * P:(u + 1) * P], hm[:, u % 2],
                                              h_hi[:, :, u * P:(u + 1) * P].bitcast(F32),
                                              ALU.subtract).then_inc(h_lo_ready, 1)

                @block.tensor
                def _(pe):
                    for t in range(TILES):
                        pe.wait_ge(xn_ready, t + 1)
                        if t >= 2:
                            pe.wait_ge(h_mod, t - 1)
                        xk = xn[:, t % 2, :].rearrange("p (d k) -> p k d", k=KD)
                        for k in range(KD):
                            mm = pe.transpose(psZ[:, 2 * (t % 2) + k // 4, (k % 4) * P:(k % 4 + 1) * P],
                                              xk[:, k, :], ident[:, :])
                        mm.then_inc(xT_done, 1)

                @block.scalar
                def _(act):
                    for t in range(TILES):
                        act.wait_ge(xT_done, t + 1)
                        if t >= 2:
                            act.wait_ge(h_lo_ready, t - 1)
                        for k in range(KD):
                            m = act.activation(hm[:, t % 2, k, :],
                                               psZ[:, 2 * (t % 2) + k // 4, (k % 4) * P:(k % 4 + 1) * P], ACT.Identity,
                                               bias=modv[:, group(t), 0, k:k + 1], scale=a1[:, group(t), k:k + 1])
                        m.then_inc(h_mod, 1)
                        act.wait_ge(h_mod, t + 1)
                        act.activation(h_hi[:, :, t * P:(t + 1) * P], hm[:, t % 2], ACT.Copy).then_inc(h_hi_ready, 1)

        with ExitStack() as c2:
            w_raw = sb(c2, "w_raw", [P, WR, KD, P])
            w_hi = sb(c2, "w_hi", [P, 2, KD, P], F32R)
            w_lo = sb(c2, "w_lo", [P, 2, KD, P], F32R)
            sg = sb(c2, "sg", [P, TOKENS])
            UW = TOKENS + 4 * PAD
            u = sb(c2, "u", [P, 3, UW])
            acc = sb(c2, "acc", [P, 2, TOKENS])
            sqz = sb(c2, "sqz", [P, 2, TOKENS])
            zg = sb(c2, "zg", [P, 2, TOKENS])
            rr = sb(c2, "rr", [P, TOKENS])
            U_P, U_S = 0, PROMPT + 2 * PAD

            w_v = A["w_in"].rearrange("(p k) n -> p k n", k=KD)
            prod = sb(c2, "prod", [P, 2, PROMPT])
            lnr = sb(c2, "lnr", [P, TOKENS])

            def chunk(n):
                return slice(n * 512, (n + 1) * 512)

            def by_block(ap):
                return ap.rearrange("p (r j c) -> p j r c", j=COL_BLOCKS, c=Q_COLS)

            with nc.Block() as block:
                @block.sync
                def _(sp):
                    def load(ct):
                        if ct >= WR:
                            sp.wait_ge(w_lo_ready, ct - WR + 1)
                        kind, j = Z_TILES[ct]
                        col = Z_COL0[kind] + j * P
                        sp.dma_start(w_raw[:, ct % WR], w_v[:, :, col:col + P]).then_inc(w_loaded[ct % WR], 16)
                    for ct in range(WR):
                        load(ct)
                    loads, n = WR, 0
                    for s in range(NZ + 3):
                        if 2 <= s and loads < NZ:
                            load(loads)
                            loads += 1
                        while n < len(stores) and stores[n][0] == s:
                            _, what, i = stores[n]
                            if what == "qk":
                                sp.wait_ge(qk_out, NCH * (sum(1 for k, _ in Z_TILES[:i + 1] if k in "qk")))
                                sp.dma_start(qk_d[(0 if Z_TILES[i][0] == "q" else 4) + Z_TILES[i][1]],
                                             zg[:, i % 2, :]).then_inc(stored[n % 3], 16)
                            elif what == "v":
                                sp.wait_ge(v_out, NCH * (Z_TILES[i][1] + 1))
                                sp.dma_start(v_d.rearrange("(t p) c -> p t c", p=P)[:, :, Z_TILES[i][1] * P:(Z_TILES[i][1] + 1) * P],
                                             zg[:, i % 2, :].rearrange("p (t c) -> p t c", c=P)).then_inc(stored[n % 3], 16)
                            else:
                                sp.wait_ge(ln_out, i + 1)
                                sp.dma_start(conv_d[i], acc[:, i % 2, :]).then_inc(stored[n % 3], 16)
                            n += 1
                    while loads < NZ:
                        load(loads)
                        loads += 1
                    for i in range(3):
                        sp.wait_ge(stored[i], 16 * len([1 for n in range(len(stores)) if n % 3 == i]))

                def wait_store(eng, what, i):
                    n = store_no[(what, i)]
                    eng.wait_ge(stored[n % 3], 16 * (n // 3 + 1))

                @block.tensor
                def _(pe):
                    done = [0]

                    def side(job):
                        i = index[job]
                        if i >= 2:
                            was, wj, wn = flat[i - 2][1]
                            if was in ("var", "ss"):
                                pe.wait_ge(side_act, sum(s_act[:i - 1]))
                            elif was == "mean":
                                pe.wait_ge(ln_cent, NCH * wj + wn + 1)
                            else:
                                pe.wait_ge(v_out, NCH * Z_TILES[wj][1] + wn + 1)
                        kind, j, n = job
                        bank = psS[:, i % 2, :]
                        if kind == "mean":
                            pe.wait_ge(conv_s, CONV_K * (j + 1))
                            pe.wait_ge(conv_p, CONV_K * (j + 1))
                            mm = pe.matmul(bank, ones64[:, :], acc[:, j % 2, chunk(n)], start=True, stop=True)
                        elif kind == "var":
                            pe.wait_ge(ln_sq, NCH * j + n + 1)
                            mm = pe.matmul(bank, ones64[:, :], lnr[:, chunk(n)], start=True, stop=True)
                        elif kind == "ss":
                            pe.wait_ge(z_act, sum(acts[:j + 1]))
                            mm = pe.matmul(bank, ones64[:, :], sqz[:, j % 2, chunk(n)], start=True, stop=True)
                        else:
                            pe.wait_ge(z_act, sum(acts[:j + 1]))
                            for b in range(4):
                                mm = pe.transpose(bank[:, b * P:(b + 1) * P],
                                                  sqz[:, j % 2, (4 * n + b) * P:(4 * n + b + 1) * P], ident[:, :])
                        mm.then_inc(side_done, 1)
                        assert i == done[0]
                        done[0] += 1

                    for s in range(NZ + 3):
                        todo = list(jobs[s])
                        per = -(-len(todo) // NCH)
                        for n in range(NCH):
                            if s < NZ:
                                if n == 0:
                                    pe.wait_ge(w_lo_ready, s + 1)
                                    if s >= 2:
                                        if acts[s - 2]:
                                            pe.wait_ge(z_act, sum(acts[:s - 1]))
                                        if dves[s - 2]:
                                            pe.wait_ge(z_dve, sum(dves[:s - 1]))
                                bank = psZ[:, 3 * (s % 2) + n, :]
                                for k in range(KD):
                                    pe.matmul(bank, w_hi[:, s % 2, k, :], h_hi[:, k, chunk(n)], start=(k == 0), stop=False)
                                    pe.matmul(bank, w_hi[:, s % 2, k, :], h_lo[:, k, chunk(n)], start=False, stop=False)
                                    mm = pe.matmul(bank, w_lo[:, s % 2, k, :], h_hi[:, k, chunk(n)], start=False,
                                                   stop=(k == KD - 1))
                                if n == NCH - 1:
                                    mm.then_inc(z_done, 1)
                            for job in todo[per * n:per * (n + 1)]:
                                side(job)

                @block.scalar
                def _(act):
                    def hi(ct):
                        act.wait_ge(w_loaded[ct % WR], 16 * (ct // WR + 1))
                        if ct >= 2:
                            act.wait_ge(z_done, ct - 1)
                        act.activation(w_hi[:, ct % 2], w_raw[:, ct % WR], ACT.Copy).then_inc(w_hi_ready, 1)

                    hi(0)
                    for s in range(NZ + 3):
                        if s + 1 < NZ:
                            hi(s + 1)
                        for job in jobs[s]:
                            kind, j, n = job
                            i = index[job]
                            if kind == "mean":
                                act.wait_ge(ln_cent, NCH * j + n + 1)
                                if j >= 1:
                                    act.wait_ge(ln_norm, NCH * j)
                                act.activation(lnr[:, chunk(n)], acc[:, j % 2, chunk(n)], ACT.Square).then_inc(ln_sq, 1)
                            elif kind == "var":
                                act.wait_ge(side_done, i + 1)
                                act.activation(lnr[:, chunk(n)], psS[:, i % 2, :], ACT.Ln, bias=eps_col[:, :]).then_inc(side_act, 1)
                                act.wait_ge(side_act, sum(s_act[:i + 1]))
                                act.activation(lnr[:, chunk(n)], lnr[:, chunk(n)], ACT.Exp, scale=-0.5).then_inc(ln_r, 1)
                            elif kind == "ss":
                                act.wait_ge(side_done, i + 1)
                                before = sum(1 for k, _ in Z_TILES[:j] if k in "qk")
                                if before:
                                    act.wait_ge(qk_out, NCH * (before - 1) + n + 1)
                                act.activation(rr[:, chunk(n)], psS[:, i % 2, :], ACT.Ln, bias=eps_col[:, :]).then_inc(side_act, 1)
                                act.wait_ge(side_act, sum(s_act[:i + 1]))
                                act.activation(rr[:, chunk(n)], rr[:, chunk(n)], ACT.Exp, scale=-0.5).then_inc(qk_r, 1)
                        for j in range(4):
                            if s == CONV_DONE[j] + 2:
                                act.wait_ge(ln_norm, NCH * (j + 1))
                                act.activation(acc[:, j % 2, :], acc[:, j % 2, :], ACT.Silu, bias=convp[:, j, CONV_K + 2:CONV_K + 3],
                                               scale=convp[:, j, CONV_K + 1:CONV_K + 2]).then_inc(ln_out, 1)
                        if s < NZ:
                            kind, j = Z_TILES[s]
                            prods = psZ[:, 3 * (s % 2):3 * (s % 2) + 3, :].rearrange("p a b -> p (a b)")
                            if kind != "value":
                                act.wait_ge(z_done, s + 1)
                            if kind == "gate":
                                if j >= 1:
                                    act.wait_ge(z_dve, j)
                                act.activation(sg[:, :], prods, ACT.Sigmoid).then_inc(z_act, 1)
                            elif kind in "qk":
                                act.activation(sqz[:, s % 2, :], prods, ACT.Square).then_inc(z_act, 1)
                            elif kind == "v":
                                act.activation(sqz[:, s % 2, :], prods, ACT.Copy).then_inc(z_act, 1)

                def tap(eng, lo, n, at, j, t, counter):
                    src = u[:, j % 3, at + t:at + t + n]
                    dst = acc[:, j % 2, lo:lo + n]
                    if t == 0:
                        eng.tensor_scalar(dst, src, convp[:, j, 0:1], convp[:, j, CONV_K:CONV_K + 1],
                                          ALU.mult, ALU.add).then_inc(counter, 1)
                    elif counter is conv_s:
                        eng.wait_ge(counter, CONV_K * j + t)
                        eng.scalar_tensor_tensor(out=dst, in0=src, scalar=convp[:, j, t:t + 1], in1=dst,
                                                 op0=ALU.mult, op1=ALU.add).then_inc(counter, 1)
                    else:
                        if t >= 3:
                            eng.wait_ge(counter, CONV_K * j + t - 1)
                        eng.tensor_scalar(prod[:, t % 2, :], src, convp[:, j, t:t + 1], None, ALU.mult).then_inc(conv_mul, 1)
                        eng.wait_ge(conv_mul, (CONV_K - 1) * j + t)
                        eng.wait_ge(counter, CONV_K * j + t)
                        eng.tensor_tensor(dst, dst, prod[:, t % 2, :], ALU.add).then_inc(counter, 1)

                @block.gpsimd
                def _(pool):
                    for b in range(3):
                        for at in (U_P, U_P + PAD + PROMPT, U_S, U_S + PAD + SAMPLE):
                            m = pool.memset(u[:, b, at:at + PAD], 0.0)
                    m.then_inc(pads_set, 1)
                    pool.wait_ge(pads_set, 1)
                    for j in range(4):
                        pool.wait_ge(z_dve, j + 1)
                        if j >= 2:
                            wait_store(pool, "conv", j - 2)
                        for t in range(CONV_K):
                            tap(pool, 0, PROMPT, U_P, j, t, conv_p)

                @block.vector
                def _(dve):
                    def lo(ct):
                        dve.wait_ge(w_hi_ready, ct + 1)
                        dve.tensor_tensor(w_lo[:, ct % 2], w_raw[:, ct % WR], w_hi[:, ct % 2].bitcast(F32),
                                          ALU.subtract).then_inc(w_lo_ready, 1)
                    lo(0)
                    taps = 0
                    dve.wait_ge(pads_set, 1)
                    for s in range(NZ + 3):
                        if s + 1 < NZ:
                            lo(s + 1)
                        if s >= 2:
                            for _ in range(TAPS_STEP):
                                if taps < 4 * CONV_K:
                                    j, t = divmod(taps, CONV_K)
                                    if t == 0:
                                        dve.wait_ge(z_dve, j + 1)
                                        if j >= 2:
                                            wait_store(dve, "conv", j - 2)
                                    tap(dve, PROMPT, SAMPLE, U_S, j, t, conv_s)
                                    taps += 1
                        for job in jobs[s]:
                            kind, j, n = job
                            i = index[job]
                            if kind == "mean":
                                dve.wait_ge(side_done, i + 1)
                                dve.tensor_tensor(acc[:, j % 2, chunk(n)], acc[:, j % 2, chunk(n)], psS[:, i % 2, :],
                                                  ALU.subtract).then_inc(ln_cent, 1)
                            elif kind == "var":
                                dve.wait_ge(ln_r, NCH * j + n + 1)
                                dve.tensor_tensor(acc[:, j % 2, chunk(n)], acc[:, j % 2, chunk(n)], lnr[:, chunk(n)],
                                                  ALU.mult).then_inc(ln_norm, 1)
                            elif kind == "ss":
                                before = sum(1 for k, _ in Z_TILES[:j] if k in "qk")
                                dve.wait_ge(z_dve, sum(dves[:j + 1]))
                                dve.wait_ge(qk_r, NCH * before + n + 1)
                                out, r = zg[:, j % 2, chunk(n)], rr[:, chunk(n)]
                                if Z_TILES[j][0] == "q":
                                    out, r = out.rearrange("p (j r c) -> p j r c", j=COL_BLOCKS, c=Q_COLS), by_block(r)
                                dve.tensor_tensor(out, out, r, ALU.mult).then_inc(qk_out, 1)
                            else:
                                dve.wait_ge(side_done, i + 1)
                                if n == 0:
                                    wait_store(dve, "v" if Z_TILES[j - 2][0] == "v" else "qk", j - 2)
                                dve.tensor_copy(zg[:, j % 2, chunk(n)], psS[:, i % 2, :]).then_inc(v_out, 1)
                        if s < NZ:
                            kind, j = Z_TILES[s]
                            if kind == "value":
                                dve.wait_ge(z_done, s + 1)
                                dve.wait_ge(z_act, j + 1)
                                if j >= 3:
                                    dve.wait_ge(conv_s, CONV_K * (j - 2))
                                    dve.wait_ge(conv_p, CONV_K * (j - 2))
                                p0 = psZ[:, 3 * (s % 2), :]
                                p1 = psZ[:, 3 * (s % 2) + 1:3 * (s % 2) + 3, :].rearrange("p a b -> p (a b)")
                                dve.tensor_tensor(u[:, j % 3, U_P + PAD:U_P + PAD + PROMPT], p0, sg[:, 0:PROMPT], ALU.mult)
                                dve.tensor_tensor(u[:, j % 3, U_S + PAD:U_S + PAD + SAMPLE], p1, sg[:, PROMPT:TOKENS],
                                                  ALU.mult).then_inc(z_dve, 1)
                            elif kind in "qk":
                                dve.wait_ge(z_act, sum(acts[:s + 1]))
                                if Z_TILES[s - 2][0] in "qk":
                                    wait_store(dve, "qk", s - 2)
                                col = 0 if kind == "q" else 1
                                for n in range(NCH):
                                    out, prods = zg[:, s % 2, chunk(n)], psZ[:, 3 * (s % 2) + n, :]
                                    if kind == "q":
                                        out = out.rearrange("p (j r c) -> p j r c", j=COL_BLOCKS, c=Q_COLS)
                                        prods = by_block(prods)
                                    m = dve.tensor_scalar(out, prods, qkg[:, col:col + 1],
                                                          DH ** -0.5 if kind == "q" else 1.0, ALU.mult, ALU.mult)
                                m.then_inc(z_dve, 1)


def attend(nc, A, sem, sb, ps, qk_d, v_d, ident, o_nat):
    NB = len(BLOCKS)
    UNITS = HEADS * NB
    qk_loaded = [sem(f"qk_loaded{i}") for i in range(4)]
    v_loaded = sem("v_loaded")
    bias_loaded = [sem(f"bias_loaded{i}") for i in range(2)]
    s_done, s_biased, m_neg, p_ready = sem("s_done"), sem("s_biased"), sem("m_neg"), sem("p_ready")
    pT_done, pT_out, o_done, r_ready, o_out = sem("pT_done"), sem("pT_out"), sem("o_done"), sem("r_ready"), sem("o_out")
    with ExitStack() as c:
        qk = sb(c, "qk", [P, 8, TOKENS])
        v = sb(c, "v", [P, len(V_ROWS) * COL_BLOCKS, WA])
        bias = sb(c, "bias", [P, 2, 3, BIAS_COLS])
        sc = sb(c, "sc", [P, 2, 384])
        pr = sb(c, "pr", [P, 2, 384])
        pT = sb(c, "pT", [P, 2, 384])
        mx = sb(c, "mx", [P, 4])
        nm = sb(c, "nm", [P, 4])
        sm = sb(c, "sm", [P, 4])
        rs = sb(c, "rs", [P, 4])
        psS = ps(c, "psSc", [P, 3, 512])
        psT = ps(c, "psPT", [P, 2, 512])
        psO = ps(c, "psOh", [P, 3, 512])

        def unit(i):
            h, b = divmod(i, NB)
            return h, b, *BLOCKS[b]

        with nc.Block() as block:
            @block.sync
            def _(sp):
                def heads(t):
                    for w in range(2):
                        sp.dma_start(qk[:, 4 * w + t, :], qk_d[4 * w + t]).then_inc(qk_loaded[t], 16)
                def biases(h):
                    if h >= 2:
                        sp.wait_ge(s_biased, NB * (h - 1))
                    sp.dma_start(bias[:, h % 2], A["bias"][h]).then_inc(bias_loaded[h % 2], 16)
                heads(0)
                biases(0)
                for n, (t0, r0) in enumerate(V_ROWS):
                    for j in range(COL_BLOCKS):
                        for r in range(4):
                            at = t0 + (r0 + r) * GRID_W + KEY_COL0[j]
                            sp.dma_start(v[r * K_COLS:(r + 1) * K_COLS, n * COL_BLOCKS + j, :],
                                         v_d[at:at + K_COLS, :]).then_inc(v_loaded, 16)
                biases(1)
                for t in range(1, 4):
                    heads(t)
                for h in range(2, HEADS):
                    biases(h)

            @block.tensor
            def _(pe):
                def scores(i):
                    h, b, s, j = unit(i)
                    t0, qr, kr, rows, _, _ = ROW_SETS[s]
                    if b == 0 and h % 2 == 0:
                        pe.wait_ge(qk_loaded[h // 2], 32)
                    if i >= 3:
                        pe.wait_ge(s_biased, i - 2)
                    lo = DH * (h % 2)
                    at = t0 + qr * GRID_W + j * P
                    q = qk[lo:lo + DH, h // 2, at:at + P]
                    k = qk[lo:lo + DH, 4 + h // 2, t0 + kr * GRID_W:t0 + (kr + rows) * GRID_W].rearrange(
                        "p (r c) -> p r c", c=GRID_W)[:, :, KEY_COL0[j]:KEY_COL0[j] + K_COLS]
                    pe.matmul(psS[:, i % 3, 0:rows * K_COLS], q, k, start=True, stop=True).then_inc(s_done, 1)

                def turn(i):
                    h, b, s, j = unit(i)
                    n = ROW_SETS[s][3] // 4
                    pe.wait_ge(p_ready, i + 1)
                    if i >= 2:
                        pe.wait_ge(pT_out, i - 1)
                    for m in range(n):
                        mm = pe.transpose(psT[:, i % 2, m * P:(m + 1) * P], pr[:, i % 2, m * P:(m + 1) * P], ident[:, :])
                    mm.then_inc(pT_done, 1)

                def pv(i):
                    h, b, s, j = unit(i)
                    t0, qr, kr, rows, _, _ = ROW_SETS[s]
                    first = V_ROWS.index((t0, kr))
                    pe.wait_ge(pT_out, i + 1)
                    if i == 0:
                        pe.wait_ge(v_loaded, 16 * 4 * len(V_ROWS) * COL_BLOCKS)
                    if i >= 3:
                        pe.wait_ge(o_out, i - 2)
                    for m in range(rows // 4):
                        mm = pe.matmul(psO[:, i % 3, 0:DH], pT[:, i % 2, m * P:(m + 1) * P],
                                       v[:, (first + m) * COL_BLOCKS + j, h * DH:(h + 1) * DH],
                                       start=(m == 0), stop=(m == rows // 4 - 1))
                    mm.then_inc(o_done, 1)

                for i in range(UNITS + 3):
                    if i < UNITS:
                        scores(i)
                    if 2 <= i < UNITS + 2:
                        turn(i - 2)
                    if i >= 3:
                        pv(i - 3)

            @block.vector
            def _(dve):
                for i in range(UNITS + 4):
                    if i < UNITS:
                        h, b, s, j = unit(i)
                        w = ROW_SETS[s][3] * K_COLS
                        at = ROW_SETS[s][5]
                        if b == 0:
                            dve.wait_ge(bias_loaded[h % 2], 16 * (h // 2 + 1))
                        dve.wait_ge(s_done, i + 1)
                        if i >= 2:
                            dve.wait_ge(p_ready, i - 1)
                        dve.tensor_tensor_reduce(out=sc[:, i % 2, 0:w], in0=psS[:, i % 3, 0:w],
                                                 in1=bias[:, h % 2, PATTERN[j], at:at + w], scale=1.0, scalar=-3e38,
                                                 op0=ALU.add, op1=ALU.max, accum_out=mx[:, i % 4:i % 4 + 1]).then_inc(s_biased, 1)
                        dve.wait_ge(s_biased, i + 1)
                        dve.tensor_scalar(nm[:, i % 4:i % 4 + 1], mx[:, i % 4:i % 4 + 1], -1.0, None,
                                          ALU.mult).then_inc(m_neg, 1)
                    if 2 <= i < UNITS + 2:
                        dve.wait_ge(p_ready, i - 1)
                        if i >= 6:
                            dve.wait_ge(o_out, i - 5)
                        dve.reciprocal(rs[:, (i - 2) % 4:(i - 2) % 4 + 1], sm[:, (i - 2) % 4:(i - 2) % 4 + 1]).then_inc(r_ready, 1)
                    if i >= 4:
                        e = i - 4
                        h, b, s, j = unit(e)
                        dve.wait_ge(o_done, e + 1)
                        dve.wait_ge(r_ready, e + 1)
                        dve.tensor_scalar(o_nat[:, b, h * DH:(h + 1) * DH], psO[:, e % 3, 0:DH], rs[:, e % 4:e % 4 + 1],
                                          None, ALU.mult).then_inc(o_out, 1)

            @block.scalar
            def _(act):
                for i in range(UNITS + 2):
                    if i < UNITS:
                        h, b, s, j = unit(i)
                        w = ROW_SETS[s][3] * K_COLS
                        act.wait_ge(m_neg, i + 1)
                        if i >= 2:
                            act.wait_ge(pT_done, i - 1)
                        if i >= 4:
                            act.wait_ge(r_ready, i - 3)
                        act.activation(pr[:, i % 2, 0:w], sc[:, i % 2, 0:w], ACT.Exp, bias=nm[:, i % 4:i % 4 + 1],
                                       accum_out=sm[:, i % 4:i % 4 + 1]).then_inc(p_ready, 1)
                    if i >= 1 and i - 1 < UNITS:
                        e = i - 1
                        w = ROW_SETS[unit(e)[2]][3] * K_COLS
                        act.wait_ge(pT_done, e + 1)
                        if e >= 2:
                            act.wait_ge(o_done, e - 1)
                        act.activation(pT[:, e % 2, 0:w], psT[:, e % 2, 0:w], ACT.Copy).then_inc(pT_out, 1)


def mix(nc, A, sem, sb, ps, rows_of, x_d, y_d, ada_d, conv_d, xhat_d, ident, eps_col, modv, a2, affT, o_nat):
    NB = len(BLOCKS)
    XR = 3
    conv_loaded, gate_loaded = sem("conv_loaded"), sem("gate1_loaded")
    w_loaded = [sem(f"w_out_loaded{i}") for i in range(2)]
    w_hi_ready, w_lo_ready = sem("w_out_hi"), sem("w_out_lo")
    oT_done, oT_act, oT_dve = sem("oT_done"), sem("oT_out_act"), sem("oT_out_dve")
    m_hi, m_lo, mixed = sem("mix_hi"), sem("mix_lo"), sem("mixed")
    x_loaded = [sem(f"x3_loaded{i}") for i in range(XR)]
    gated, x1_ready, sq_done, ms_done, rt_done, r_done, xh_ready = (
        sem("gated"), sem("x1_ready"), sem("x1_sq"), sem("x1_ms"), sem("x1_rt"), sem("x1_rstd"), sem("xh_ready"))
    x1_stored = [sem(f"x1_stored{i}") for i in range(XR)]
    xh_stored = [sem(f"xh_stored{i}") for i in range(2)]
    xhT_done, h2_ready, logit_done, l_max, l_neg, l_exp, l_rec, aff_ready, aff_t, aff_out, wr_loaded, aff_zero = (
        sem("xhT_done"), sem("h2_ready"), sem("logit_done"), sem("l_max"), sem("l_neg"), sem("l_exp"), sem("l_rec"),
        sem("aff_ready"), sem("aff_turned"), sem("aff_out"), sem("w_router_loaded"), sem("aff_zero"))
    with ExitStack() as c:
        conv = sb(c, "conv3", [P, 4, TOKENS])
        attn = sb(c, "attn3", [P, 4, TOKENS])
        w_raw = sb(c, "wo_raw", [P, 2, D])
        w_hi = sb(c, "wo_hi", [P, KD, D], F32R)
        w_lo = sb(c, "wo_lo", [P, KD, D], F32R)
        mh = sb(c, "mh", [P, 2, KD, P], F32R)
        ml = sb(c, "ml", [P, 2, KD, P], F32R)
        gate1 = sb(c, "gate1", [P, 2, D])
        xt = sb(c, "xt3", [P, XR, D])
        tg = sb(c, "tg", [P, 2, D])
        xh = sb(c, "xh", [P, 2, D])
        h2 = sb(c, "h2", [P, KD, P])
        wr = sb(c, "wr", [P, KD, EXPERTS])
        st = sb(c, "st3", [P, 4, TILES])
        lg = sb(c, "lg", [P, 4, 2])
        ex = sb(c, "ex", [P, 2, EXPERTS])
        af = sb(c, "af", [P, 2, 48])
        psO = ps(c, "psMix", [P, 4, 512])
        psT = ps(c, "psXT", [P, 2, 512])
        psL = ps(c, "psLog", [P, 2, 512])

        with nc.Block() as block:
            @block.sync
            def _(sp):
                for k in range(KD):
                    if k >= 2:
                        sp.wait_ge(w_lo_ready, k - 1)
                    sp.dma_start(w_raw[:, k % 2, :], A["w_out"][k * P:(k + 1) * P, :]).then_inc(w_loaded[k % 2], 16)
                for j in range(4):
                    sp.dma_start(conv[:, j, :], conv_d[j]).then_inc(conv_loaded, 16)
                for grp in range(2):
                    sp.dma_start(gate1[:, grp, :], ada_d[grp:grp + 1, 2 * D:3 * D].to_broadcast([P, D])).then_inc(gate_loaded, 16)
                sp.dma_start(wr[:, :, :], A["w_router"].rearrange("(p k) n -> p k n", k=KD)).then_inc(wr_loaded, 16)
                for s in range(TILES + 2):
                    if s < TILES:
                        if s >= XR:
                            sp.wait_ge(x1_stored[s % XR], 16 * (s // XR))
                            sp.wait_ge(xh_ready, s - XR + 1)
                        sp.dma_start(xt[:, s % XR, :], rows_of(x_d, s)).then_inc(x_loaded[s % XR], 16)
                    if s >= 2:
                        t = s - 2
                        sp.wait_ge(x1_ready, t + 1)
                        sp.dma_start(rows_of(y_d, t), xt[:, t % XR, :]).then_inc(x1_stored[t % XR], 16)
                        sp.wait_ge(xh_ready, t + 1)
                        sp.dma_start(xhat_d[t * P:(t + 1) * P, :], xh[:, t % 2, :]).then_inc(xh_stored[t % 2], 16)
                for i in range(XR):
                    sp.wait_ge(x1_stored[i], 16 * (TILES // XR))
                for i in range(2):
                    sp.wait_ge(xh_stored[i], 16 * (TILES // 2))

            @block.gpsimd
            def _(pool):
                pool.memset(af[:, :, :], 0.0).then_inc(aff_zero, 1)
                pool.memset(affT[:, :], -1.0).then_inc(aff_zero, 1)

            @block.tensor
            def _(pe):
                for b in range(NB):
                    if b >= 4:
                        if b % 2:
                            pe.wait_ge(oT_dve, (b - 4) // 2 + 1)
                        else:
                            pe.wait_ge(oT_act, (b - 4) // 2 + 1)
                    for k in range(4):
                        mm = pe.transpose(psO[:, b % 4, k * P:(k + 1) * P], o_nat[:, b, k * P:(k + 1) * P], ident[:, :])
                    mm.then_inc(oT_done, 1)
                for s in range(TILES + 2):
                    if s < TILES:
                        pe.wait_ge(m_lo, s + 1)
                        if s == 0:
                            pe.wait_ge(w_lo_ready, KD)
                        if s >= 2:
                            pe.wait_ge(gated, s - 1)
                        for n in range(2):
                            for k in range(KD):
                                for i, (m, w) in enumerate(((mh, w_hi), (mh, w_lo), (ml, w_hi))):
                                    mm = pe.matmul(psO[:, 2 * (s % 2) + n, :], m[:, s % 2, k, :],
                                                   w[:, k, n * 512:(n + 1) * 512], start=(k == 0 and i == 0),
                                                   stop=(k == KD - 1 and i == 2))
                        mm.then_inc(mixed, 1)
                    if 1 <= s < TILES + 1:
                        t = s - 1
                        pe.wait_ge(xh_ready, t + 1)
                        if t >= 1:
                            pe.wait_ge(h2_ready, t)
                        xk = xh[:, t % 2, :].rearrange("p (d k) -> p k d", k=KD)
                        for k in range(KD):
                            mm = pe.transpose(psT[:, k // 4, (k % 4) * P:(k % 4 + 1) * P], xk[:, k, :], ident[:, :])
                        mm.then_inc(xhT_done, 1)
                        pe.wait_ge(h2_ready, t + 1)
                        if t >= 1:
                            pe.wait_ge(l_exp, t)
                        for k in range(KD):
                            mm = pe.matmul(psL[:, 0, 0:EXPERTS], h2[:, k, :], wr[:, k, :], start=(k == 0), stop=(k == KD - 1))
                        mm.then_inc(logit_done, 1)
                    if s >= 2:
                        t = s - 2
                        pe.wait_ge(aff_ready, t + 1)
                        if t >= 1:
                            pe.wait_ge(aff_out, t)
                        pe.transpose(psL[0:48, 1, 0:P], af[:, t % 2, :], ident[:, :]).then_inc(aff_t, 1)

            def oT(eng, b, counter):
                s, j = BLOCKS[b]
                t0, qr, _, _, _, _ = ROW_SETS[s]
                eng.wait_ge(oT_done, b + 1)
                dst = attn[:, :, t0 + qr * GRID_W:t0 + (qr + 8) * GRID_W].rearrange(
                    "p k (r c) -> p k r c", c=GRID_W)
                for k in range(4):
                    d = dst[:, k, :, j * Q_COLS:(j + 1) * Q_COLS]
                    src = psO[:, b % 4, k * P:(k + 1) * P].rearrange("p (r c) -> p r c", c=Q_COLS)
                    m = eng.tensor_copy(d, src) if counter is oT_dve else eng.activation(d, src, ACT.Copy)
                m.then_inc(counter, 1)

            @block.scalar
            def _(act):
                for k in range(KD):
                    act.wait_ge(w_loaded[k % 2], 16 * (k // 2 + 1))
                    act.activation(w_hi[:, k, :], w_raw[:, k % 2, :], ACT.Copy).then_inc(w_hi_ready, 1)
                for b in range(0, NB, 2):
                    oT(act, b, oT_act)

                def split(t):
                    if t >= 2:
                        act.wait_ge(mixed, t - 1)
                    act.activation(mh[:, t % 2, 0:4], attn[:, :, t * P:(t + 1) * P], ACT.Copy)
                    act.activation(mh[:, t % 2, 4:8], conv[:, :, t * P:(t + 1) * P], ACT.Copy).then_inc(m_hi, 1)
                act.wait_ge(oT_dve, NB // 2)
                act.wait_ge(oT_act, NB // 2)
                act.wait_ge(conv_loaded, 64)
                act.wait_ge(aff_zero, 2)
                split(0)
                for s in range(TILES + 2):
                    if s + 1 < TILES:
                        split(s + 1)
                    if 1 <= s < TILES + 1:
                        t = s - 1
                        act.wait_ge(x1_ready, t + 1)
                        act.activation(tg[:, t % 2, :], xt[:, t % XR, :], ACT.Square,
                                       accum_out=st[:, 0, t:t + 1]).then_inc(sq_done, 1)
                        act.wait_ge(ms_done, t + 1)
                        act.activation(st[:, 2, t:t + 1], st[:, 1, t:t + 1], ACT.Sqrt).then_inc(rt_done, 1)
                        act.wait_ge(xhT_done, t + 1)
                        if t >= 1:
                            act.wait_ge(logit_done, t)
                        for k in range(KD):
                            m = act.activation(h2[:, k, :], psT[:, k // 4, (k % 4) * P:(k % 4 + 1) * P], ACT.Identity,
                                               bias=modv[:, group(t), 2, k:k + 1], scale=a2[:, group(t), k:k + 1])
                        m.then_inc(h2_ready, 1)
                        act.wait_ge(l_neg, t + 1)
                        if t >= 2:
                            act.wait_ge(aff_ready, t - 1)
                        act.activation(ex[:, t % 2, :], psL[:, 0, 0:EXPERTS], ACT.Exp, bias=lg[:, 1, t % 2:t % 2 + 1],
                                       accum_out=lg[:, 2, t % 2:t % 2 + 1]).then_inc(l_exp, 1)

            @block.vector
            def _(dve):
                for k in range(KD):
                    dve.wait_ge(w_hi_ready, k + 1)
                    dve.tensor_tensor(w_lo[:, k, :], w_raw[:, k % 2, :], w_hi[:, k, :].bitcast(F32),
                                      ALU.subtract).then_inc(w_lo_ready, 1)
                for b in range(1, NB, 2):
                    oT(dve, b, oT_dve)
                dve.wait_ge(oT_act, NB // 2)
                dve.wait_ge(oT_dve, NB // 2)
                dve.wait_ge(gate_loaded, 32)

                def split(t):
                    dve.wait_ge(m_hi, t + 1)
                    dve.tensor_tensor(ml[:, t % 2, 0:4], attn[:, :, t * P:(t + 1) * P], mh[:, t % 2, 0:4].bitcast(F32),
                                      ALU.subtract)
                    dve.tensor_tensor(ml[:, t % 2, 4:8], conv[:, :, t * P:(t + 1) * P], mh[:, t % 2, 4:8].bitcast(F32),
                                      ALU.subtract).then_inc(m_lo, 1)
                split(0)
                for s in range(TILES + 2):
                    if s + 1 < TILES:
                        split(s + 1)
                    if 1 <= s < TILES + 1:
                        t = s - 1
                        dve.wait_ge(mixed, t + 1)
                        dve.wait_ge(x_loaded[t % XR], 16 * (t // XR + 1))
                        if t >= 2:
                            dve.wait_ge(sq_done, t - 1)
                        dve.tensor_tensor(tg[:, t % 2, :], psO[:, 2 * (t % 2):2 * (t % 2) + 2, :].rearrange("p a b -> p (a b)"),
                                          gate1[:, group(t), :], ALU.mult).then_inc(gated, 1)
                        dve.wait_ge(gated, t + 1)
                        dve.tensor_tensor(xt[:, t % XR, :], xt[:, t % XR, :], tg[:, t % 2, :], ALU.add).then_inc(x1_ready, 1)
                        dve.wait_ge(sq_done, t + 1)
                        dve.tensor_scalar(st[:, 1, t:t + 1], st[:, 0, t:t + 1], 1.0 / D, EPS, ALU.mult, ALU.add).then_inc(ms_done, 1)
                        dve.wait_ge(rt_done, t + 1)
                        dve.reciprocal(st[:, 3, t:t + 1], st[:, 2, t:t + 1]).then_inc(r_done, 1)
                        dve.wait_ge(r_done, t + 1)
                        if t >= 2:
                            dve.wait_ge(xhT_done, t - 1)
                            dve.wait_ge(xh_stored[t % 2], 16 * (t // 2))
                        dve.tensor_scalar(xh[:, t % 2, :], xt[:, t % XR, :], st[:, 3, t:t + 1], None, ALU.mult).then_inc(xh_ready, 1)
                        dve.wait_ge(logit_done, t + 1)
                        dve.reduce_max(lg[:, 0, t % 2:t % 2 + 1], psL[:, 0, 0:EXPERTS], AX.X).then_inc(l_max, 1)
                        dve.wait_ge(l_max, t + 1)
                        dve.tensor_scalar(lg[:, 1, t % 2:t % 2 + 1], lg[:, 0, t % 2:t % 2 + 1], -1.0, None, ALU.mult).then_inc(l_neg, 1)
                        dve.wait_ge(l_exp, t + 1)
                        dve.reciprocal(lg[:, 3, t % 2:t % 2 + 1], lg[:, 2, t % 2:t % 2 + 1]).then_inc(l_rec, 1)
                        dve.wait_ge(l_rec, t + 1)
                        at = 32 * group(t)
                        if t >= 2:
                            dve.wait_ge(aff_t, t - 1)
                        if t == 4 or t == 5:
                            dve.memset(af[:, t % 2, 0:EXPERTS], 0.0)
                        dve.tensor_scalar(af[:, t % 2, at:at + EXPERTS], ex[:, t % 2, :], lg[:, 3, t % 2:t % 2 + 1], None,
                                          ALU.mult).then_inc(aff_ready, 1)
                    if s >= 2:
                        t = s - 2
                        grp = group(t)
                        dve.wait_ge(aff_t, t + 1)
                        col = t * P - (PROMPT if grp else 0)
                        dve.tensor_copy(affT[32 * grp:32 * grp + EXPERTS, col:col + P],
                                        psL[32 * grp:32 * grp + EXPERTS, 1, 0:P]).then_inc(aff_out, 1)


def experts(nc, A, sem, sb, ps, y_d, ada_d, xhat_d, ident, modv, a2, affT):
    RAW = 3
    ROUNDS = CAP_S // 8
    f_all = sem("top_vals"), sem("top_idx"), sem("top_drop")
    top_v, top_i, top_d = f_all
    idx_f, tT_done, sel_ready, sel_p = sem("idx_float"), sem("top_turned"), sem("sel_ready"), sem("sel_p")
    gate_loaded = sem("gate2_loaded")
    raw_loaded = [sem(f"raw_loaded{i}") for i in range(RAW)]
    hi_done, lo_done = sem("w_hi_split"), sem("w_lo_split")
    gu_done, dn_done = sem("gate_up_done"), sem("down_done")
    gu_low, gu_sum, silu_done, hid_done, hid_hi, hid_lo = (
        sem("gu_low"), sem("gu_sum"), sem("silu_done"), sem("hid_done"), sem("hid_hi"), sem("hid_lo"))
    pool_steps = sem("pool_steps")
    idx_now, g_loaded_p, g_loaded_s = sem("idx_now"), sem("gathered_p"), sem("gathered_s")
    x_turned, xs_ready, x_hi, x_lo = sem("x_turned"), sem("xe_staged"), sem("xe_hi"), sem("xe_lo")
    y_half, y_sent_s, y_sent_p, y_scaled = sem("y_half"), sem("scattered_s"), sem("scattered_p"), sem("y_scaled")

    with ExitStack() as c:
        raw = sb(c, "raw", [P, RAW, 3, 2, KD * P])
        whi = sb(c, "whi", [P, 2, 3, KD * P], F32R)
        wlo = sb(c, "wlo", [P, 2, 3, KD * P], F32R)
        xg_s = sb(c, "xg_s", [P, D])
        xg_p = sb(c, "xg_p", [CAP_P, D])
        xst = sb(c, "xst", [P, KD, CAP])
        xhi = sb(c, "xhi", [P, KD, 2 * CAP], F32R)
        low = sb(c, "low", [P, 2, CAP])
        gu = sb(c, "gu", [P, 2, CAP])
        sl = sb(c, "sl", [P, CAP])
        hid = sb(c, "hid", [P, 2, CAP])
        hs = sb(c, "hs", [P, 2, 2 * CAP], F32R)
        ye = sb(c, "ye", [P, 2, D])
        yp = sb(c, "yp", [CAP_P, D])
        gate2 = sb(c, "gate2", [P, 2, D])
        vals = sb(c, "vals", [48, CAP_S])
        idxu = sb(c, "idxu", [48, CAP_S], U32)
        idxf = sb(c, "idxf", [48, CAP_S])
        gsel = sb(c, "gsel", [P, 48])
        isel = sb(c, "isel", [P, 48], U32)
        iall = sb(c, "iall", [P, EXPERTS], U32)
        gnow = sb(c, "gnow", [P, 2])
        inow = sb(c, "inow", [P, 2, 4], U32)
        psG = ps(c, "psG", [P, 4, 512])
        psY = ps(c, "psY", [P, 4, 512])

        def e_at(ap, e):
            return ap[bass.ds(e, 1)]

        w_gu = A["w_gu"]
        w_dn = A["w_down"].rearrange("e (c t p) d -> e c p t d", c=CHUNKS, t=2)

        with nc.Block() as block:
            @block.sync
            def _(sp):
                for grp in range(2):
                    sp.dma_start(gate2[:, grp, :], ada_d[grp:grp + 1, 5 * D:6 * D].to_broadcast([P, D])).then_inc(gate_loaded, 16)
                uses = [len(range(s, CHUNKS, RAW)) for s in range(RAW)]

                def load(e, ci):
                    s = ci % RAW
                    sp.dma_start(raw[:, s, 0:2], e_at(w_gu, e)[0, ci]).then_inc(raw_loaded[s], 16)
                    sp.dma_start(raw[:, s, 2], e_at(w_dn, e)[0, ci]).then_inc(raw_loaded[s], 16)

                def loads(e, first):
                    for ci in range(CHUNKS):
                        back = ci - RAW if ci >= RAW else max(range(ci % RAW, CHUNKS, RAW)) - CHUNKS
                        if not (first and back < 0):
                            sp.wait_ge(lo_done, (e * CHUNKS + back + 1) * 2)
                        load(e, ci)
                loads(0, True)
                with sp.Fori(1, EXPERTS) as e:
                    loads(e, False)

            @block.tensor
            def _(pe):
                for i, (src, dst) in enumerate(((vals, 0), (idxf, 1))):
                    if i == 0:
                        pe.wait_ge(top_v, ROUNDS)
                    else:
                        pe.wait_ge(idx_f, 1)
                    pe.transpose(psG[:, dst, 0:48], src[:, :], ident[0:48, 0:48]).then_inc(tT_done, 1)

                def turn(k):
                    pe.transpose(psG[:, 0, 2 * CAP:2 * CAP + P], xg_s[:, :].rearrange("p (d k) -> p k d", k=KD)[:, k, :], ident[:, :])
                    pe.transpose(psG[:, 1, 2 * CAP:2 * CAP + CAP_P], xg_p[:, :].rearrange("p (d k) -> p k d", k=KD)[:, k, :],
                                 ident[0:CAP_P, 0:CAP_P]).then_inc(x_turned, 1)

                pe.wait_ge(sel_ready, 1)
                pe.wait_ge(g_loaded_s, 16)
                pe.wait_ge(g_loaded_p, 16)
                for k in range(KD):
                    if k >= 1:
                        pe.wait_ge(xs_ready, k)
                    turn(k)

                def gate_up(e, i, first):
                    a = i % 2
                    n = e * FT + i
                    pe.wait_ge(lo_done, n + 1)
                    if not (first and i < 2):
                        pe.wait_ge(gu_sum, n - 1)
                    if i % 2 == 0 and 2 <= i < 2 + 2 * KD:
                        k = i // 2 - 1
                        if k == 0:
                            pe.wait_ge(g_loaded_s, 16 * (e + 2))
                            pe.wait_ge(g_loaded_p, 16 * (e + 2))
                        pe.wait_ge(xs_ready, KD * (e + 1) + k)
                        turn(k)
                    if i == 0:
                        pe.wait_ge(x_lo, e + 1)
                    for m in range(2):
                        bank = psG[:, 2 * a + m, :]
                        for k in range(KD):
                            pe.matmul(bank[:, 0:2 * CAP], whi[:, a, m, k * P:(k + 1) * P], xhi[:, k, :],
                                      start=(k == 0), stop=False, skip_group_check=True)
                            mm = pe.matmul(bank[:, 0:CAP], wlo[:, a, m, k * P:(k + 1) * P], xhi[:, k, 0:CAP],
                                           start=False, stop=(k == KD - 1), skip_group_check=True)
                    mm.then_inc(gu_done, 1)

                def down(e, i, first):
                    a = i % 2
                    n = e * FT + i
                    pe.wait_ge(hid_lo, n + 1)
                    if i == 0 and not first:
                        pe.wait_ge(y_scaled, 3 * e)
                    st, en = i == 0, i == FT - 1
                    s_hi, pp, s_lo = hs[:, a, 0:P], hs[:, a, P:2 * P], hs[:, a, 2 * P:3 * P]
                    for h in range(2):
                        wh, wl = (w[:, a, 2, h * 512:(h + 1) * 512] for w in (whi, wlo))
                        pe.matmul(psY[:, h, :], s_hi, wh, start=st, stop=False)
                        pe.matmul(psY[:, h, :], s_hi, wl, start=False, stop=False)
                        pe.matmul(psY[:, h, :], s_lo, wh, start=False, stop=en)
                        pe.matmul(psY[:, 2 + h, :], pp, wh, start=st, stop=False)
                        mm = pe.matmul(psY[:, 2 + h, :], pp, wl, start=False, stop=en)
                    mm.then_inc(dn_done, 1)

                def expert(e, first):
                    for i in range(FT):
                        gate_up(e, i, first)
                        if i >= 1:
                            down(e, i - 1, first)
                    down(e, FT - 1, first)
                expert(0, True)
                with pe.Fori(1, EXPERTS) as e:
                    expert(e, False)

            @block.gpsimd
            def _(pool):
                def gather(e_next):
                    pool.indirect_dma_start(out=xg_p[:, :], out_offset=None, in_=xhat_d,
                                            in_offset=bass.IndirectOffsetOnAxis(ap=inow[0:CAP_P, 1, 0:1], axis=0)).then_inc(g_loaded_p, 16)
                    pool.indirect_dma_start(out=xg_s[:, :], out_offset=None, in_=xhat_d,
                                            in_offset=bass.IndirectOffsetOnAxis(ap=inow[:, 1, 1:2], axis=0)).then_inc(g_loaded_s, 16)

                def lists(e, slot):
                    pool.tensor_copy(inow[:, slot, 0:1], isel[:, bass.ds(e, 1)])
                    pool.tensor_copy(inow[:, slot, 2:3], isel[:, bass.ds(e, 1)])
                    pool.tensor_copy(inow[:, slot, 3:4], isel[:, bass.ds(e + 32, 1)])
                    pool.tensor_copy(inow[:, slot, 1:2], iall[:, bass.ds(e, 1)]).then_inc(idx_now, 1)

                def scatter(e):
                    pool.wait_ge(y_scaled, 3 * e + 3)
                    pool.sem_inc(pool_steps)
                    pool.indirect_dma_start(out=y_d[1], out_offset=bass.IndirectOffsetOnAxis(ap=inow[:, 0, 3:4], axis=0),
                                            in_=ye[:, 0, :], in_offset=None, compute_op=ALU.add).then_inc(y_sent_s, 16)
                    pool.indirect_dma_start(out=y_d[0], out_offset=bass.IndirectOffsetOnAxis(ap=inow[0:CAP_P, 0, 2:3], axis=0),
                                            in_=yp[:, :], in_offset=None, compute_op=ALU.add).then_inc(y_sent_p, 16)
                    pool.wait_ge(y_sent_s, 16 * (e + 1))
                    pool.wait_ge(y_sent_p, 16 * (e + 1))

                pool.wait_ge(sel_ready, 1)
                lists(0, 1)
                pool.wait_ge(idx_now, 1)
                gather(0)

                def expert(e, nxt):
                    pool.wait_ge(g_loaded_s, 16 * (e + 1))
                    pool.wait_ge(g_loaded_p, 16 * (e + 1))
                    pool.wait_ge(x_turned, KD * (e + 1))
                    lists(e, 0)
                    lists(nxt, 1)
                    pool.wait_ge(idx_now, 2 * e + 3)
                    pool.sem_inc(pool_steps)
                    gather(e + 1)
                    scatter(e)
                with pool.Fori(0, EXPERTS - 1) as e:
                    expert(e, e + 1)
                expert(EXPERTS - 1, 0)
                pool.wait_ge(g_loaded_s, 16 * (EXPERTS + 1))
                pool.wait_ge(g_loaded_p, 16 * (EXPERTS + 1))

            def modulate(act, k, grp, src, dst):
                return act.activation(dst, src, ACT.Identity, bias=modv[:, grp, 2, k:k + 1], scale=a2[:, grp, k:k + 1])

            def stage(act, k):
                modulate(act, k, 1, psG[:, 0, 2 * CAP:2 * CAP + P], xst[:, k, 0:P])
                modulate(act, k, 0, psG[:, 1, 2 * CAP:2 * CAP + CAP_P], xst[:, k, P:CAP]).then_inc(xs_ready, 1)

            @block.scalar
            def _(act):
                for k in range(KD):
                    act.wait_ge(x_turned, k + 1)
                    stage(act, k)

                def hi(e, i, first):
                    n = e * FT + i
                    ci, a = divmod(i, 2)
                    s = ci % RAW
                    if a == 0:
                        per = len(range(s, CHUNKS, RAW))
                        act.wait_ge(raw_loaded[s], (e * per + ci // RAW + 1) * 32)
                    if not (first and i < 2):
                        act.wait_ge(dn_done, n - 1)
                    act.activation(whi[:, a], raw[:, s, :, a], ACT.Copy).then_inc(hi_done, 1)

                def xsplit(e):
                    act.wait_ge(xs_ready, KD * (e + 1))
                    act.activation(xhi[:, :, 0:CAP], xst[:, :, :], ACT.Copy).then_inc(x_hi, 1)

                def out(e, i, first):
                    a = i % 2
                    n = e * FT + i
                    act.wait_ge(gu_done, n + 1)
                    if i % 2 == 0 and 2 <= i < 2 + 2 * KD:
                        stage(act, i // 2 - 1)
                    act.activation(low[:, :, :], psG[:, 2 * a:2 * a + 2, CAP:2 * CAP], ACT.Copy).then_inc(gu_low, 1)
                    act.wait_ge(gu_sum, n + 1)
                    act.activation(sl[:, :], gu[:, 0, :], ACT.Silu).then_inc(silu_done, 1)
                    act.wait_ge(hid_done, n + 1)
                    act.activation(hs[:, a, 0:CAP], hid[:, a, :], ACT.Copy).then_inc(hid_hi, 1)

                def yhalf(e, first):
                    act.wait_ge(dn_done, (e + 1) * FT)
                    act.activation(yp[:, :], psY[CAP_P:P, 2:4, :].rearrange("p a b -> p (a b)"), ACT.Copy).then_inc(y_half, 1)

                def steps(e, first, last):
                    for i in range(FT):
                        if i == 0 and first:
                            xsplit(e)
                            hi(e, 0, True)
                        if i + 1 < FT:
                            hi(e, i + 1, first)
                        out(e, i, first)
                    if not last:
                        act.wait_ge(gu_done, (e + 1) * FT)
                        xsplit(e + 1)
                        hi(e + 1, 0, False)
                    if not first:
                        act.wait_ge(y_sent_p, 16 * e)
                    yhalf(e, first)
                steps(0, True, False)
                with act.Fori(1, EXPERTS - 1) as e:
                    steps(e, False, False)
                steps(EXPERTS - 1, False, True)

            @block.vector
            def _(dve):
                for r in range(ROUNDS):
                    sl8 = slice(8 * r, 8 * r + 8)
                    if r:
                        dve.wait_ge(top_d, r)
                    dve.max(vals[:, sl8], affT[:, :]).then_inc(top_v, 1)
                    dve.wait_ge(top_v, r + 1)
                    dve.max_index(idxu[:, sl8], vals[:, sl8], affT[:, :]).then_inc(top_i, 1)
                    dve.wait_ge(top_i, r + 1)
                    dve.match_replace(affT[:, :], vals[:, sl8], affT[:, :], -2.0).then_inc(top_d, 1)
                dve.tensor_copy(idxf[:, :], idxu[:, :]).then_inc(idx_f, 1)
                dve.wait_ge(tT_done, 2)
                dve.tensor_copy(gsel[:, :], psG[:, 0, 0:48])
                dve.tensor_scalar(iall[:, :], psG[:, 1, 32:48], float(PROMPT), None, ALU.add)
                dve.tensor_copy(isel[:, :], psG[:, 1, 0:48]).then_inc(sel_ready, 1)
                dve.wait_ge(sel_ready, 1)
                dve.wait_ge(gate_loaded, 32)

                def lo(e, i, first):
                    n = e * FT + i
                    ci, a = divmod(i, 2)
                    dve.wait_ge(hi_done, n + 1)
                    dve.tensor_tensor(wlo[:, a], raw[:, ci % RAW, :, a], whi[:, a].bitcast(F32), ALU.subtract).then_inc(lo_done, 1)

                def xsplit(e):
                    dve.wait_ge(x_hi, e + 1)
                    dve.tensor_tensor(xhi[:, :, CAP:2 * CAP], xst[:, :, :], xhi[:, :, 0:CAP].bitcast(F32), ALU.subtract).then_inc(x_lo, 1)

                def out(e, i, first):
                    a = i % 2
                    n = e * FT + i
                    dve.wait_ge(gu_low, n + 1)
                    if not (first and i == 0):
                        dve.wait_ge(silu_done, n)
                        dve.wait_ge(hid_done, n)
                    dve.tensor_tensor(gu[:, :, :], psG[:, 2 * a:2 * a + 2, 0:CAP], low[:, :, :], ALU.add).then_inc(gu_sum, 1)
                    dve.wait_ge(silu_done, n + 1)
                    dve.tensor_tensor(hid[:, a, :], sl[:, :], gu[:, 1, :], ALU.mult).then_inc(hid_done, 1)
                    dve.wait_ge(hid_hi, n + 1)
                    dve.tensor_tensor(hs[:, a, CAP:CAP + CAP_P], hid[:, a, P:CAP], hs[:, a, P:CAP].bitcast(F32), ALU.subtract)
                    dve.tensor_tensor(hs[:, a, CAP + CAP_P:2 * CAP], hid[:, a, 0:P], hs[:, a, 0:P].bitcast(F32),
                                      ALU.subtract).then_inc(hid_lo, 1)

                def y_out(e, first):
                    if first:
                        pass
                    else:
                        dve.wait_ge(y_sent_s, 16 * e)
                        dve.wait_ge(y_sent_p, 16 * e)
                    dve.tensor_copy(gnow[:, 0:1], gsel[:, bass.ds(e, 1)])
                    dve.tensor_copy(gnow[:, 1:2], gsel[:, bass.ds(e + 32, 1)]).then_inc(y_scaled, 1)
                    dve.wait_ge(y_scaled, 3 * e + 1)
                    dve.wait_ge(dn_done, (e + 1) * FT)
                    dve.scalar_tensor_tensor(out=ye[:, 0, :], in0=psY[:, 0:2, :].rearrange("p a b -> p (a b)"), scalar=gnow[:, 1:2],
                                             in1=gate2[:, 1, :], op0=ALU.mult, op1=ALU.mult)
                    dve.wait_ge(y_half, e + 1)
                    dve.tensor_tensor(yp[:, :], psY[0:CAP_P, 2:4, :].rearrange("p a b -> p (a b)"), yp[:, :], ALU.add).then_inc(y_scaled, 1)
                    dve.wait_ge(y_scaled, 3 * e + 2)
                    dve.scalar_tensor_tensor(out=yp[:, :], in0=yp[:, :], scalar=gnow[0:CAP_P, 0:1],
                                             in1=gate2[0:CAP_P, 0, :], op0=ALU.mult, op1=ALU.mult).then_inc(y_scaled, 1)

                def steps(e, first, last):
                    for i in range(FT):
                        if i == 0 and first:
                            xsplit(e)
                            lo(e, 0, True)
                        if i + 1 < FT:
                            lo(e, i + 1, first)
                        out(e, i, first)
                    if not last:
                        xsplit(e + 1)
                        lo(e + 1, 0, False)
                    y_out(e, first)
                steps(0, True, False)
                with dve.Fori(1, EXPERTS - 1) as e:
                    steps(e, False, False)
                steps(EXPERTS - 1, False, True)


_OUTS = [((1, PROMPT, D), "float32"), ((1, SAMPLE, D), "float32")]


def bias_layout(rpb):
    padded = np.concatenate([rpb.reshape(HEADS, -1), np.full((HEADS, 1), NEG, rpb.dtype)], axis=1)
    off = rpb.shape[1] * rpb.shape[2]
    where = np.full((P, 3, BIAS_COLS), off, np.int64)
    for t0, qr0, kr0, rows, grid_rows, at in ROW_SETS:
        for j in (0, 1, 3):
            for q in range(P):
                r, cq = qr0 + q // Q_COLS, j * Q_COLS + q % Q_COLS
                rs = min(max(r - WIN_ROWS // 2, 0), grid_rows - WIN_ROWS)
                cs = min(max(cq - WIN_COLS // 2, 0), GRID_W - WIN_COLS)
                for kr in range(rs, rs + WIN_ROWS):
                    a = (kr - r + WIN_ROWS - 1) * (2 * WIN_COLS - 1) + (cs - cq + WIN_COLS - 1)
                    b = at + (kr - kr0) * K_COLS + cs - KEY_COL0[j]
                    where[q, PATTERN[j], b:b + WIN_COLS] = np.arange(a, a + WIN_COLS)
    return np.ascontiguousarray(padded[:, where])


def lay_out(inputs):
    a = {n: np.ascontiguousarray(inputs[n]) for n in (
        "x_prompt", "x_sample", "c_prompt", "c_sample", "ada_w", "ada_b", "norm1_g", "w_in", "w_out", "norm2_g",
        "w_router", "w_down")}
    a["ident"] = np.eye(P, dtype=np.float32)
    a["ones64"] = np.kron(np.eye(P // DH), np.full((DH, DH), 1.0 / DH)).astype(np.float32)
    a["qk_gain"] = np.stack([np.tile(np.asarray(inputs[n]), P // DH) for n in ("q_norm_g", "k_norm_g")], axis=1)
    per = np.concatenate([np.asarray(inputs["conv_w"])] + [np.asarray(inputs[n])[None] for n in
                         ("conv_b", "conv_ln_g", "conv_ln_b")], axis=0)
    a["conv_pack"] = np.ascontiguousarray(per.reshape(CONV_K + 3, 4, P).transpose(2, 1, 0))
    a["bias"] = bias_layout(np.asarray(inputs["rpb"]))
    gu = np.empty((EXPERTS, CHUNKS, P, 2, 2, KD, P), np.float32)
    for m, n in enumerate(("w_gate", "w_up")):
        w = np.asarray(inputs[n]).reshape(EXPERTS, P, KD, CHUNKS, 2, P)
        gu[:, :, :, m] = w.transpose(0, 3, 1, 4, 2, 5)
    a["w_gu"] = gu.reshape(EXPERTS, CHUNKS, P, 2, 2, KD * P)
    return a


def kernel(**inputs):
    import concourse.bacc as _bacc
    from concourse.bass_utils import run_bass_kernel_spmd as _run

    nc = _bacc.Bacc("TRN2", target_bir_lowering=False, num_devices=1)
    arrays, aps = {}, {}
    for name, a in lay_out(inputs).items():
        arrays[f"in_{name}"] = a
        aps[name] = nc.dram_tensor(f"in_{name}", a.shape, mybir.dt.from_np(a.dtype), kind="ExternalInput").ap()
    outs = [nc.dram_tensor(f"out_{i}", s, mybir.dt.from_np(np.dtype(d)), kind="ExternalOutput").ap()
            for i, (s, d) in enumerate(_OUTS)]
    program(nc, aps, outs)
    r = _run(nc, [arrays], core_ids=[0])
    return tuple(r.results[0][f"out_{i}"] for i in range(len(_OUTS)))
```

```python
from contextlib import ExitStack

import numpy as np

import concourse.bass as bass
from concourse import mybir

F32 = mybir.dt.float32
F32R = mybir.dt.float32r
U32 = mybir.dt.uint32
ALU = mybir.AluOpType
ACT = mybir.ActivationFunctionType
AX = mybir.AxisListType

P = 128
D = 1024
KD = D // P
PROMPT, SAMPLE = 512, 1024
TOKENS = PROMPT + SAMPLE
TILES = TOKENS // P
NCH = TOKENS // 512
MODS = 6
HEADS, DH = 8, 64
WA = HEADS * DH
WC = D - WA
IN_COLS = 3 * WA + 2 * WC
GRID_W, WIN_ROWS, WIN_COLS = 64, 8, 16
CONV_K = 31
PAD = CONV_K // 2
EXPERTS, FACTOR, FF = 16, 2, 2816
EPS = 1e-6
CAP_P = FACTOR * PROMPT // EXPERTS
CAP_S = FACTOR * SAMPLE // EXPERTS
CAP = CAP_P + CAP_S
FT = FF // P
CHUNKS = FT // 2
NEG = -1e30

Q_COLS, K_COLS = 16, 32
COL_BLOCKS = GRID_W // Q_COLS
KEY_COL0 = [min(max(Q_COLS * j - WIN_COLS // 2, 0), GRID_W - K_COLS) for j in range(COL_BLOCKS)]
ROW_SETS = [(0, 0, 0, 8, 8, 0), (PROMPT, 0, 0, 12, 16, 256), (PROMPT, 8, 4, 12, 16, 640)]
PATTERN = [0, 1, 1, 2]
BIAS_COLS = 1024
BLOCKS = [(s, j) for s in range(3) for j in range(COL_BLOCKS)]
V_ROWS = [(0, 0), (0, 4), (PROMPT, 0), (PROMPT, 4), (PROMPT, 8), (PROMPT, 12)]


def group(tile):
    return 0 if tile * P < PROMPT else 1


def program(nc, A, outs):
    g = ExitStack()
    sems = {}

    def sem(name):
        if name not in sems:
            sems[name] = g.enter_context(nc.semaphore(name))
        return sems[name]

    def dram(name, shape):
        return nc.dram_tensor(name, shape, F32, kind="Internal").ap()

    ada_d = dram("ada_d", [2, MODS * D])
    qk_d = dram("qk_d", [8, P, TOKENS])
    conv_d = dram("conv_d", [4, P, TOKENS])
    v_d = dram("v_d", [TOKENS, WA])
    xhat_d = dram("xhat_d", [TOKENS, D])
    y_d = [outs[0].rearrange("b l d -> (b l) d"), outs[1].rearrange("b l d -> (b l) d")]
    x_d = [A["x_prompt"].rearrange("b l d -> (b l) d"), A["x_sample"].rearrange("b l d -> (b l) d")]

    def rows_of(pair, t):
        r = t * P if group(t) == 0 else t * P - PROMPT
        return pair[group(t)][r:r + P, :]

    def sb(ctx, name, shape, dt=F32):
        return ctx.enter_context(nc.sbuf_tensor(name, shape, dt))

    def ps(ctx, name, shape):
        return ctx.enter_context(nc.psum_tensor(name, shape, F32))

    with g:
        ident = sb(g, "ident", [P, P])
        ones64 = sb(g, "ones64", [P, P])
        eps_col = sb(g, "eps_col", [P, 1])
        vecs = sb(g, "vecs", [P, 32])
        convp = sb(g, "convp", [P, 4, CONV_K + 3])
        qkg = sb(g, "qkg", [P, 2])
        modv = sb(g, "modv", [P, 2, 4, KD])
        a1 = sb(g, "a1", [P, 2, KD])
        a2 = sb(g, "a2", [P, 2, KD])
        rstd1 = sb(g, "rstd1", [P, TILES])

        condition(nc, A, g, sem, sb, ps, ada_d, rows_of, x_d,
                  ident, ones64, eps_col, vecs, convp, qkg, modv, a1, a2, rstd1)
        project(nc, A, sem, sb, ps, rows_of, x_d, qk_d, conv_d, v_d,
                ident, ones64, eps_col, convp, qkg, modv, a1, rstd1)
        affT = sb(g, "affT", [48, SAMPLE])
        o_ctx = ExitStack()
        with o_ctx:
            o_nat = sb(o_ctx, "o_nat", [P, len(BLOCKS), WA])
            attend(nc, A, sem, sb, ps, qk_d, v_d, ident, o_nat)
            mix(nc, A, sem, sb, ps, rows_of, x_d, y_d, ada_d, conv_d, xhat_d, ident, eps_col, modv, a2, affT, o_nat)
        experts(nc, A, sem, sb, ps, y_d, ada_d, xhat_d, ident, modv, a2, affT)


def condition(nc, A, g, sem, sb, ps, ada_d, rows_of, x_d,
              ident, ones64, eps_col, vecs, convp, qkg, modv, a1, a2, rstd1):
    NJ = MODS * D // 512
    RING, XR = 3, 3
    consts = sem("consts_loaded")
    c_loaded, cs_ready = sem("c_loaded"), sem("cs_ready")
    w_loaded = [sem(f"ada_w_loaded{i}") for i in range(RING)]
    x_loaded = [sem(f"x_loaded{i}") for i in range(XR)]
    mm_done, ada_row, ada_stored, mod_loaded = sem("ada_mm"), sem("ada_row"), sem("ada_stored"), sem("mod_loaded")
    sq_done, ms_done, rt_done, rstd_done, a_ready = (
        sem("x_sq"), sem("x_ms"), sem("x_rt"), sem("rstd1_done"), sem("a_ready"))
    eps_set = sem("eps_set")
    with ExitStack() as c:
        cT = sb(c, "cT", [P, 2, KD])
        cs = sb(c, "cs", [P, 2, KD])
        aw = sb(c, "aw", [P, RING, KD, 512])
        ada_b2 = sb(c, "ada_b2", [2, MODS * D])
        ada_sb = sb(c, "ada_sb", [2, MODS * D])
        xt = sb(c, "xt0", [P, XR, D])
        junk = sb(c, "junk0", [P, 2, D])
        ss = sb(c, "ss", [P, TILES])
        psA = ps(c, "psA", [P, 2, 512])
        w_v = A["ada_w"].rearrange("(p k) n -> p k n", k=KD)
        CONSTS = 16 * 8

        with nc.Block() as block:
            @block.sync
            def _(sp):
                for i, name in enumerate(("c_prompt", "c_sample")):
                    sp.dma_start(cT[:, i, :], A[name].rearrange("b (p k) -> (b p) k", k=KD)).then_inc(c_loaded, 16)
                for j in range(NJ):
                    if j >= RING:
                        sp.wait_ge(mm_done, j - RING + 1)
                    sp.dma_start(aw[:, j % RING], w_v[:, :, j * 512:(j + 1) * 512]).then_inc(w_loaded[j % RING], 16)
                sp.wait_ge(ada_row, NJ)
                sp.dma_start(ada_d, ada_sb[:, :]).then_inc(ada_stored, 16)
                sp.wait_ge(ada_stored, 16)
                for grp in range(2):
                    for v, m in enumerate((0, 1, 3, 4)):
                        sp.dma_start(modv[:, grp, v, :],
                                     ada_d[grp, m * D:(m + 1) * D].rearrange("(p k) -> p k", k=KD)).then_inc(mod_loaded, 16)
                sp.wait_ge(mod_loaded, 16 * 8)

            @block.gpsimd
            def _(pool):
                pool.memset(eps_col[:, :], EPS).then_inc(eps_set, 1)

            def square(act, t):
                act.wait_ge(x_loaded[t % XR], 16 * (t // XR + 1))
                if t >= 2:
                    act.wait_ge(sq_done, t - 1)
                act.activation(junk[:, t % 2, :], xt[:, t % XR, :], ACT.Square,
                               accum_out=ss[:, t:t + 1]).then_inc(sq_done, 1)

            @block.scalar
            def _(act):
                act.dma_start(ident[:, :], A["ident"]).then_inc(consts, 16)
                act.dma_start(ones64[:, :], A["ones64"]).then_inc(consts, 16)
                act.dma_start(vecs[:, 0:KD], A["norm1_g"].rearrange("(p k) -> p k", k=KD)).then_inc(consts, 16)
                act.dma_start(vecs[:, KD:2 * KD], A["norm2_g"].rearrange("(p k) -> p k", k=KD)).then_inc(consts, 16)
                act.dma_start(convp[:, :, :], A["conv_pack"]).then_inc(consts, 16)
                act.dma_start(qkg[:, :], A["qk_gain"]).then_inc(consts, 16)
                act.dma_start(ada_b2[0:1, :], A["ada_b"].rearrange("(a n) -> a n", a=1)).then_inc(consts, 16)
                act.dma_start(ada_b2[1:2, :], A["ada_b"].rearrange("(a n) -> a n", a=1)).then_inc(consts, 16)
                act.wait_ge(c_loaded, 32)
                act.activation(cs[:, :, :], cT[:, :, :], ACT.Silu).then_inc(cs_ready, 1)
                for t in range(TILES):
                    if t >= XR:
                        act.wait_ge(sq_done, t - XR + 1)
                    act.dma_start(xt[:, t % XR, :], rows_of(x_d, t)).then_inc(x_loaded[t % XR], 16)
                    if t >= 1:
                        square(act, t - 1)
                square(act, TILES - 1)
                act.wait_ge(ms_done, 1)
                act.activation(ss[:, :], ss[:, :], ACT.Sqrt).then_inc(rt_done, 1)

            @block.tensor
            def _(pe):
                pe.wait_ge(cs_ready, 1)
                for j in range(NJ):
                    pe.wait_ge(w_loaded[j % RING], 16 * (j // RING + 1))
                    if j >= 2:
                        pe.wait_ge(ada_row, j - 1)
                    for k in range(KD):
                        mm = pe.matmul(psA[0:2, j % 2, :], cs[:, :, k], aw[:, j % RING, k, :],
                                       start=(k == 0), stop=(k == KD - 1))
                    mm.then_inc(mm_done, 1)

            @block.vector
            def _(dve):
                dve.wait_ge(consts, CONSTS)
                for j in range(NJ):
                    dve.wait_ge(mm_done, j + 1)
                    dve.tensor_tensor(ada_sb[:, j * 512:(j + 1) * 512], psA[0:2, j % 2, :],
                                      ada_b2[:, j * 512:(j + 1) * 512], ALU.add).then_inc(ada_row, 1)
                dve.wait_ge(sq_done, TILES)
                dve.tensor_scalar(ss[:, :], ss[:, :], 1.0 / D, EPS, ALU.mult, ALU.add).then_inc(ms_done, 1)
                dve.wait_ge(rt_done, 1)
                dve.reciprocal(rstd1[:, :], ss[:, :]).then_inc(rstd_done, 1)
                dve.wait_ge(mod_loaded, 16 * 8)
                for grp in range(2):
                    dve.scalar_tensor_tensor(out=a1[:, grp, :], in0=modv[:, grp, 1, :], scalar=1.0,
                                             in1=vecs[:, 0:KD], op0=ALU.add, op1=ALU.mult).then_inc(a_ready, 1)
                    dve.scalar_tensor_tensor(out=a2[:, grp, :], in0=modv[:, grp, 3, :], scalar=1.0,
                                             in1=vecs[:, KD:2 * KD], op0=ALU.add, op1=ALU.mult).then_inc(a_ready, 1)


Z_TILES = ([("gate", j) if s == 0 else ("value", j) for j in range(4) for s in range(2)]
           + [("q", j) for j in range(4)] + [("k", j) for j in range(4)] + [("v", j) for j in range(4)])
Z_COL0 = {"q": 0, "k": WA, "v": 2 * WA, "value": 3 * WA, "gate": 3 * WA + WC}
NZ = len(Z_TILES)
TAPS_STEP = 9
CONV_DONE = [2 + (CONV_K * (j + 1) - 1) // TAPS_STEP for j in range(4)]


def side_jobs():
    jobs = {s: [] for s in range(NZ + 3)}
    for i, (kind, j) in enumerate(Z_TILES):
        if kind in "qkv":
            jobs[i + 1] += [("turn" if kind == "v" else "ss", i, n) for n in range(NCH)]
    for j in range(4):
        m = CONV_DONE[j] + 1
        jobs[m] += [("mean", j, n) for n in range(NCH)]
        jobs[m + 1] += [("var", j, n) for n in range(NCH)]
    return jobs


def project(nc, A, sem, sb, ps, rows_of, x_d, qk_d, conv_d, v_d,
            ident, ones64, eps_col, convp, qkg, modv, a1, rstd1):
    XR, WR = 2, 3
    jobs = side_jobs()
    flat = [(s, job) for s in sorted(jobs) for job in jobs[s]]
    index = {job: i for i, (s, job) in enumerate(flat)}
    x_loaded = [sem(f"x1_loaded{i}") for i in range(XR)]
    xn_ready, xT_done, h_hi_ready, h_lo_ready = sem("xn_ready"), sem("xT_done"), sem("h_hi_ready"), sem("h_lo_ready")
    h_mod = sem("h_mod")
    w_loaded = [sem(f"w_in_loaded{i}") for i in range(WR)]
    w_hi_ready, w_lo_ready, z_done = sem("w_in_hi"), sem("w_in_lo"), sem("z_done")
    z_act, z_dve = sem("z_out_act"), sem("z_out_dve")
    side_done = sem("side_done")
    side_act = sem("side_out_act")
    pads_set, conv_s, conv_p = sem("pads_set"), sem("conv_sample_taps"), sem("conv_prompt_taps")
    ln_cent, ln_sq, ln_r, ln_norm, ln_out = sem("ln_centred"), sem("ln_square"), sem("ln_rstd"), sem("ln_normed"), sem("ln_out")
    ln_log, qk_log, qk_r, qk_out, v_out = sem("ln_log"), sem("qk_log"), sem("qk_rstd"), sem("qk_out"), sem("v_out")
    stored = [sem(f"z_stored{i}") for i in range(3)]
    conv_mul = sem("conv_prompt_products")

    acts = [1 if kind in ("gate", "q", "k", "v") else 0 for kind, _ in Z_TILES]
    dves = [1 if kind in ("value", "q", "k") else 0 for kind, _ in Z_TILES]
    s_act = [1 if job[0] in ("var", "ss") else 0 for _, job in flat]
    stores = []
    for s in range(NZ + 3):
        if s - 1 < NZ and s >= 1 and Z_TILES[s - 1][0] in "qk":
            stores.append((s, "qk", s - 1))
        if s - 1 < NZ and s >= 1 and Z_TILES[s - 1][0] == "v":
            stores.append((s, "v", s - 1))
        for j in range(4):
            if s == CONV_DONE[j] + 2:
                stores.append((s, "conv", j))
    store_no = {(what, i): n for n, (_, what, i) in enumerate(stores)}

    with ExitStack() as c:
        h_hi = sb(c, "h_hi", [P, KD, TOKENS], F32R)
        h_lo = sb(c, "h_lo", [P, KD, TOKENS], F32R)
        psZ = ps(c, "psZ", [P, 6, 512])
        psS = ps(c, "psS", [P, 2, 512])
        with ExitStack() as c2:
            xt = sb(c2, "xt1", [P, XR, D])
            xn = sb(c2, "xn", [P, 2, D])
            hm = sb(c2, "hm", [P, 2, KD, P])
            with nc.Block() as block:
                @block.sync
                def _(sp):
                    for t in range(TILES):
                        if t >= XR:
                            sp.wait_ge(xn_ready, t - XR + 1)
                        sp.dma_start(xt[:, t % XR, :], rows_of(x_d, t)).then_inc(x_loaded[t % XR], 16)

                @block.vector
                def _(dve):
                    for t in range(TILES + 1):
                        if t < TILES:
                            dve.wait_ge(x_loaded[t % XR], 16 * (t // XR + 1))
                            if t >= 2:
                                dve.wait_ge(xT_done, t - 1)
                            dve.tensor_scalar(xn[:, t % 2, :], xt[:, t % XR, :], rstd1[:, t:t + 1], None,
                                              ALU.mult).then_inc(xn_ready, 1)
                        if t >= 1:
                            u = t - 1
                            dve.wait_ge(h_hi_ready, u + 1)
                            dve.tensor_tensor(h_lo[:, :, u * P:(u + 1) * P], hm[:, u % 2],
                                              h_hi[:, :, u * P:(u + 1) * P].bitcast(F32),
                                              ALU.subtract).then_inc(h_lo_ready, 1)

                @block.tensor
                def _(pe):
                    for t in range(TILES):
                        pe.wait_ge(xn_ready, t + 1)
                        if t >= 2:
                            pe.wait_ge(h_mod, t - 1)
                        xk = xn[:, t % 2, :].rearrange("p (d k) -> p k d", k=KD)
                        for k in range(KD):
                            mm = pe.transpose(psZ[:, 2 * (t % 2) + k // 4, (k % 4) * P:(k % 4 + 1) * P],
                                              xk[:, k, :], ident[:, :])
                        mm.then_inc(xT_done, 1)

                @block.scalar
                def _(act):
                    for t in range(TILES):
                        act.wait_ge(xT_done, t + 1)
                        if t >= 2:
                            act.wait_ge(h_lo_ready, t - 1)
                        for k in range(KD):
                            m = act.activation(hm[:, t % 2, k, :],
                                               psZ[:, 2 * (t % 2) + k // 4, (k % 4) * P:(k % 4 + 1) * P], ACT.Identity,
                                               bias=modv[:, group(t), 0, k:k + 1], scale=a1[:, group(t), k:k + 1])
                        m.then_inc(h_mod, 1)
                        act.wait_ge(h_mod, t + 1)
                        act.activation(h_hi[:, :, t * P:(t + 1) * P], hm[:, t % 2], ACT.Copy).then_inc(h_hi_ready, 1)

        with ExitStack() as c2:
            w_raw = sb(c2, "w_raw", [P, WR, KD, P])
            w_hi = sb(c2, "w_hi", [P, 2, KD, P], F32R)
            w_lo = sb(c2, "w_lo", [P, 2, KD, P], F32R)
            sg = sb(c2, "sg", [P, TOKENS])
            UW = TOKENS + 4 * PAD
            u = sb(c2, "u", [P, 3, UW])
            acc = sb(c2, "acc", [P, 2, TOKENS])
            sqz = sb(c2, "sqz", [P, 2, TOKENS])
            zg = sb(c2, "zg", [P, 2, TOKENS])
            rr = sb(c2, "rr", [P, TOKENS])
            U_P, U_S = 0, PROMPT + 2 * PAD

            w_v = A["w_in"].rearrange("(p k) n -> p k n", k=KD)
            prod = sb(c2, "prod", [P, 2, PROMPT])
            lnr = sb(c2, "lnr", [P, TOKENS])

            def chunk(n):
                return slice(n * 512, (n + 1) * 512)

            def by_block(ap):
                return ap.rearrange("p (r j c) -> p j r c", j=COL_BLOCKS, c=Q_COLS)

            with nc.Block() as block:
                @block.sync
                def _(sp):
                    def load(ct):
                        if ct >= WR:
                            sp.wait_ge(w_lo_ready, ct - WR + 1)
                        kind, j = Z_TILES[ct]
                        col = Z_COL0[kind] + j * P
                        sp.dma_start(w_raw[:, ct % WR], w_v[:, :, col:col + P]).then_inc(w_loaded[ct % WR], 16)
                    for ct in range(WR):
                        load(ct)
                    loads, n = WR, 0
                    for s in range(NZ + 3):
                        if 2 <= s and loads < NZ:
                            load(loads)
                            loads += 1
                        while n < len(stores) and stores[n][0] == s:
                            _, what, i = stores[n]
                            if what == "qk":
                                sp.wait_ge(qk_out, NCH * (sum(1 for k, _ in Z_TILES[:i + 1] if k in "qk")))
                                sp.dma_start(qk_d[(0 if Z_TILES[i][0] == "q" else 4) + Z_TILES[i][1]],
                                             zg[:, i % 2, :]).then_inc(stored[n % 3], 16)
                            elif what == "v":
                                sp.wait_ge(v_out, NCH * (Z_TILES[i][1] + 1))
                                sp.dma_start(v_d.rearrange("(t p) c -> p t c", p=P)[:, :, Z_TILES[i][1] * P:(Z_TILES[i][1] + 1) * P],
                                             zg[:, i % 2, :].rearrange("p (t c) -> p t c", c=P)).then_inc(stored[n % 3], 16)
                            else:
                                sp.wait_ge(ln_out, i + 1)
                                sp.dma_start(conv_d[i], acc[:, i % 2, :]).then_inc(stored[n % 3], 16)
                            n += 1
                    while loads < NZ:
                        load(loads)
                        loads += 1
                    for i in range(3):
                        sp.wait_ge(stored[i], 16 * len([1 for n in range(len(stores)) if n % 3 == i]))

                def wait_store(eng, what, i):
                    n = store_no[(what, i)]
                    eng.wait_ge(stored[n % 3], 16 * (n // 3 + 1))

                @block.tensor
                def _(pe):
                    done = [0]

                    def side(job):
                        i = index[job]
                        if i >= 2:
                            was, wj, wn = flat[i - 2][1]
                            if was in ("var", "ss"):
                                pe.wait_ge(side_act, sum(s_act[:i - 1]))
                            elif was == "mean":
                                pe.wait_ge(ln_cent, NCH * wj + wn + 1)
                            else:
                                pe.wait_ge(v_out, NCH * Z_TILES[wj][1] + wn + 1)
                        kind, j, n = job
                        bank = psS[:, i % 2, :]
                        if kind == "mean":
                            pe.wait_ge(conv_s, CONV_K * (j + 1))
                            pe.wait_ge(conv_p, CONV_K * (j + 1))
                            mm = pe.matmul(bank, ones64[:, :], acc[:, j % 2, chunk(n)], start=True, stop=True)
                        elif kind == "var":
                            pe.wait_ge(ln_sq, NCH * j + n + 1)
                            mm = pe.matmul(bank, ones64[:, :], lnr[:, chunk(n)], start=True, stop=True)
                        elif kind == "ss":
                            pe.wait_ge(z_act, sum(acts[:j + 1]))
                            mm = pe.matmul(bank, ones64[:, :], sqz[:, j % 2, chunk(n)], start=True, stop=True)
                        else:
                            pe.wait_ge(z_act, sum(acts[:j + 1]))
                            for b in range(4):
                                mm = pe.transpose(bank[:, b * P:(b + 1) * P],
                                                  sqz[:, j % 2, (4 * n + b) * P:(4 * n + b + 1) * P], ident[:, :])
                        mm.then_inc(side_done, 1)
                        assert i == done[0]
                        done[0] += 1

                    for s in range(NZ + 3):
                        todo = list(jobs[s])
                        per = -(-len(todo) // NCH)
                        for n in range(NCH):
                            if s < NZ:
                                if n == 0:
                                    pe.wait_ge(w_lo_ready, s + 1)
                                    if s >= 2:
                                        if acts[s - 2]:
                                            pe.wait_ge(z_act, sum(acts[:s - 1]))
                                        if dves[s - 2]:
                                            pe.wait_ge(z_dve, sum(dves[:s - 1]))
                                bank = psZ[:, 3 * (s % 2) + n, :]
                                for k in range(KD):
                                    pe.matmul(bank, w_hi[:, s % 2, k, :], h_hi[:, k, chunk(n)], start=(k == 0), stop=False)
                                    pe.matmul(bank, w_hi[:, s % 2, k, :], h_lo[:, k, chunk(n)], start=False, stop=False)
                                    mm = pe.matmul(bank, w_lo[:, s % 2, k, :], h_hi[:, k, chunk(n)], start=False,
                                                   stop=(k == KD - 1))
                                if n == NCH - 1:
                                    mm.then_inc(z_done, 1)
                            for job in todo[per * n:per * (n + 1)]:
                                side(job)

                @block.scalar
                def _(act):
                    def hi(ct):
                        act.wait_ge(w_loaded[ct % WR], 16 * (ct // WR + 1))
                        if ct >= 2:
                            act.wait_ge(z_done, ct - 1)
                        act.activation(w_hi[:, ct % 2], w_raw[:, ct % WR], ACT.Copy).then_inc(w_hi_ready, 1)

                    hi(0)
                    for s in range(NZ + 3):
                        if s + 1 < NZ:
                            hi(s + 1)
                        for job in jobs[s]:
                            kind, j, n = job
                            i = index[job]
                            if kind == "mean":
                                act.wait_ge(ln_cent, NCH * j + n + 1)
                                if j >= 1:
                                    act.wait_ge(ln_norm, NCH * j)
                                act.activation(lnr[:, chunk(n)], acc[:, j % 2, chunk(n)], ACT.Square).then_inc(ln_sq, 1)
                            elif kind == "var":
                                act.wait_ge(side_done, i + 1)
                                act.activation(lnr[:, chunk(n)], psS[:, i % 2, :], ACT.Ln, bias=eps_col[:, :]).then_inc(side_act, 1)
                                act.wait_ge(side_act, sum(s_act[:i + 1]))
                                act.activation(lnr[:, chunk(n)], lnr[:, chunk(n)], ACT.Exp, scale=-0.5).then_inc(ln_r, 1)
                            elif kind == "ss":
                                act.wait_ge(side_done, i + 1)
                                before = sum(1 for k, _ in Z_TILES[:j] if k in "qk")
                                if before:
                                    act.wait_ge(qk_out, NCH * (before - 1) + n + 1)
                                act.activation(rr[:, chunk(n)], psS[:, i % 2, :], ACT.Ln, bias=eps_col[:, :]).then_inc(side_act, 1)
                                act.wait_ge(side_act, sum(s_act[:i + 1]))
                                act.activation(rr[:, chunk(n)], rr[:, chunk(n)], ACT.Exp, scale=-0.5).then_inc(qk_r, 1)
                        for j in range(4):
                            if s == CONV_DONE[j] + 2:
                                act.wait_ge(ln_norm, NCH * (j + 1))
                                act.activation(acc[:, j % 2, :], acc[:, j % 2, :], ACT.Silu, bias=convp[:, j, CONV_K + 2:CONV_K + 3],
                                               scale=convp[:, j, CONV_K + 1:CONV_K + 2]).then_inc(ln_out, 1)
                        if s < NZ:
                            kind, j = Z_TILES[s]
                            prods = psZ[:, 3 * (s % 2):3 * (s % 2) + 3, :].rearrange("p a b -> p (a b)")
                            if kind != "value":
                                act.wait_ge(z_done, s + 1)
                            if kind == "gate":
                                if j >= 1:
                                    act.wait_ge(z_dve, j)
                                act.activation(sg[:, :], prods, ACT.Sigmoid).then_inc(z_act, 1)
                            elif kind in "qk":
                                act.activation(sqz[:, s % 2, :], prods, ACT.Square).then_inc(z_act, 1)
                            elif kind == "v":
                                act.activation(sqz[:, s % 2, :], prods, ACT.Copy).then_inc(z_act, 1)

                def tap(eng, lo, n, at, j, t, counter):
                    src = u[:, j % 3, at + t:at + t + n]
                    dst = acc[:, j % 2, lo:lo + n]
                    if t == 0:
                        eng.tensor_scalar(dst, src, convp[:, j, 0:1], convp[:, j, CONV_K:CONV_K + 1],
                                          ALU.mult, ALU.add).then_inc(counter, 1)
                    elif counter is conv_s:
                        eng.wait_ge(counter, CONV_K * j + t)
                        eng.scalar_tensor_tensor(out=dst, in0=src, scalar=convp[:, j, t:t + 1], in1=dst,
                                                 op0=ALU.mult, op1=ALU.add).then_inc(counter, 1)
                    else:
                        if t >= 3:
                            eng.wait_ge(counter, CONV_K * j + t - 1)
                        eng.tensor_scalar(prod[:, t % 2, :], src, convp[:, j, t:t + 1], None, ALU.mult).then_inc(conv_mul, 1)
                        eng.wait_ge(conv_mul, (CONV_K - 1) * j + t)
                        eng.wait_ge(counter, CONV_K * j + t)
                        eng.tensor_tensor(dst, dst, prod[:, t % 2, :], ALU.add).then_inc(counter, 1)

                @block.gpsimd
                def _(pool):
                    for b in range(3):
                        for at in (U_P, U_P + PAD + PROMPT, U_S, U_S + PAD + SAMPLE):
                            m = pool.memset(u[:, b, at:at + PAD], 0.0)
                    m.then_inc(pads_set, 1)
                    pool.wait_ge(pads_set, 1)
                    for j in range(4):
                        pool.wait_ge(z_dve, j + 1)
                        if j >= 2:
                            wait_store(pool, "conv", j - 2)
                        for t in range(CONV_K):
                            tap(pool, 0, PROMPT, U_P, j, t, conv_p)

                @block.vector
                def _(dve):
                    def lo(ct):
                        dve.wait_ge(w_hi_ready, ct + 1)
                        dve.tensor_tensor(w_lo[:, ct % 2], w_raw[:, ct % WR], w_hi[:, ct % 2].bitcast(F32),
                                          ALU.subtract).then_inc(w_lo_ready, 1)
                    lo(0)
                    taps = 0
                    dve.wait_ge(pads_set, 1)
                    for s in range(NZ + 3):
                        if s + 1 < NZ:
                            lo(s + 1)
                        if s >= 2:
                            for _ in range(TAPS_STEP):
                                if taps < 4 * CONV_K:
                                    j, t = divmod(taps, CONV_K)
                                    if t == 0:
                                        dve.wait_ge(z_dve, j + 1)
                                        if j >= 2:
                                            wait_store(dve, "conv", j - 2)
                                    tap(dve, PROMPT, SAMPLE, U_S, j, t, conv_s)
                                    taps += 1
                        for job in jobs[s]:
                            kind, j, n = job
                            i = index[job]
                            if kind == "mean":
                                dve.wait_ge(side_done, i + 1)
                                dve.tensor_tensor(acc[:, j % 2, chunk(n)], acc[:, j % 2, chunk(n)], psS[:, i % 2, :],
                                                  ALU.subtract).then_inc(ln_cent, 1)
                            elif kind == "var":
                                dve.wait_ge(ln_r, NCH * j + n + 1)
                                dve.tensor_tensor(acc[:, j % 2, chunk(n)], acc[:, j % 2, chunk(n)], lnr[:, chunk(n)],
                                                  ALU.mult).then_inc(ln_norm, 1)
                            elif kind == "ss":
                                before = sum(1 for k, _ in Z_TILES[:j] if k in "qk")
                                dve.wait_ge(z_dve, sum(dves[:j + 1]))
                                dve.wait_ge(qk_r, NCH * before + n + 1)
                                out, r = zg[:, j % 2, chunk(n)], rr[:, chunk(n)]
                                if Z_TILES[j][0] == "q":
                                    out, r = out.rearrange("p (j r c) -> p j r c", j=COL_BLOCKS, c=Q_COLS), by_block(r)
                                dve.tensor_tensor(out, out, r, ALU.mult).then_inc(qk_out, 1)
                            else:
                                dve.wait_ge(side_done, i + 1)
                                if n == 0:
                                    wait_store(dve, "v" if Z_TILES[j - 2][0] == "v" else "qk", j - 2)
                                dve.tensor_copy(zg[:, j % 2, chunk(n)], psS[:, i % 2, :]).then_inc(v_out, 1)
                        if s < NZ:
                            kind, j = Z_TILES[s]
                            if kind == "value":
                                dve.wait_ge(z_done, s + 1)
                                dve.wait_ge(z_act, j + 1)
                                if j >= 3:
                                    dve.wait_ge(conv_s, CONV_K * (j - 2))
                                    dve.wait_ge(conv_p, CONV_K * (j - 2))
                                p0 = psZ[:, 3 * (s % 2), :]
                                p1 = psZ[:, 3 * (s % 2) + 1:3 * (s % 2) + 3, :].rearrange("p a b -> p (a b)")
                                dve.tensor_tensor(u[:, j % 3, U_P + PAD:U_P + PAD + PROMPT], p0, sg[:, 0:PROMPT], ALU.mult)
                                dve.tensor_tensor(u[:, j % 3, U_S + PAD:U_S + PAD + SAMPLE], p1, sg[:, PROMPT:TOKENS],
                                                  ALU.mult).then_inc(z_dve, 1)
                            elif kind in "qk":
                                dve.wait_ge(z_act, sum(acts[:s + 1]))
                                if Z_TILES[s - 2][0] in "qk":
                                    wait_store(dve, "qk", s - 2)
                                col = 0 if kind == "q" else 1
                                for n in range(NCH):
                                    out, prods = zg[:, s % 2, chunk(n)], psZ[:, 3 * (s % 2) + n, :]
                                    if kind == "q":
                                        out = out.rearrange("p (j r c) -> p j r c", j=COL_BLOCKS, c=Q_COLS)
                                        prods = by_block(prods)
                                    m = dve.tensor_scalar(out, prods, qkg[:, col:col + 1],
                                                          DH ** -0.5 if kind == "q" else 1.0, ALU.mult, ALU.mult)
                                m.then_inc(z_dve, 1)


def attend(nc, A, sem, sb, ps, qk_d, v_d, ident, o_nat):
    NB = len(BLOCKS)
    UNITS = HEADS * NB
    qk_loaded = [sem(f"qk_loaded{i}") for i in range(4)]
    v_loaded = sem("v_loaded")
    bias_loaded = [sem(f"bias_loaded{i}") for i in range(2)]
    s_done, s_biased, m_neg, p_ready = sem("s_done"), sem("s_biased"), sem("m_neg"), sem("p_ready")
    pT_done, pT_out, o_done, r_ready, o_out = sem("pT_done"), sem("pT_out"), sem("o_done"), sem("r_ready"), sem("o_out")
    with ExitStack() as c:
        qk = sb(c, "qk", [P, 8, TOKENS])
        v = sb(c, "v", [P, len(V_ROWS) * COL_BLOCKS, WA])
        bias = sb(c, "bias", [P, 2, 3, BIAS_COLS])
        sc = sb(c, "sc", [P, 2, 384])
        pr = sb(c, "pr", [P, 2, 384])
        pT = sb(c, "pT", [P, 2, 384])
        mx = sb(c, "mx", [P, 4])
        nm = sb(c, "nm", [P, 4])
        sm = sb(c, "sm", [P, 4])
        rs = sb(c, "rs", [P, 4])
        psS = ps(c, "psSc", [P, 3, 512])
        psT = ps(c, "psPT", [P, 2, 512])
        psO = ps(c, "psOh", [P, 3, 512])

        def unit(i):
            h, b = divmod(i, NB)
            return h, b, *BLOCKS[b]

        with nc.Block() as block:
            @block.sync
            def _(sp):
                def heads(t):
                    for w in range(2):
                        sp.dma_start(qk[:, 4 * w + t, :], qk_d[4 * w + t]).then_inc(qk_loaded[t], 16)
                def biases(h):
                    if h >= 2:
                        sp.wait_ge(s_biased, NB * (h - 1))
                    sp.dma_start(bias[:, h % 2], A["bias"][h]).then_inc(bias_loaded[h % 2], 16)
                heads(0)
                biases(0)
                for n, (t0, r0) in enumerate(V_ROWS):
                    for j in range(COL_BLOCKS):
                        for r in range(4):
                            at = t0 + (r0 + r) * GRID_W + KEY_COL0[j]
                            sp.dma_start(v[r * K_COLS:(r + 1) * K_COLS, n * COL_BLOCKS + j, :],
                                         v_d[at:at + K_COLS, :]).then_inc(v_loaded, 16)
                biases(1)
                for t in range(1, 4):
                    heads(t)
                for h in range(2, HEADS):
                    biases(h)

            @block.tensor
            def _(pe):
                def scores(i):
                    h, b, s, j = unit(i)
                    t0, qr, kr, rows, _, _ = ROW_SETS[s]
                    if b == 0 and h % 2 == 0:
                        pe.wait_ge(qk_loaded[h // 2], 32)
                    if i >= 3:
                        pe.wait_ge(s_biased, i - 2)
                    lo = DH * (h % 2)
                    at = t0 + qr * GRID_W + j * P
                    q = qk[lo:lo + DH, h // 2, at:at + P]
                    k = qk[lo:lo + DH, 4 + h // 2, t0 + kr * GRID_W:t0 + (kr + rows) * GRID_W].rearrange(
                        "p (r c) -> p r c", c=GRID_W)[:, :, KEY_COL0[j]:KEY_COL0[j] + K_COLS]
                    pe.matmul(psS[:, i % 3, 0:rows * K_COLS], q, k, start=True, stop=True).then_inc(s_done, 1)

                def turn(i):
                    h, b, s, j = unit(i)
                    n = ROW_SETS[s][3] // 4
                    pe.wait_ge(p_ready, i + 1)
                    if i >= 2:
                        pe.wait_ge(pT_out, i - 1)
                    for m in range(n):
                        mm = pe.transpose(psT[:, i % 2, m * P:(m + 1) * P], pr[:, i % 2, m * P:(m + 1) * P], ident[:, :])
                    mm.then_inc(pT_done, 1)

                def pv(i):
                    h, b, s, j = unit(i)
                    t0, qr, kr, rows, _, _ = ROW_SETS[s]
                    first = V_ROWS.index((t0, kr))
                    pe.wait_ge(pT_out, i + 1)
                    if i == 0:
                        pe.wait_ge(v_loaded, 16 * 4 * len(V_ROWS) * COL_BLOCKS)
                    if i >= 3:
                        pe.wait_ge(o_out, i - 2)
                    for m in range(rows // 4):
                        mm = pe.matmul(psO[:, i % 3, 0:DH], pT[:, i % 2, m * P:(m + 1) * P],
                                       v[:, (first + m) * COL_BLOCKS + j, h * DH:(h + 1) * DH],
                                       start=(m == 0), stop=(m == rows // 4 - 1))
                    mm.then_inc(o_done, 1)

                for i in range(UNITS + 3):
                    if i < UNITS:
                        scores(i)
                    if 2 <= i < UNITS + 2:
                        turn(i - 2)
                    if i >= 3:
                        pv(i - 3)

            @block.vector
            def _(dve):
                for i in range(UNITS + 4):
                    if i < UNITS:
                        h, b, s, j = unit(i)
                        w = ROW_SETS[s][3] * K_COLS
                        at = ROW_SETS[s][5]
                        if b == 0:
                            dve.wait_ge(bias_loaded[h % 2], 16 * (h // 2 + 1))
                        dve.wait_ge(s_done, i + 1)
                        if i >= 2:
                            dve.wait_ge(p_ready, i - 1)
                        dve.tensor_tensor_reduce(out=sc[:, i % 2, 0:w], in0=psS[:, i % 3, 0:w],
                                                 in1=bias[:, h % 2, PATTERN[j], at:at + w], scale=1.0, scalar=-3e38,
                                                 op0=ALU.add, op1=ALU.max, accum_out=mx[:, i % 4:i % 4 + 1]).then_inc(s_biased, 1)
                        dve.wait_ge(s_biased, i + 1)
                        dve.tensor_scalar(nm[:, i % 4:i % 4 + 1], mx[:, i % 4:i % 4 + 1], -1.0, None,
                                          ALU.mult).then_inc(m_neg, 1)
                    if 2 <= i < UNITS + 2:
                        dve.wait_ge(p_ready, i - 1)
                        if i >= 6:
                            dve.wait_ge(o_out, i - 5)
                        dve.reciprocal(rs[:, (i - 2) % 4:(i - 2) % 4 + 1], sm[:, (i - 2) % 4:(i - 2) % 4 + 1]).then_inc(r_ready, 1)
                    if i >= 4:
                        e = i - 4
                        h, b, s, j = unit(e)
                        dve.wait_ge(o_done, e + 1)
                        dve.wait_ge(r_ready, e + 1)
                        dve.tensor_scalar(o_nat[:, b, h * DH:(h + 1) * DH], psO[:, e % 3, 0:DH], rs[:, e % 4:e % 4 + 1],
                                          None, ALU.mult).then_inc(o_out, 1)

            @block.scalar
            def _(act):
                for i in range(UNITS + 2):
                    if i < UNITS:
                        h, b, s, j = unit(i)
                        w = ROW_SETS[s][3] * K_COLS
                        act.wait_ge(m_neg, i + 1)
                        if i >= 2:
                            act.wait_ge(pT_done, i - 1)
                        if i >= 4:
                            act.wait_ge(r_ready, i - 3)
                        act.activation(pr[:, i % 2, 0:w], sc[:, i % 2, 0:w], ACT.Exp, bias=nm[:, i % 4:i % 4 + 1],
                                       accum_out=sm[:, i % 4:i % 4 + 1]).then_inc(p_ready, 1)
                    if i >= 1 and i - 1 < UNITS:
                        e = i - 1
                        w = ROW_SETS[unit(e)[2]][3] * K_COLS
                        act.wait_ge(pT_done, e + 1)
                        if e >= 2:
                            act.wait_ge(o_done, e - 1)
                        act.activation(pT[:, e % 2, 0:w], psT[:, e % 2, 0:w], ACT.Copy).then_inc(pT_out, 1)


def mix(nc, A, sem, sb, ps, rows_of, x_d, y_d, ada_d, conv_d, xhat_d, ident, eps_col, modv, a2, affT, o_nat):
    NB = len(BLOCKS)
    XR = 3
    conv_loaded, gate_loaded = sem("conv_loaded"), sem("gate1_loaded")
    w_loaded = [sem(f"w_out_loaded{i}") for i in range(2)]
    w_hi_ready, w_lo_ready = sem("w_out_hi"), sem("w_out_lo")
    oT_done, oT_act, oT_dve = sem("oT_done"), sem("oT_out_act"), sem("oT_out_dve")
    m_hi, m_lo, mixed = sem("mix_hi"), sem("mix_lo"), sem("mixed")
    x_loaded = [sem(f"x3_loaded{i}") for i in range(XR)]
    gated, x1_ready, sq_done, ms_done, rt_done, r_done, xh_ready = (
        sem("gated"), sem("x1_ready"), sem("x1_sq"), sem("x1_ms"), sem("x1_rt"), sem("x1_rstd"), sem("xh_ready"))
    x1_stored = [sem(f"x1_stored{i}") for i in range(XR)]
    xh_stored = [sem(f"xh_stored{i}") for i in range(2)]
    xhT_done, h2_ready, logit_done, l_max, l_neg, l_exp, l_rec, aff_ready, aff_t, aff_out, wr_loaded, aff_zero = (
        sem("xhT_done"), sem("h2_ready"), sem("logit_done"), sem("l_max"), sem("l_neg"), sem("l_exp"), sem("l_rec"),
        sem("aff_ready"), sem("aff_turned"), sem("aff_out"), sem("w_router_loaded"), sem("aff_zero"))
    with ExitStack() as c:
        conv = sb(c, "conv3", [P, 4, TOKENS])
        attn = sb(c, "attn3", [P, 4, TOKENS])
        w_raw = sb(c, "wo_raw", [P, 2, D])
        w_hi = sb(c, "wo_hi", [P, KD, D], F32R)
        w_lo = sb(c, "wo_lo", [P, KD, D], F32R)
        mh = sb(c, "mh", [P, 2, KD, P], F32R)
        ml = sb(c, "ml", [P, 2, KD, P], F32R)
        gate1 = sb(c, "gate1", [P, 2, D])
        xt = sb(c, "xt3", [P, XR, D])
        tg = sb(c, "tg", [P, 2, D])
        xh = sb(c, "xh", [P, 2, D])
        h2 = sb(c, "h2", [P, KD, P])
        wr = sb(c, "wr", [P, KD, EXPERTS])
        st = sb(c, "st3", [P, 4, TILES])
        lg = sb(c, "lg", [P, 4, 2])
        ex = sb(c, "ex", [P, 2, EXPERTS])
        af = sb(c, "af", [P, 2, 48])
        psO = ps(c, "psMix", [P, 4, 512])
        psT = ps(c, "psXT", [P, 2, 512])
        psL = ps(c, "psLog", [P, 2, 512])

        with nc.Block() as block:
            @block.sync
            def _(sp):
                for k in range(KD):
                    if k >= 2:
                        sp.wait_ge(w_lo_ready, k - 1)
                    sp.dma_start(w_raw[:, k % 2, :], A["w_out"][k * P:(k + 1) * P, :]).then_inc(w_loaded[k % 2], 16)
                for j in range(4):
                    sp.dma_start(conv[:, j, :], conv_d[j]).then_inc(conv_loaded, 16)
                for grp in range(2):
                    sp.dma_start(gate1[:, grp, :], ada_d[grp:grp + 1, 2 * D:3 * D].to_broadcast([P, D])).then_inc(gate_loaded, 16)
                sp.dma_start(wr[:, :, :], A["w_router"].rearrange("(p k) n -> p k n", k=KD)).then_inc(wr_loaded, 16)
                for s in range(TILES + 2):
                    if s < TILES:
                        if s >= XR:
                            sp.wait_ge(x1_stored[s % XR], 16 * (s // XR))
                            sp.wait_ge(xh_ready, s - XR + 1)
                        sp.dma_start(xt[:, s % XR, :], rows_of(x_d, s)).then_inc(x_loaded[s % XR], 16)
                    if s >= 2:
                        t = s - 2
                        sp.wait_ge(x1_ready, t + 1)
                        sp.dma_start(rows_of(y_d, t), xt[:, t % XR, :]).then_inc(x1_stored[t % XR], 16)
                        sp.wait_ge(xh_ready, t + 1)
                        sp.dma_start(xhat_d[t * P:(t + 1) * P, :], xh[:, t % 2, :]).then_inc(xh_stored[t % 2], 16)
                for i in range(XR):
                    sp.wait_ge(x1_stored[i], 16 * (TILES // XR))
                for i in range(2):
                    sp.wait_ge(xh_stored[i], 16 * (TILES // 2))

            @block.gpsimd
            def _(pool):
                pool.memset(af[:, :, :], 0.0).then_inc(aff_zero, 1)
                pool.memset(affT[:, :], -1.0).then_inc(aff_zero, 1)

            @block.tensor
            def _(pe):
                for b in range(NB):
                    if b >= 4:
                        if b % 2:
                            pe.wait_ge(oT_dve, (b - 4) // 2 + 1)
                        else:
                            pe.wait_ge(oT_act, (b - 4) // 2 + 1)
                    for k in range(4):
                        mm = pe.transpose(psO[:, b % 4, k * P:(k + 1) * P], o_nat[:, b, k * P:(k + 1) * P], ident[:, :])
                    mm.then_inc(oT_done, 1)
                for s in range(TILES + 2):
                    if s < TILES:
                        pe.wait_ge(m_lo, s + 1)
                        if s == 0:
                            pe.wait_ge(w_lo_ready, KD)
                        if s >= 2:
                            pe.wait_ge(gated, s - 1)
                        for n in range(2):
                            for k in range(KD):
                                for i, (m, w) in enumerate(((mh, w_hi), (mh, w_lo), (ml, w_hi))):
                                    mm = pe.matmul(psO[:, 2 * (s % 2) + n, :], m[:, s % 2, k, :],
                                                   w[:, k, n * 512:(n + 1) * 512], start=(k == 0 and i == 0),
                                                   stop=(k == KD - 1 and i == 2))
                        mm.then_inc(mixed, 1)
                    if 1 <= s < TILES + 1:
                        t = s - 1
                        pe.wait_ge(xh_ready, t + 1)
                        if t >= 1:
                            pe.wait_ge(h2_ready, t)
                        xk = xh[:, t % 2, :].rearrange("p (d k) -> p k d", k=KD)
                        for k in range(KD):
                            mm = pe.transpose(psT[:, k // 4, (k % 4) * P:(k % 4 + 1) * P], xk[:, k, :], ident[:, :])
                        mm.then_inc(xhT_done, 1)
                        pe.wait_ge(h2_ready, t + 1)
                        if t >= 1:
                            pe.wait_ge(l_exp, t)
                        for k in range(KD):
                            mm = pe.matmul(psL[:, 0, 0:EXPERTS], h2[:, k, :], wr[:, k, :], start=(k == 0), stop=(k == KD - 1))
                        mm.then_inc(logit_done, 1)
                    if s >= 2:
                        t = s - 2
                        pe.wait_ge(aff_ready, t + 1)
                        if t >= 1:
                            pe.wait_ge(aff_out, t)
                        pe.transpose(psL[0:48, 1, 0:P], af[:, t % 2, :], ident[:, :]).then_inc(aff_t, 1)

            def oT(eng, b, counter):
                s, j = BLOCKS[b]
                t0, qr, _, _, _, _ = ROW_SETS[s]
                eng.wait_ge(oT_done, b + 1)
                dst = attn[:, :, t0 + qr * GRID_W:t0 + (qr + 8) * GRID_W].rearrange(
                    "p k (r c) -> p k r c", c=GRID_W)
                for k in range(4):
                    d = dst[:, k, :, j * Q_COLS:(j + 1) * Q_COLS]
                    src = psO[:, b % 4, k * P:(k + 1) * P].rearrange("p (r c) -> p r c", c=Q_COLS)
                    m = eng.tensor_copy(d, src) if counter is oT_dve else eng.activation(d, src, ACT.Copy)
                m.then_inc(counter, 1)

            @block.scalar
            def _(act):
                for k in range(KD):
                    act.wait_ge(w_loaded[k % 2], 16 * (k // 2 + 1))
                    act.activation(w_hi[:, k, :], w_raw[:, k % 2, :], ACT.Copy).then_inc(w_hi_ready, 1)
                for b in range(0, NB, 2):
                    oT(act, b, oT_act)

                def split(t):
                    if t >= 2:
                        act.wait_ge(mixed, t - 1)
                    act.activation(mh[:, t % 2, 0:4], attn[:, :, t * P:(t + 1) * P], ACT.Copy)
                    act.activation(mh[:, t % 2, 4:8], conv[:, :, t * P:(t + 1) * P], ACT.Copy).then_inc(m_hi, 1)
                act.wait_ge(oT_dve, NB // 2)
                act.wait_ge(oT_act, NB // 2)
                act.wait_ge(conv_loaded, 64)
                act.wait_ge(aff_zero, 2)
                split(0)
                for s in range(TILES + 2):
                    if s + 1 < TILES:
                        split(s + 1)
                    if 1 <= s < TILES + 1:
                        t = s - 1
                        act.wait_ge(x1_ready, t + 1)
                        act.activation(tg[:, t % 2, :], xt[:, t % XR, :], ACT.Square,
                                       accum_out=st[:, 0, t:t + 1]).then_inc(sq_done, 1)
                        act.wait_ge(ms_done, t + 1)
                        act.activation(st[:, 2, t:t + 1], st[:, 1, t:t + 1], ACT.Sqrt).then_inc(rt_done, 1)
                        act.wait_ge(xhT_done, t + 1)
                        if t >= 1:
                            act.wait_ge(logit_done, t)
                        for k in range(KD):
                            m = act.activation(h2[:, k, :], psT[:, k // 4, (k % 4) * P:(k % 4 + 1) * P], ACT.Identity,
                                               bias=modv[:, group(t), 2, k:k + 1], scale=a2[:, group(t), k:k + 1])
                        m.then_inc(h2_ready, 1)
                        act.wait_ge(l_neg, t + 1)
                        if t >= 2:
                            act.wait_ge(aff_ready, t - 1)
                        act.activation(ex[:, t % 2, :], psL[:, 0, 0:EXPERTS], ACT.Exp, bias=lg[:, 1, t % 2:t % 2 + 1],
                                       accum_out=lg[:, 2, t % 2:t % 2 + 1]).then_inc(l_exp, 1)

            @block.vector
            def _(dve):
                for k in range(KD):
                    dve.wait_ge(w_hi_ready, k + 1)
                    dve.tensor_tensor(w_lo[:, k, :], w_raw[:, k % 2, :], w_hi[:, k, :].bitcast(F32),
                                      ALU.subtract).then_inc(w_lo_ready, 1)
                for b in range(1, NB, 2):
                    oT(dve, b, oT_dve)
                dve.wait_ge(oT_act, NB // 2)
                dve.wait_ge(oT_dve, NB // 2)
                dve.wait_ge(gate_loaded, 32)

                def split(t):
                    dve.wait_ge(m_hi, t + 1)
                    dve.tensor_tensor(ml[:, t % 2, 0:4], attn[:, :, t * P:(t + 1) * P], mh[:, t % 2, 0:4].bitcast(F32),
                                      ALU.subtract)
                    dve.tensor_tensor(ml[:, t % 2, 4:8], conv[:, :, t * P:(t + 1) * P], mh[:, t % 2, 4:8].bitcast(F32),
                                      ALU.subtract).then_inc(m_lo, 1)
                split(0)
                for s in range(TILES + 2):
                    if s + 1 < TILES:
                        split(s + 1)
                    if 1 <= s < TILES + 1:
                        t = s - 1
                        dve.wait_ge(mixed, t + 1)
                        dve.wait_ge(x_loaded[t % XR], 16 * (t // XR + 1))
                        if t >= 2:
                            dve.wait_ge(sq_done, t - 1)
                        dve.tensor_tensor(tg[:, t % 2, :], psO[:, 2 * (t % 2):2 * (t % 2) + 2, :].rearrange("p a b -> p (a b)"),
                                          gate1[:, group(t), :], ALU.mult).then_inc(gated, 1)
                        dve.wait_ge(gated, t + 1)
                        dve.tensor_tensor(xt[:, t % XR, :], xt[:, t % XR, :], tg[:, t % 2, :], ALU.add).then_inc(x1_ready, 1)
                        dve.wait_ge(sq_done, t + 1)
                        dve.tensor_scalar(st[:, 1, t:t + 1], st[:, 0, t:t + 1], 1.0 / D, EPS, ALU.mult, ALU.add).then_inc(ms_done, 1)
                        dve.wait_ge(rt_done, t + 1)
                        dve.reciprocal(st[:, 3, t:t + 1], st[:, 2, t:t + 1]).then_inc(r_done, 1)
                        dve.wait_ge(r_done, t + 1)
                        if t >= 2:
                            dve.wait_ge(xhT_done, t - 1)
                            dve.wait_ge(xh_stored[t % 2], 16 * (t // 2))
                        dve.tensor_scalar(xh[:, t % 2, :], xt[:, t % XR, :], st[:, 3, t:t + 1], None, ALU.mult).then_inc(xh_ready, 1)
                        dve.wait_ge(logit_done, t + 1)
                        dve.reduce_max(lg[:, 0, t % 2:t % 2 + 1], psL[:, 0, 0:EXPERTS], AX.X).then_inc(l_max, 1)
                        dve.wait_ge(l_max, t + 1)
                        dve.tensor_scalar(lg[:, 1, t % 2:t % 2 + 1], lg[:, 0, t % 2:t % 2 + 1], -1.0, None, ALU.mult).then_inc(l_neg, 1)
                        dve.wait_ge(l_exp, t + 1)
                        dve.reciprocal(lg[:, 3, t % 2:t % 2 + 1], lg[:, 2, t % 2:t % 2 + 1]).then_inc(l_rec, 1)
                        dve.wait_ge(l_rec, t + 1)
                        at = 32 * group(t)
                        if t >= 2:
                            dve.wait_ge(aff_t, t - 1)
                        if t == 4 or t == 5:
                            dve.memset(af[:, t % 2, 0:EXPERTS], 0.0)
                        dve.tensor_scalar(af[:, t % 2, at:at + EXPERTS], ex[:, t % 2, :], lg[:, 3, t % 2:t % 2 + 1], None,
                                          ALU.mult).then_inc(aff_ready, 1)
                    if s >= 2:
                        t = s - 2
                        grp = group(t)
                        dve.wait_ge(aff_t, t + 1)
                        col = t * P - (PROMPT if grp else 0)
                        dve.tensor_copy(affT[32 * grp:32 * grp + EXPERTS, col:col + P],
                                        psL[32 * grp:32 * grp + EXPERTS, 1, 0:P]).then_inc(aff_out, 1)


def experts(nc, A, sem, sb, ps, y_d, ada_d, xhat_d, ident, modv, a2, affT):
    RING_GU, RING_DN = 3, 3
    HS = 3
    ROUNDS = CAP_S // 8
    AHEAD, BEHIND = 2, 2
    top_v, top_i, top_d = sem("top_vals"), sem("top_idx"), sem("top_drop")
    idx_f, tT_done, sel_ready = sem("idx_float"), sem("top_turned"), sem("sel_ready")
    gate_loaded = sem("gate2_loaded")
    gu_loaded = [sem(f"w_gu_loaded{i}") for i in range(RING_GU)]
    dn_loaded = [sem(f"w_dn_loaded{i}") for i in range(RING_DN)]
    gu_hi, gu_lo = sem("w_gu_hi"), sem("w_gu_lo")
    dn_hi, dn_lo = sem("w_dn_hi"), sem("w_dn_lo")
    gu_done, dn_done = sem("gate_up_done"), sem("down_done")
    silu_done, hid_done, hid_hi, hid_lo = sem("silu_done"), sem("hid_done"), sem("hid_hi"), sem("hid_lo")
    pool_steps = sem("pool_steps")
    idx_now, g_loaded_p, g_loaded_s = sem("idx_now"), sem("gathered_p"), sem("gathered_s")
    x_turned, xs_ready, x_hi, x_lo = sem("x_turned"), sem("xe_staged"), sem("xe_hi"), sem("xe_lo")
    y_half, y_sent_s, y_sent_p, y_scaled = sem("y_half"), sem("scattered_s"), sem("scattered_p"), sem("y_scaled")

    def last_user(j, ring, count):
        return j - ring if j >= ring else max(range(j % ring, count, ring)) - count

    with ExitStack() as c:
        raw_gu = sb(c, "raw_gu", [P, RING_GU, 2, 2, KD * P])
        raw_dn = sb(c, "raw_dn", [P, RING_DN, 2, D])
        w_hi = sb(c, "w_gu_hi_part", [P, 2, 2, KD * P], F32R)
        w_lo = sb(c, "w_gu_lo_part", [P, 2, 2, KD * P], F32R)
        d_hi = sb(c, "w_dn_hi_part", [P, 2, D], F32R)
        d_lo = sb(c, "w_dn_lo_part", [P, 2, D], F32R)
        xg_s = sb(c, "xg_s", [P, D])
        xg_p = sb(c, "xg_p", [CAP_P, D])
        xst = sb(c, "xst", [P, KD, CAP])
        xhi = sb(c, "xhi", [P, KD, CAP], F32R)
        xlo = sb(c, "xlo", [P, KD, CAP], F32R)
        sl = sb(c, "sl", [P, 2, CAP])
        hid = sb(c, "hid", [P, 2, CAP])
        hs = sb(c, "hs", [P, HS, 2 * CAP], F32R)
        ye = sb(c, "ye", [P, D])
        yp = sb(c, "yp", [CAP_P, D])
        gate2 = sb(c, "gate2", [P, 2, D])
        vals = sb(c, "vals", [48, CAP_S])
        idxu = sb(c, "idxu", [48, CAP_S], U32)
        idxf = sb(c, "idxf", [48, CAP_S])
        gsel = sb(c, "gsel", [P, 48])
        isel = sb(c, "isel", [P, 48], U32)
        iall = sb(c, "iall", [P, EXPERTS], U32)
        gnow = sb(c, "gnow", [P, 2])
        inow = sb(c, "inow", [P, 2, 4], U32)
        psG = ps(c, "psG", [P, 2, 512])
        psX = ps(c, "psX", [P, 2, 512])
        psY = ps(c, "psY", [P, 4, 512])

        def e_at(ap, e):
            return ap[bass.ds(e, 1)]

        w_gu = A["w_gu"]
        w_dn = A["w_down"].rearrange("e (c t p) d -> e c p t d", c=CHUNKS, t=2)

        with nc.Block() as block:
            @block.sync
            def _(sp):
                for grp in range(2):
                    sp.dma_start(gate2[:, grp, :], ada_d[grp:grp + 1, 5 * D:6 * D].to_broadcast([P, D])).then_inc(gate_loaded, 16)

                def load_gu(e, ci, first):
                    back = last_user(ci, RING_GU, CHUNKS)
                    if not (first and back < 0):
                        sp.wait_ge(gu_lo, (e * CHUNKS + back + 1) * 4)
                    s = ci % RING_GU
                    sp.dma_start(raw_gu[:, s], e_at(w_gu, e)[0, ci]).then_inc(gu_loaded[s], 16)

                def load_dn(e, ci, first):
                    back = last_user(ci, RING_DN, CHUNKS)
                    if not (first and back < 0):
                        sp.wait_ge(dn_lo, (e * CHUNKS + back + 1) * 2)
                    s = ci % RING_DN
                    sp.dma_start(raw_dn[:, s], e_at(w_dn, e)[0, ci]).then_inc(dn_loaded[s], 16)

                def loads(e, first):
                    for ci in range(CHUNKS):
                        load_gu(e, ci, first)
                        if ci >= 1:
                            load_dn(e, ci - 1, first)
                    load_dn(e, CHUNKS - 1, first)
                loads(0, True)
                with sp.Fori(1, EXPERTS) as e:
                    loads(e, False)

            @block.tensor
            def _(pe):
                pe.wait_ge(top_v, ROUNDS)
                pe.transpose(psG[:, 0, 0:48], vals[:, :], ident[0:48, 0:48]).then_inc(tT_done, 1)
                pe.wait_ge(idx_f, 1)
                pe.transpose(psG[:, 1, 0:48], idxf[:, :], ident[0:48, 0:48]).then_inc(tT_done, 1)

                def turn(k):
                    pe.transpose(psX[:, k % 2, 0:P], xg_s[:, :].rearrange("p (d k) -> p k d", k=KD)[:, k, :], ident[:, :])
                    pe.transpose(psX[:, k % 2, P:CAP], xg_p[:, :].rearrange("p (d k) -> p k d", k=KD)[:, k, :],
                                 ident[0:CAP_P, 0:CAP_P]).then_inc(x_turned, 1)

                pe.wait_ge(sel_ready, 1)
                pe.wait_ge(g_loaded_s, 16)
                pe.wait_ge(g_loaded_p, 16)
                for k in range(KD):
                    if k >= 2:
                        pe.wait_ge(xs_ready, k - 1)
                    turn(k)

                def gate_up(e, i, first):
                    a = i % 2
                    n = e * FT + i
                    if i == 0:
                        pe.wait_ge(x_lo, e + 1)
                    if not (first and i < 2):
                        pe.wait_ge(hid_done, n - 1)
                    for m in range(2):
                        pe.wait_ge(gu_lo, 2 * n + m + 1)
                        bank = psG[:, a, m * CAP:(m + 1) * CAP]
                        for k in range(KD):
                            wh, wl = (w[:, a, m, k * P:(k + 1) * P] for w in (w_hi, w_lo))
                            pe.matmul(bank, wh, xhi[:, k, :], start=(k == 0), stop=False)
                            pe.matmul(bank, wh, xlo[:, k, :], start=False, stop=False)
                            mm = pe.matmul(bank, wl, xhi[:, k, :], start=False, stop=(k == KD - 1))
                    mm.then_inc(gu_done, 1)
                    if i % 2 == 0 and 4 <= i < 4 + 2 * KD:
                        k = i // 2 - 2
                        if k == 0:
                            pe.wait_ge(g_loaded_s, 16 * (e + 2))
                            pe.wait_ge(g_loaded_p, 16 * (e + 2))
                        pe.wait_ge(xs_ready, KD * (e + 1) + k - 1)
                        turn(k)

                def down(e, i, first):
                    a = i % 2
                    n = e * FT + i
                    pe.wait_ge(dn_lo, n + 1)
                    pe.wait_ge(hid_lo, n + 1)
                    if i == 0 and not first:
                        pe.wait_ge(y_scaled, 3 * e)
                    st, en = i == 0, i == FT - 1
                    s_hi, pp, s_lo = (hs[:, i % HS, at * P:(at + 1) * P] for at in range(3))
                    for h in range(2):
                        wh, wl = (w[:, a, h * 512:(h + 1) * 512] for w in (d_hi, d_lo))
                        pe.matmul(psY[:, h, :], s_hi, wh, start=st, stop=False)
                        pe.matmul(psY[:, h, :], s_hi, wl, start=False, stop=False)
                        pe.matmul(psY[:, h, :], s_lo, wh, start=False, stop=en)
                        pe.matmul(psY[:, 2 + h, :], pp, wh, start=st, stop=False)
                        mm = pe.matmul(psY[:, 2 + h, :], pp, wl, start=False, stop=en)
                    mm.then_inc(dn_done, 1)

                def expert(e, first):
                    for i in range(FT + BEHIND):
                        if i < FT:
                            gate_up(e, i, first)
                        if i >= BEHIND:
                            down(e, i - BEHIND, first)
                expert(0, True)
                with pe.Fori(1, EXPERTS) as e:
                    expert(e, False)

            @block.gpsimd
            def _(pool):
                def gather(e_next):
                    pool.indirect_dma_start(out=xg_p[:, :], out_offset=None, in_=xhat_d,
                                            in_offset=bass.IndirectOffsetOnAxis(ap=inow[0:CAP_P, 1, 0:1], axis=0)).then_inc(g_loaded_p, 16)
                    pool.indirect_dma_start(out=xg_s[:, :], out_offset=None, in_=xhat_d,
                                            in_offset=bass.IndirectOffsetOnAxis(ap=inow[:, 1, 1:2], axis=0)).then_inc(g_loaded_s, 16)

                def lists(e, slot):
                    pool.tensor_copy(inow[:, slot, 0:1], isel[:, bass.ds(e, 1)])
                    pool.tensor_copy(inow[:, slot, 2:3], isel[:, bass.ds(e, 1)])
                    pool.tensor_copy(inow[:, slot, 3:4], isel[:, bass.ds(e + 32, 1)])
                    pool.tensor_copy(inow[:, slot, 1:2], iall[:, bass.ds(e, 1)]).then_inc(idx_now, 1)

                def scatter(e):
                    pool.wait_ge(y_scaled, 3 * e + 3)
                    pool.sem_inc(pool_steps)
                    pool.indirect_dma_start(out=y_d[1], out_offset=bass.IndirectOffsetOnAxis(ap=inow[:, 0, 3:4], axis=0),
                                            in_=ye[:, :], in_offset=None, compute_op=ALU.add).then_inc(y_sent_s, 16)
                    pool.indirect_dma_start(out=y_d[0], out_offset=bass.IndirectOffsetOnAxis(ap=inow[0:CAP_P, 0, 2:3], axis=0),
                                            in_=yp[:, :], in_offset=None, compute_op=ALU.add).then_inc(y_sent_p, 16)
                    pool.wait_ge(y_sent_s, 16 * (e + 1))
                    pool.wait_ge(y_sent_p, 16 * (e + 1))

                pool.wait_ge(sel_ready, 1)
                lists(0, 1)
                pool.wait_ge(idx_now, 1)
                gather(0)

                def expert(e, nxt):
                    pool.wait_ge(g_loaded_s, 16 * (e + 1))
                    pool.wait_ge(g_loaded_p, 16 * (e + 1))
                    pool.wait_ge(x_turned, KD * (e + 1))
                    lists(e, 0)
                    lists(nxt, 1)
                    pool.wait_ge(idx_now, 2 * e + 3)
                    pool.sem_inc(pool_steps)
                    gather(e + 1)
                    scatter(e)
                with pool.Fori(0, EXPERTS - 1) as e:
                    expert(e, e + 1)
                expert(EXPERTS - 1, 0)
                pool.wait_ge(g_loaded_s, 16 * (EXPERTS + 1))
                pool.wait_ge(g_loaded_p, 16 * (EXPERTS + 1))

            def splits(e, i, last):
                if i + AHEAD < FT:
                    return e, i + AHEAD
                return None if last else (e + 1, i + AHEAD - FT)

            @block.scalar
            def _(act):
                def stage(k):
                    for grp, cols in ((1, slice(0, P)), (0, slice(P, CAP))):
                        m = act.activation(xst[:, k, cols], psX[:, k % 2, cols], ACT.Identity,
                                           bias=modv[:, grp, 2, k:k + 1], scale=a2[:, grp, k:k + 1])
                    m.then_inc(xs_ready, 1)

                def hi(e, i, m):
                    ci = i // 2
                    s = ci % RING_GU
                    per = len(range(s, CHUNKS, RING_GU))
                    if m == 0 and i % 2 == 0:
                        act.wait_ge(gu_loaded[s], (e * per + ci // RING_GU + 1) * 16)
                    act.activation(w_hi[:, i % 2, m], raw_gu[:, s, m, i % 2], ACT.Copy).then_inc(gu_hi, 1)

                def hi_down(e, i, first):
                    ci = i // 2
                    s = ci % RING_DN
                    per = len(range(s, CHUNKS, RING_DN))
                    if i % 2 == 0:
                        act.wait_ge(dn_loaded[s], (e * per + ci // RING_DN + 1) * 16)
                    if not (first and i < 2):
                        act.wait_ge(dn_done, e * FT + i - 1)
                    act.activation(d_hi[:, i % 2], raw_dn[:, s, i % 2], ACT.Copy).then_inc(dn_hi, 1)

                def xsplit(e):
                    act.wait_ge(xs_ready, KD * (e + 1))
                    act.activation(xhi[:, :, :], xst[:, :, :], ACT.Copy).then_inc(x_hi, 1)

                def yhalf(e):
                    act.wait_ge(pool_steps, 2 * e + 1)
                    act.wait_ge(dn_done, (e + 1) * FT)
                    act.activation(yp[:, :], psY[CAP_P:P, 2:4, :].rearrange("p a b -> p (a b)"), ACT.Copy).then_inc(y_half, 1)

                def step(e, i, first, last):
                    a = i % 2
                    n = e * FT + i
                    nxt = splits(e, i, last)
                    act.wait_ge(gu_done, n + 1)
                    if not (first and i < 2):
                        act.wait_ge(hid_done, n - 1)
                    act.activation(sl[:, a, :], psG[:, a, 0:CAP], ACT.Silu).then_inc(silu_done, 1)
                    if nxt and i < FT - 1:
                        hi(*nxt, 0)
                    back = last_user(i, HS, FT)
                    if not (first and back < 0):
                        act.wait_ge(dn_done, e * FT + back + 1)
                    act.wait_ge(hid_done, n + 1)
                    act.activation(hs[:, i % HS, 0:CAP], hid[:, a, :], ACT.Copy).then_inc(hid_hi, 1)
                    if nxt and i == FT - 1:
                        xsplit(e + 1)
                        hi(*nxt, 0)
                    if nxt:
                        hi(*nxt, 1)
                    if i % 2 == 0 and 4 <= i < 4 + 2 * KD:
                        k = i // 2 - 2
                        act.wait_ge(x_turned, KD * (e + 1) + k + 1)
                        stage(k)
                    hi_down(e, i, first)

                def expert(e, first, last):
                    for i in range(FT):
                        if i == 0 and not first:
                            yhalf(e - 1)
                        step(e, i, first, last)

                for i in range(AHEAD):
                    for m in range(2):
                        hi(0, i, m)
                for k in range(KD):
                    act.wait_ge(x_turned, k + 1)
                    stage(k)
                xsplit(0)
                expert(0, True, False)
                with act.Fori(1, EXPERTS - 1) as e:
                    expert(e, False, False)
                expert(EXPERTS - 1, False, True)
                yhalf(EXPERTS - 1)

            @block.vector
            def _(dve):
                for r in range(ROUNDS):
                    sl8 = slice(8 * r, 8 * r + 8)
                    if r:
                        dve.wait_ge(top_d, r)
                    dve.max(vals[:, sl8], affT[:, :]).then_inc(top_v, 1)
                    dve.wait_ge(top_v, r + 1)
                    dve.max_index(idxu[:, sl8], vals[:, sl8], affT[:, :]).then_inc(top_i, 1)
                    dve.wait_ge(top_i, r + 1)
                    dve.match_replace(affT[:, :], vals[:, sl8], affT[:, :], -2.0).then_inc(top_d, 1)
                dve.tensor_copy(idxf[:, :], idxu[:, :]).then_inc(idx_f, 1)
                dve.wait_ge(tT_done, 2)
                dve.tensor_copy(gsel[:, :], psG[:, 0, 0:48])
                dve.tensor_scalar(iall[:, :], psG[:, 1, 32:48], float(PROMPT), None, ALU.add)
                dve.tensor_copy(isel[:, :], psG[:, 1, 0:48]).then_inc(sel_ready, 1)

                def lo(e, i, m):
                    dve.wait_ge(gu_hi, 2 * (e * FT + i) + m + 1)
                    dve.tensor_tensor(w_lo[:, i % 2, m], raw_gu[:, (i // 2) % RING_GU, m, i % 2],
                                      w_hi[:, i % 2, m].bitcast(F32), ALU.subtract).then_inc(gu_lo, 1)

                def lo_down(e, i):
                    dve.wait_ge(dn_hi, e * FT + i + 1)
                    dve.tensor_tensor(d_lo[:, i % 2], raw_dn[:, (i // 2) % RING_DN, i % 2],
                                      d_hi[:, i % 2].bitcast(F32), ALU.subtract).then_inc(dn_lo, 1)

                def xsplit(e):
                    dve.wait_ge(x_hi, e + 1)
                    dve.tensor_tensor(xlo[:, :, :], xst[:, :, :], xhi[:, :, :].bitcast(F32), ALU.subtract).then_inc(x_lo, 1)

                def y_out(e):
                    dve.wait_ge(pool_steps, 2 * e + 1)
                    dve.tensor_copy(gnow[:, 0:1], gsel[:, bass.ds(e, 1)])
                    dve.tensor_copy(gnow[:, 1:2], gsel[:, bass.ds(e + 32, 1)]).then_inc(y_scaled, 1)
                    dve.wait_ge(y_scaled, 3 * e + 1)
                    dve.wait_ge(dn_done, (e + 1) * FT)
                    dve.scalar_tensor_tensor(out=ye[:, :], in0=psY[:, 0:2, :].rearrange("p a b -> p (a b)"), scalar=gnow[:, 1:2],
                                             in1=gate2[:, 1, :], op0=ALU.mult, op1=ALU.mult)
                    dve.wait_ge(y_half, e + 1)
                    dve.tensor_tensor(yp[:, :], psY[0:CAP_P, 2:4, :].rearrange("p a b -> p (a b)"), yp[:, :], ALU.add).then_inc(y_scaled, 1)
                    dve.wait_ge(y_scaled, 3 * e + 2)
                    dve.scalar_tensor_tensor(out=yp[:, :], in0=yp[:, :], scalar=gnow[0:CAP_P, 0:1],
                                             in1=gate2[0:CAP_P, 0, :], op0=ALU.mult, op1=ALU.mult).then_inc(y_scaled, 1)

                def step(e, i, first, last):
                    a = i % 2
                    n = e * FT + i
                    nxt = splits(e, i, last)
                    dve.wait_ge(silu_done, n + 1)
                    if not (first and i < 2):
                        dve.wait_ge(hid_lo, n - 1)
                    dve.tensor_tensor(hid[:, a, :], sl[:, a, :], psG[:, a, CAP:2 * CAP], ALU.mult).then_inc(hid_done, 1)
                    if nxt and i < FT - 1:
                        lo(*nxt, 0)
                    dve.wait_ge(hid_hi, n + 1)
                    part = hs[:, i % HS]
                    dve.tensor_tensor(part[:, CAP:CAP + CAP_P], hid[:, a, P:CAP], part[:, P:CAP].bitcast(F32), ALU.subtract)
                    dve.tensor_tensor(part[:, CAP + CAP_P:2 * CAP], hid[:, a, 0:P], part[:, 0:P].bitcast(F32),
                                      ALU.subtract).then_inc(hid_lo, 1)
                    if nxt and i == FT - 1:
                        xsplit(e + 1)
                        lo(*nxt, 0)
                    if nxt:
                        lo(*nxt, 1)
                    lo_down(e, i)

                def expert(e, first, last):
                    for i in range(FT):
                        if i == 0 and not first:
                            y_out(e - 1)
                        step(e, i, first, last)

                dve.wait_ge(sel_ready, 1)
                dve.wait_ge(gate_loaded, 32)
                for i in range(AHEAD):
                    for m in range(2):
                        lo(0, i, m)
                xsplit(0)
                expert(0, True, False)
                with dve.Fori(1, EXPERTS - 1) as e:
                    expert(e, False, False)
                expert(EXPERTS - 1, False, True)
                y_out(EXPERTS - 1)


_OUTS = [((1, PROMPT, D), "float32"), ((1, SAMPLE, D), "float32")]


def bias_layout(rpb):
    padded = np.concatenate([rpb.reshape(HEADS, -1), np.full((HEADS, 1), NEG, rpb.dtype)], axis=1)
    off = rpb.shape[1] * rpb.shape[2]
    where = np.full((P, 3, BIAS_COLS), off, np.int64)
    for t0, qr0, kr0, rows, grid_rows, at in ROW_SETS:
        for j in (0, 1, 3):
            for q in range(P):
                r, cq = qr0 + q // Q_COLS, j * Q_COLS + q % Q_COLS
                rs = min(max(r - WIN_ROWS // 2, 0), grid_rows - WIN_ROWS)
                cs = min(max(cq - WIN_COLS // 2, 0), GRID_W - WIN_COLS)
                for kr in range(rs, rs + WIN_ROWS):
                    a = (kr - r + WIN_ROWS - 1) * (2 * WIN_COLS - 1) + (cs - cq + WIN_COLS - 1)
                    b = at + (kr - kr0) * K_COLS + cs - KEY_COL0[j]
                    where[q, PATTERN[j], b:b + WIN_COLS] = np.arange(a, a + WIN_COLS)
    return np.ascontiguousarray(padded[:, where])


def lay_out(inputs):
    a = {n: np.ascontiguousarray(inputs[n]) for n in (
        "x_prompt", "x_sample", "c_prompt", "c_sample", "ada_w", "ada_b", "norm1_g", "w_in", "w_out", "norm2_g",
        "w_router", "w_down")}
    a["ident"] = np.eye(P, dtype=np.float32)
    a["ones64"] = np.kron(np.eye(P // DH), np.full((DH, DH), 1.0 / DH)).astype(np.float32)
    a["qk_gain"] = np.stack([np.tile(np.asarray(inputs[n]), P // DH) for n in ("q_norm_g", "k_norm_g")], axis=1)
    per = np.concatenate([np.asarray(inputs["conv_w"])] + [np.asarray(inputs[n])[None] for n in
                         ("conv_b", "conv_ln_g", "conv_ln_b")], axis=0)
    a["conv_pack"] = np.ascontiguousarray(per.reshape(CONV_K + 3, 4, P).transpose(2, 1, 0))
    a["bias"] = bias_layout(np.asarray(inputs["rpb"]))
    gu = np.empty((EXPERTS, CHUNKS, P, 2, 2, KD, P), np.float32)
    for m, n in enumerate(("w_gate", "w_up")):
        w = np.asarray(inputs[n]).reshape(EXPERTS, P, KD, CHUNKS, 2, P)
        gu[:, :, :, m] = w.transpose(0, 3, 1, 4, 2, 5)
    a["w_gu"] = gu.reshape(EXPERTS, CHUNKS, P, 2, 2, KD * P)
    return a


def kernel(**inputs):
    import concourse.bacc as _bacc
    from concourse.bass_utils import run_bass_kernel_spmd as _run

    nc = _bacc.Bacc("TRN2", target_bir_lowering=False, num_devices=1)
    arrays, aps = {}, {}
    for name, a in lay_out(inputs).items():
        arrays[f"in_{name}"] = a
        aps[name] = nc.dram_tensor(f"in_{name}", a.shape, mybir.dt.from_np(a.dtype), kind="ExternalInput").ap()
    outs = [nc.dram_tensor(f"out_{i}", s, mybir.dt.from_np(np.dtype(d)), kind="ExternalOutput").ap()
            for i, (s, d) in enumerate(_OUTS)]
    program(nc, aps, outs)
    r = _run(nc, [arrays], core_ids=[0])
    return tuple(r.results[0][f"out_{i}"] for i in range(len(_OUTS)))
```

```python
from contextlib import ExitStack

import numpy as np

import concourse.bass as bass
from concourse import mybir

F32 = mybir.dt.float32
F32R = mybir.dt.float32r
U32 = mybir.dt.uint32
ALU = mybir.AluOpType
ACT = mybir.ActivationFunctionType
AX = mybir.AxisListType

P = 128
D = 1024
KD = D // P
PROMPT, SAMPLE = 512, 1024
TOKENS = PROMPT + SAMPLE
TILES = TOKENS // P
NCH = TOKENS // 512
MODS = 6
HEADS, DH = 8, 64
WA = HEADS * DH
WC = D - WA
IN_COLS = 3 * WA + 2 * WC
GRID_W, WIN_ROWS, WIN_COLS = 64, 8, 16
CONV_K = 31
PAD = CONV_K // 2
EXPERTS, FACTOR, FF = 16, 2, 2816
EPS = 1e-6
CAP_P = FACTOR * PROMPT // EXPERTS
CAP_S = FACTOR * SAMPLE // EXPERTS
CAP = CAP_P + CAP_S
FT = FF // P
CHUNKS = FT // 2
NEG = -1e30

Q_COLS, K_COLS = 16, 32
COL_BLOCKS = GRID_W // Q_COLS
KEY_COL0 = [min(max(Q_COLS * j - WIN_COLS // 2, 0), GRID_W - K_COLS) for j in range(COL_BLOCKS)]
ROW_SETS = [(0, 0, 0, 8, 8, 0), (PROMPT, 0, 0, 12, 16, 256), (PROMPT, 8, 4, 12, 16, 640)]
PATTERN = [0, 1, 1, 2]
BIAS_COLS = 1024
BLOCKS = [(s, j) for s in range(3) for j in range(COL_BLOCKS)]
V_ROWS = [(0, 0), (0, 4), (PROMPT, 0), (PROMPT, 4), (PROMPT, 8), (PROMPT, 12)]


def group(tile):
    return 0 if tile * P < PROMPT else 1


def program(nc, A, outs):
    g = ExitStack()
    sems = {}

    def sem(name):
        if name not in sems:
            sems[name] = g.enter_context(nc.semaphore(name))
        return sems[name]

    def dram(name, shape):
        return nc.dram_tensor(name, shape, F32, kind="Internal").ap()

    ada_d = dram("ada_d", [2, MODS * D])
    qk_d = dram("qk_d", [8, P, TOKENS])
    conv_d = dram("conv_d", [4, P, TOKENS])
    v_d = dram("v_d", [TOKENS, WA])
    xhat_d = dram("xhat_d", [TOKENS, D])
    y_d = [outs[0].rearrange("b l d -> (b l) d"), outs[1].rearrange("b l d -> (b l) d")]
    x_d = [A["x_prompt"].rearrange("b l d -> (b l) d"), A["x_sample"].rearrange("b l d -> (b l) d")]

    def rows_of(pair, t):
        r = t * P if group(t) == 0 else t * P - PROMPT
        return pair[group(t)][r:r + P, :]

    def sb(ctx, name, shape, dt=F32):
        return ctx.enter_context(nc.sbuf_tensor(name, shape, dt))

    def ps(ctx, name, shape):
        return ctx.enter_context(nc.psum_tensor(name, shape, F32))

    with g:
        ident = sb(g, "ident", [P, P])
        ones64 = sb(g, "ones64", [P, P])
        eps_col = sb(g, "eps_col", [P, 1])
        vecs = sb(g, "vecs", [P, 32])
        convp = sb(g, "convp", [P, 4, CONV_K + 3])
        qkg = sb(g, "qkg", [P, 2])
        modv = sb(g, "modv", [P, 2, 4, KD])
        a1 = sb(g, "a1", [P, 2, KD])
        a2 = sb(g, "a2", [P, 2, KD])
        rstd1 = sb(g, "rstd1", [P, TILES])

        condition(nc, A, g, sem, sb, ps, ada_d, rows_of, x_d,
                  ident, ones64, eps_col, vecs, convp, qkg, modv, a1, a2, rstd1)
        project(nc, A, sem, sb, ps, rows_of, x_d, qk_d, conv_d, v_d,
                ident, ones64, eps_col, convp, qkg, modv, a1, rstd1)
        affT = sb(g, "affT", [48, SAMPLE])
        o_ctx = ExitStack()
        with o_ctx:
            attn = sb(o_ctx, "attn", [P, 4, TOKENS])
            attend(nc, A, sem, sb, ps, qk_d, v_d, ident, attn)
            mix(nc, A, sem, sb, ps, rows_of, x_d, y_d, ada_d, conv_d, xhat_d, ident, eps_col, modv, a2, affT, attn)
        experts(nc, A, sem, sb, ps, y_d, ada_d, xhat_d, ident, modv, a2, affT)


def condition(nc, A, g, sem, sb, ps, ada_d, rows_of, x_d,
              ident, ones64, eps_col, vecs, convp, qkg, modv, a1, a2, rstd1):
    NJ = MODS * D // 512
    RING, XR = 3, 3
    consts = sem("consts_loaded")
    c_loaded, cs_ready = sem("c_loaded"), sem("cs_ready")
    w_loaded = [sem(f"ada_w_loaded{i}") for i in range(RING)]
    x_loaded = [sem(f"x_loaded{i}") for i in range(XR)]
    mm_done, ada_row, ada_stored, mod_loaded = sem("ada_mm"), sem("ada_row"), sem("ada_stored"), sem("mod_loaded")
    sq_done, ms_done, rt_done, rstd_done, a_ready = (
        sem("x_sq"), sem("x_ms"), sem("x_rt"), sem("rstd1_done"), sem("a_ready"))
    eps_set = sem("eps_set")
    with ExitStack() as c:
        cT = sb(c, "cT", [P, 2, KD])
        cs = sb(c, "cs", [P, 2, KD])
        aw = sb(c, "aw", [P, RING, KD, 512])
        ada_b2 = sb(c, "ada_b2", [2, MODS * D])
        ada_sb = sb(c, "ada_sb", [2, MODS * D])
        xt = sb(c, "xt0", [P, XR, D])
        junk = sb(c, "junk0", [P, 2, D])
        ss = sb(c, "ss", [P, TILES])
        psA = ps(c, "psA", [P, 2, 512])
        w_v = A["ada_w"].rearrange("(p k) n -> p k n", k=KD)
        CONSTS = 16 * 8

        with nc.Block() as block:
            @block.sync
            def _(sp):
                for i, name in enumerate(("c_prompt", "c_sample")):
                    sp.dma_start(cT[:, i, :], A[name].rearrange("b (p k) -> (b p) k", k=KD)).then_inc(c_loaded, 16)
                for j in range(NJ):
                    if j >= RING:
                        sp.wait_ge(mm_done, j - RING + 1)
                    sp.dma_start(aw[:, j % RING], w_v[:, :, j * 512:(j + 1) * 512]).then_inc(w_loaded[j % RING], 16)
                sp.wait_ge(ada_row, NJ)
                sp.dma_start(ada_d, ada_sb[:, :]).then_inc(ada_stored, 16)
                sp.wait_ge(ada_stored, 16)
                for grp in range(2):
                    for v, m in enumerate((0, 1, 3, 4)):
                        sp.dma_start(modv[:, grp, v, :],
                                     ada_d[grp, m * D:(m + 1) * D].rearrange("(p k) -> p k", k=KD)).then_inc(mod_loaded, 16)
                sp.wait_ge(mod_loaded, 16 * 8)

            @block.gpsimd
            def _(pool):
                pool.memset(eps_col[:, :], EPS).then_inc(eps_set, 1)

            def square(act, t):
                act.wait_ge(x_loaded[t % XR], 16 * (t // XR + 1))
                if t >= 2:
                    act.wait_ge(sq_done, t - 1)
                act.activation(junk[:, t % 2, :], xt[:, t % XR, :], ACT.Square,
                               accum_out=ss[:, t:t + 1]).then_inc(sq_done, 1)

            @block.scalar
            def _(act):
                act.dma_start(ident[:, :], A["ident"]).then_inc(consts, 16)
                act.dma_start(ones64[:, :], A["ones64"]).then_inc(consts, 16)
                act.dma_start(vecs[:, 0:KD], A["norm1_g"].rearrange("(p k) -> p k", k=KD)).then_inc(consts, 16)
                act.dma_start(vecs[:, KD:2 * KD], A["norm2_g"].rearrange("(p k) -> p k", k=KD)).then_inc(consts, 16)
                act.dma_start(convp[:, :, :], A["conv_pack"]).then_inc(consts, 16)
                act.dma_start(qkg[:, :], A["qk_gain"]).then_inc(consts, 16)
                act.dma_start(ada_b2[0:1, :], A["ada_b"].rearrange("(a n) -> a n", a=1)).then_inc(consts, 16)
                act.dma_start(ada_b2[1:2, :], A["ada_b"].rearrange("(a n) -> a n", a=1)).then_inc(consts, 16)
                act.wait_ge(c_loaded, 32)
                act.activation(cs[:, :, :], cT[:, :, :], ACT.Silu).then_inc(cs_ready, 1)
                act.wait_ge(mm_done, NJ - RING - 1)
                for t in range(TILES):
                    if t >= XR:
                        act.wait_ge(sq_done, t - XR + 1)
                    act.dma_start(xt[:, t % XR, :], rows_of(x_d, t)).then_inc(x_loaded[t % XR], 16)
                    if t >= 1:
                        square(act, t - 1)
                square(act, TILES - 1)
                act.wait_ge(ms_done, 1)
                act.activation(ss[:, :], ss[:, :], ACT.Sqrt).then_inc(rt_done, 1)

            @block.tensor
            def _(pe):
                pe.wait_ge(cs_ready, 1)
                for j in range(NJ):
                    pe.wait_ge(w_loaded[j % RING], 16 * (j // RING + 1))
                    if j >= 2:
                        pe.wait_ge(ada_row, j - 1)
                    for k in range(KD):
                        mm = pe.matmul(psA[0:2, j % 2, :], cs[:, :, k], aw[:, j % RING, k, :],
                                       start=(k == 0), stop=(k == KD - 1))
                    mm.then_inc(mm_done, 1)

            @block.vector
            def _(dve):
                dve.wait_ge(consts, CONSTS)
                for j in range(NJ):
                    dve.wait_ge(mm_done, j + 1)
                    dve.tensor_tensor(ada_sb[:, j * 512:(j + 1) * 512], psA[0:2, j % 2, :],
                                      ada_b2[:, j * 512:(j + 1) * 512], ALU.add).then_inc(ada_row, 1)
                dve.wait_ge(sq_done, TILES)
                dve.tensor_scalar(ss[:, :], ss[:, :], 1.0 / D, EPS, ALU.mult, ALU.add).then_inc(ms_done, 1)
                dve.wait_ge(rt_done, 1)
                dve.reciprocal(rstd1[:, :], ss[:, :]).then_inc(rstd_done, 1)
                dve.wait_ge(mod_loaded, 16 * 8)
                for grp in range(2):
                    dve.scalar_tensor_tensor(out=a1[:, grp, :], in0=modv[:, grp, 1, :], scalar=1.0,
                                             in1=vecs[:, 0:KD], op0=ALU.add, op1=ALU.mult).then_inc(a_ready, 1)
                    dve.scalar_tensor_tensor(out=a2[:, grp, :], in0=modv[:, grp, 3, :], scalar=1.0,
                                             in1=vecs[:, KD:2 * KD], op0=ALU.add, op1=ALU.mult).then_inc(a_ready, 1)


Z_TILES = [("gate", 0), ("value", 0), ("q", 0), ("gate", 1), ("value", 1), ("q", 1), ("q", 2),
           ("gate", 2), ("value", 2), ("q", 3), ("k", 0), ("gate", 3), ("value", 3), ("k", 1), ("k", 2), ("k", 3),
           ("v", 0), ("v", 1), ("v", 2), ("v", 3)]
Z_COL0 = {"q": 0, "k": WA, "v": 2 * WA, "value": 3 * WA, "gate": 3 * WA + WC}
NZ = len(Z_TILES)
TAPS_STEP = 8
CONV_DONE = [2 + (CONV_K * (j + 1) - 1) // TAPS_STEP for j in range(4)]


def side_jobs():
    jobs = {s: [] for s in range(NZ + 3)}
    for i, (kind, j) in enumerate(Z_TILES):
        if kind in "qkv":
            jobs[i + 1] += [("turn" if kind == "v" else "ss", i, n) for n in range(NCH)]
    for j in range(4):
        m = CONV_DONE[j] + 1
        jobs[m] += [("mean", j, n) for n in range(NCH)]
        jobs[m + 1] += [("var", j, n) for n in range(NCH)]
    return jobs


def project(nc, A, sem, sb, ps, rows_of, x_d, qk_d, conv_d, v_d,
            ident, ones64, eps_col, convp, qkg, modv, a1, rstd1):
    XR, WR = 2, 3
    jobs = side_jobs()
    flat = [(s, job) for s in sorted(jobs) for job in jobs[s]]
    index = {job: i for i, (s, job) in enumerate(flat)}
    x_loaded = [sem(f"x1_loaded{i}") for i in range(XR)]
    xn_ready, xT_done, h_hi_ready, h_lo_ready = sem("xn_ready"), sem("xT_done"), sem("h_hi_ready"), sem("h_lo_ready")
    h_mod = sem("h_mod")
    w_loaded = [sem(f"w_in_loaded{i}") for i in range(WR)]
    w_hi_ready, w_lo_ready, z_done = sem("w_in_hi"), sem("w_in_lo"), sem("z_done")
    z_act, z_dve = sem("z_out_act"), sem("z_out_dve")
    side_done = sem("side_done")
    side_act = sem("side_out_act")
    pads_set, conv_s, conv_p = sem("pads_set"), sem("conv_sample_taps"), sem("conv_prompt_taps")
    ln_cent, ln_sq, ln_r, ln_norm, ln_out = sem("ln_centred"), sem("ln_square"), sem("ln_rstd"), sem("ln_normed"), sem("ln_out")
    qk_r, qk_out, v_out = sem("qk_rstd"), sem("qk_out"), sem("v_out")
    stored = [sem(f"z_stored{i}") for i in range(3)]
    conv_mul = sem("conv_prompt_products")

    acts = [1 if kind in ("gate", "q", "k", "v") else 0 for kind, _ in Z_TILES]
    dves = [1 if kind in ("value", "q", "k") else 0 for kind, _ in Z_TILES]

    def gated_by(j):
        return sum(dves[:Z_TILES.index(("value", j)) + 1])

    s_act = [1 if job[0] in ("var", "ss") else 0 for _, job in flat]
    stores = []
    for s in range(NZ + 3):
        if s - 1 < NZ and s >= 1 and Z_TILES[s - 1][0] in "qk":
            stores.append((s, "qk", s - 1))
        if s - 1 < NZ and s >= 1 and Z_TILES[s - 1][0] == "v":
            stores.append((s, "v", s - 1))
        for j in range(4):
            if s == CONV_DONE[j] + 2:
                stores.append((s, "conv", j))
    store_no = {(what, i): n for n, (_, what, i) in enumerate(stores)}

    with ExitStack() as c:
        h_hi = sb(c, "h_hi", [P, KD, TOKENS], F32R)
        h_lo = sb(c, "h_lo", [P, KD, TOKENS], F32R)
        psZ = ps(c, "psZ", [P, 6, 512])
        psS = ps(c, "psS", [P, 2, 512])
        w_raw = sb(c, "w_raw", [P, WR, KD, P])
        w_hi = sb(c, "w_hi", [P, 2, KD, P], F32R)
        w_lo = sb(c, "w_lo", [P, 2, KD, P], F32R)
        w_v = A["w_in"].rearrange("(p k) n -> p k n", k=KD)

        def load_w(sp, ct):
            if ct >= WR:
                sp.wait_ge(w_lo_ready, ct - WR + 1)
            kind, j = Z_TILES[ct]
            col = Z_COL0[kind] + j * P
            sp.dma_start(w_raw[:, ct % WR], w_v[:, :, col:col + P]).then_inc(w_loaded[ct % WR], 16)

        def split_hi(act, ct):
            act.wait_ge(w_loaded[ct % WR], 16 * (ct // WR + 1))
            if ct >= 2:
                act.wait_ge(z_done, ct - 1)
            act.activation(w_hi[:, ct % 2], w_raw[:, ct % WR], ACT.Copy).then_inc(w_hi_ready, 1)

        def split_lo(dve, ct):
            dve.wait_ge(w_hi_ready, ct + 1)
            dve.tensor_tensor(w_lo[:, ct % 2], w_raw[:, ct % WR], w_hi[:, ct % 2].bitcast(F32),
                              ALU.subtract).then_inc(w_lo_ready, 1)

        with ExitStack() as c2:
            xt = sb(c2, "xt1", [P, XR, D])
            xn = sb(c2, "xn", [P, 2, D])
            hm = sb(c2, "hm", [P, 2, KD, P])
            with nc.Block() as block:
                @block.sync
                def _(sp):
                    for t in range(TILES):
                        if t >= XR:
                            sp.wait_ge(xn_ready, t - XR + 1)
                        sp.dma_start(xt[:, t % XR, :], rows_of(x_d, t)).then_inc(x_loaded[t % XR], 16)
                        if t in (2, 4, 6):
                            load_w(sp, t // 2 - 1)

                @block.vector
                def _(dve):
                    for t in range(TILES + 1):
                        if t < TILES:
                            dve.wait_ge(x_loaded[t % XR], 16 * (t // XR + 1))
                            if t >= 2:
                                dve.wait_ge(xT_done, t - 1)
                            dve.tensor_scalar(xn[:, t % 2, :], xt[:, t % XR, :], rstd1[:, t:t + 1], None,
                                              ALU.mult).then_inc(xn_ready, 1)
                        if t >= 1:
                            u = t - 1
                            dve.wait_ge(h_hi_ready, u + 1)
                            dve.tensor_tensor(h_lo[:, :, u * P:(u + 1) * P], hm[:, u % 2],
                                              h_hi[:, :, u * P:(u + 1) * P].bitcast(F32),
                                              ALU.subtract).then_inc(h_lo_ready, 1)
                        if t == 8:
                            split_lo(dve, 0)

                @block.tensor
                def _(pe):
                    for t in range(TILES):
                        pe.wait_ge(xn_ready, t + 1)
                        if t >= 2:
                            pe.wait_ge(h_mod, t - 1)
                        xk = xn[:, t % 2, :].rearrange("p (d k) -> p k d", k=KD)
                        for k in range(KD):
                            mm = pe.transpose(psZ[:, 2 * (t % 2) + k // 4, (k % 4) * P:(k % 4 + 1) * P],
                                              xk[:, k, :], ident[:, :])
                        mm.then_inc(xT_done, 1)

                @block.scalar
                def _(act):
                    for t in range(TILES):
                        act.wait_ge(xT_done, t + 1)
                        if t >= 2:
                            act.wait_ge(h_lo_ready, t - 1)
                        for k in range(KD):
                            m = act.activation(hm[:, t % 2, k, :],
                                               psZ[:, 2 * (t % 2) + k // 4, (k % 4) * P:(k % 4 + 1) * P], ACT.Identity,
                                               bias=modv[:, group(t), 0, k:k + 1], scale=a1[:, group(t), k:k + 1])
                        m.then_inc(h_mod, 1)
                        act.wait_ge(h_mod, t + 1)
                        act.activation(h_hi[:, :, t * P:(t + 1) * P], hm[:, t % 2], ACT.Copy).then_inc(h_hi_ready, 1)
                        if t == 6:
                            split_hi(act, 0)

        with ExitStack() as c2:
            sg = sb(c2, "sg", [P, TOKENS])
            UW = TOKENS + 4 * PAD
            u = sb(c2, "u", [P, 3, UW])
            acc = sb(c2, "acc", [P, 2, TOKENS])
            sqz = sb(c2, "sqz", [P, 2, TOKENS])
            zg = sb(c2, "zg", [P, 2, TOKENS])
            rr = sb(c2, "rr", [P, TOKENS])
            U_P, U_S = 0, PROMPT + 2 * PAD

            prod = sb(c2, "prod", [P, 2, PROMPT])
            lnr = sb(c2, "lnr", [P, TOKENS])

            def chunk(n):
                return slice(n * 512, (n + 1) * 512)

            def by_block(ap):
                return ap.rearrange("p (r j c) -> p j r c", j=COL_BLOCKS, c=Q_COLS)

            with nc.Block() as block:
                @block.sync
                def _(sp):
                    loads, n = WR, 0
                    for s in range(NZ + 3):
                        if 2 <= s and loads < NZ:
                            load_w(sp, loads)
                            loads += 1
                        while n < len(stores) and stores[n][0] == s:
                            _, what, i = stores[n]
                            if what == "qk":
                                sp.wait_ge(qk_out, NCH * (sum(1 for k, _ in Z_TILES[:i + 1] if k in "qk")))
                                sp.dma_start(qk_d[(0 if Z_TILES[i][0] == "q" else 4) + Z_TILES[i][1]],
                                             zg[:, i % 2, :]).then_inc(stored[n % 3], 16)
                            elif what == "v":
                                sp.wait_ge(v_out, NCH * (Z_TILES[i][1] + 1))
                                sp.dma_start(v_d.rearrange("(t p) c -> p t c", p=P)[:, :, Z_TILES[i][1] * P:(Z_TILES[i][1] + 1) * P],
                                             zg[:, i % 2, :].rearrange("p (t c) -> p t c", c=P)).then_inc(stored[n % 3], 16)
                            else:
                                sp.wait_ge(ln_out, i + 1)
                                sp.dma_start(conv_d[i], acc[:, i % 2, :]).then_inc(stored[n % 3], 16)
                            n += 1
                    while loads < NZ:
                        load_w(sp, loads)
                        loads += 1
                    for i in range(3):
                        sp.wait_ge(stored[i], 16 * len([1 for n in range(len(stores)) if n % 3 == i]))

                def wait_store(eng, what, i):
                    n = store_no[(what, i)]
                    eng.wait_ge(stored[n % 3], 16 * (n // 3 + 1))

                def wait_row(eng, s):
                    was = [i for i in range(s % 2, s, 2) if Z_TILES[i][0] in "qkv"]
                    if was:
                        wait_store(eng, "v" if Z_TILES[was[-1]][0] == "v" else "qk", was[-1])

                @block.tensor
                def _(pe):
                    done = [0]

                    def side(job):
                        i = index[job]
                        if i >= 2:
                            was, wj, wn = flat[i - 2][1]
                            if was in ("var", "ss"):
                                pe.wait_ge(side_act, sum(s_act[:i - 1]))
                            elif was == "mean":
                                pe.wait_ge(ln_cent, NCH * wj + wn + 1)
                            else:
                                pe.wait_ge(v_out, NCH * Z_TILES[wj][1] + wn + 1)
                        kind, j, n = job
                        bank = psS[:, i % 2, :]
                        if kind == "mean":
                            pe.wait_ge(conv_s, CONV_K * (j + 1))
                            pe.wait_ge(conv_p, CONV_K * (j + 1))
                            mm = pe.matmul(bank, ones64[:, :], acc[:, j % 2, chunk(n)], start=True, stop=True)
                        elif kind == "var":
                            pe.wait_ge(ln_sq, NCH * j + n + 1)
                            mm = pe.matmul(bank, ones64[:, :], lnr[:, chunk(n)], start=True, stop=True)
                        elif kind == "ss":
                            pe.wait_ge(z_act, sum(acts[:j + 1]))
                            mm = pe.matmul(bank, ones64[:, :], sqz[:, j % 2, chunk(n)], start=True, stop=True)
                        else:
                            pe.wait_ge(z_act, sum(acts[:j + 1]))
                            for b in range(4):
                                mm = pe.transpose(bank[:, b * P:(b + 1) * P],
                                                  sqz[:, j % 2, (4 * n + b) * P:(4 * n + b + 1) * P], ident[:, :])
                        mm.then_inc(side_done, 1)
                        assert i == done[0]
                        done[0] += 1

                    for s in range(NZ + 3):
                        todo = list(jobs[s])
                        per = -(-len(todo) // NCH)
                        for n in range(NCH):
                            if s < NZ:
                                if n == 0:
                                    pe.wait_ge(w_lo_ready, s + 1)
                                    if s >= 2:
                                        if acts[s - 2]:
                                            pe.wait_ge(z_act, sum(acts[:s - 1]))
                                        if dves[s - 2]:
                                            pe.wait_ge(z_dve, sum(dves[:s - 1]))
                                bank = psZ[:, 3 * (s % 2) + n, :]
                                for k in range(KD):
                                    pe.matmul(bank, w_hi[:, s % 2, k, :], h_hi[:, k, chunk(n)], start=(k == 0), stop=False)
                                    pe.matmul(bank, w_hi[:, s % 2, k, :], h_lo[:, k, chunk(n)], start=False, stop=False)
                                    mm = pe.matmul(bank, w_lo[:, s % 2, k, :], h_hi[:, k, chunk(n)], start=False,
                                                   stop=(k == KD - 1))
                                if n == NCH - 1:
                                    mm.then_inc(z_done, 1)
                            for job in todo[per * n:per * (n + 1)]:
                                side(job)

                @block.scalar
                def _(act):
                    for s in range(NZ + 3):
                        if s + 1 < NZ:
                            split_hi(act, s + 1)
                        for job in jobs[s]:
                            kind, j, n = job
                            i = index[job]
                            if kind == "ss":
                                before = sum(1 for k, _ in Z_TILES[:j] if k in "qk")
                                if before:
                                    act.wait_ge(qk_out, NCH * (before - 1) + n + 1)
                            if kind in ("var", "ss"):
                                act.wait_ge(side_done, i + 1)
                                row = lnr if kind == "var" else rr
                                act.activation(row[:, chunk(n)], psS[:, i % 2, :], ACT.Ln, bias=eps_col[:, :]).then_inc(side_act, 1)
                        for job in jobs[s]:
                            kind, j, n = job
                            if kind in ("var", "ss"):
                                act.wait_ge(side_act, sum(s_act[:index[job] + 1]))
                                row, counter = (lnr, ln_r) if kind == "var" else (rr, qk_r)
                                act.activation(row[:, chunk(n)], row[:, chunk(n)], ACT.Exp, scale=-0.5).then_inc(counter, 1)
                        for job in jobs[s]:
                            kind, j, n = job
                            if kind == "mean":
                                act.wait_ge(ln_cent, NCH * j + n + 1)
                                if j >= 1:
                                    act.wait_ge(ln_norm, NCH * j)
                                act.activation(lnr[:, chunk(n)], acc[:, j % 2, chunk(n)], ACT.Square).then_inc(ln_sq, 1)
                        for j in range(4):
                            if s == CONV_DONE[j] + 2:
                                act.wait_ge(ln_norm, NCH * (j + 1))
                                act.activation(acc[:, j % 2, :], acc[:, j % 2, :], ACT.Silu, bias=convp[:, j, CONV_K + 2:CONV_K + 3],
                                               scale=convp[:, j, CONV_K + 1:CONV_K + 2]).then_inc(ln_out, 1)
                        if s < NZ:
                            kind, j = Z_TILES[s]
                            prods = psZ[:, 3 * (s % 2):3 * (s % 2) + 3, :].rearrange("p a b -> p (a b)")
                            if kind != "value":
                                act.wait_ge(z_done, s + 1)
                            if kind == "gate":
                                if j >= 1:
                                    act.wait_ge(z_dve, gated_by(j - 1))
                                act.activation(sg[:, :], prods, ACT.Sigmoid).then_inc(z_act, 1)
                            elif kind in "qk":
                                act.activation(sqz[:, s % 2, :], prods, ACT.Square).then_inc(z_act, 1)
                            elif kind == "v":
                                act.activation(sqz[:, s % 2, :], prods, ACT.Copy).then_inc(z_act, 1)

                def tap(eng, lo, n, at, j, t, counter):
                    src = u[:, j % 3, at + t:at + t + n]
                    dst = acc[:, j % 2, lo:lo + n]
                    if t == 0:
                        eng.tensor_scalar(dst, src, convp[:, j, 0:1], convp[:, j, CONV_K:CONV_K + 1],
                                          ALU.mult, ALU.add).then_inc(counter, 1)
                    elif counter is conv_s:
                        eng.wait_ge(counter, CONV_K * j + t)
                        eng.scalar_tensor_tensor(out=dst, in0=src, scalar=convp[:, j, t:t + 1], in1=dst,
                                                 op0=ALU.mult, op1=ALU.add).then_inc(counter, 1)
                    else:
                        if t >= 3:
                            eng.wait_ge(counter, CONV_K * j + t - 1)
                        eng.tensor_scalar(prod[:, t % 2, :], src, convp[:, j, t:t + 1], 0.0, ALU.mult, ALU.add).then_inc(conv_mul, 1)
                        eng.wait_ge(conv_mul, (CONV_K - 1) * j + t)
                        eng.wait_ge(counter, CONV_K * j + t)
                        eng.tensor_tensor(dst, dst, prod[:, t % 2, :], ALU.add).then_inc(counter, 1)

                @block.gpsimd
                def _(pool):
                    for b in range(3):
                        for at in (U_P, U_P + PAD + PROMPT, U_S, U_S + PAD + SAMPLE):
                            m = pool.memset(u[:, b, at:at + PAD], 0.0)
                    m.then_inc(pads_set, 1)
                    pool.wait_ge(pads_set, 1)
                    for j in range(4):
                        pool.wait_ge(z_dve, gated_by(j))
                        if j >= 2:
                            wait_store(pool, "conv", j - 2)
                        for t in range(CONV_K):
                            tap(pool, 0, PROMPT, U_P, j, t, conv_p)

                @block.vector
                def _(dve):
                    taps = 0
                    dve.wait_ge(pads_set, 1)
                    for s in range(NZ + 3):
                        if s + 1 < NZ:
                            split_lo(dve, s + 1)
                        if s >= 2:
                            for _ in range(TAPS_STEP):
                                if taps < 4 * CONV_K:
                                    j, t = divmod(taps, CONV_K)
                                    if t == 0:
                                        dve.wait_ge(z_dve, gated_by(j))
                                        if j >= 2:
                                            wait_store(dve, "conv", j - 2)
                                    tap(dve, PROMPT, SAMPLE, U_S, j, t, conv_s)
                                    taps += 1
                        for job in jobs[s]:
                            kind, j, n = job
                            i = index[job]
                            if kind == "mean":
                                dve.wait_ge(side_done, i + 1)
                                dve.tensor_tensor(acc[:, j % 2, chunk(n)], acc[:, j % 2, chunk(n)], psS[:, i % 2, :],
                                                  ALU.subtract).then_inc(ln_cent, 1)
                            elif kind == "var":
                                dve.wait_ge(ln_r, NCH * j + n + 1)
                                dve.tensor_tensor(acc[:, j % 2, chunk(n)], acc[:, j % 2, chunk(n)], lnr[:, chunk(n)],
                                                  ALU.mult).then_inc(ln_norm, 1)
                            elif kind == "ss":
                                before = sum(1 for k, _ in Z_TILES[:j] if k in "qk")
                                dve.wait_ge(z_dve, sum(dves[:j + 1]))
                                dve.wait_ge(qk_r, NCH * before + n + 1)
                                out, r = zg[:, j % 2, chunk(n)], rr[:, chunk(n)]
                                if Z_TILES[j][0] == "q":
                                    out, r = out.rearrange("p (j r c) -> p j r c", j=COL_BLOCKS, c=Q_COLS), by_block(r)
                                dve.tensor_tensor(out, out, r, ALU.mult).then_inc(qk_out, 1)
                            else:
                                dve.wait_ge(side_done, i + 1)
                                if n == 0:
                                    wait_row(dve, j)
                                dve.tensor_copy(zg[:, j % 2, chunk(n)], psS[:, i % 2, :]).then_inc(v_out, 1)
                        if s < NZ:
                            kind, j = Z_TILES[s]
                            if kind == "value":
                                dve.wait_ge(z_done, s + 1)
                                dve.wait_ge(z_act, sum(acts[:s + 1]))
                                if j >= 3:
                                    dve.wait_ge(conv_s, CONV_K * (j - 2))
                                    dve.wait_ge(conv_p, CONV_K * (j - 2))
                                p0 = psZ[:, 3 * (s % 2), :]
                                p1 = psZ[:, 3 * (s % 2) + 1:3 * (s % 2) + 3, :].rearrange("p a b -> p (a b)")
                                dve.tensor_tensor(u[:, j % 3, U_P + PAD:U_P + PAD + PROMPT], p0, sg[:, 0:PROMPT], ALU.mult)
                                dve.tensor_tensor(u[:, j % 3, U_S + PAD:U_S + PAD + SAMPLE], p1, sg[:, PROMPT:TOKENS],
                                                  ALU.mult).then_inc(z_dve, 1)
                            elif kind in "qk":
                                dve.wait_ge(z_act, sum(acts[:s + 1]))
                                wait_row(dve, s)
                                col = 0 if kind == "q" else 1
                                for n in range(NCH):
                                    out, prods = zg[:, s % 2, chunk(n)], psZ[:, 3 * (s % 2) + n, :]
                                    if kind == "q":
                                        out = out.rearrange("p (j r c) -> p j r c", j=COL_BLOCKS, c=Q_COLS)
                                        prods = by_block(prods)
                                    m = dve.tensor_scalar(out, prods, qkg[:, col:col + 1],
                                                          DH ** -0.5 if kind == "q" else 1.0, ALU.mult, ALU.mult)
                                m.then_inc(z_dve, 1)


def attend(nc, A, sem, sb, ps, qk_d, v_d, ident, attn):
    NB = len(BLOCKS)
    UNITS = HEADS * NB
    PAIRS = UNITS // 2
    qk_loaded = [sem(f"qk_loaded{i}") for i in range(4)]
    v_loaded = [sem(f"v_loaded{i}") for i in range(len(V_ROWS))]
    bias_loaded = [sem(f"bias_loaded{i}") for i in range(4)]
    s_done, s_biased, m_neg, p_ready, p_scaled = (
        sem("s_done"), sem("s_biased"), sem("m_neg"), sem("p_ready"), sem("p_scaled"))
    pT_done, pT_out, o_done, r_ready, o_out = sem("pT_done"), sem("pT_out"), sem("o_done"), sem("r_ready"), sem("o_out")
    with ExitStack() as c:
        qk = sb(c, "qk", [P, 8, TOKENS])
        v = sb(c, "v", [P, len(V_ROWS) * COL_BLOCKS, WA])
        bias = sb(c, "bias", [P, 4, 3, BIAS_COLS])
        sc = sb(c, "sc", [P, 2, 384])
        pr = sb(c, "pr", [P, 3, 384])
        pT = sb(c, "pT", [P, 2, 3, 2, P])
        mx = sb(c, "mx", [P, 4])
        nm = sb(c, "nm", [P, 4])
        sm = sb(c, "sm", [P, 4])
        rs = sb(c, "rs", [P, 4])
        psS = ps(c, "psSc", [P, 3, 512])
        psT = ps(c, "psPT", [P, 2, 512])
        psO = ps(c, "psOh", [P, 3, 512])

        def unit(i):
            u, w = divmod(i, 2)
            t, b = divmod(u, NB)
            return 2 * t + w, b, *BLOCKS[b]

        def load_v(eng, n):
            t0, r0 = V_ROWS[n]
            for j in range(COL_BLOCKS):
                for r in range(4):
                    at = t0 + (r0 + r) * GRID_W + KEY_COL0[j]
                    eng.dma_start(v[r * K_COLS:(r + 1) * K_COLS, n * COL_BLOCKS + j, :],
                                  v_d[at:at + K_COLS, :]).then_inc(v_loaded[n], 16)

        with nc.Block() as block:
            @block.sync
            def _(sp):
                def heads(t):
                    for w in range(2):
                        sp.dma_start(qk[:, 4 * w + t, :], qk_d[4 * w + t]).then_inc(qk_loaded[t], 16)

                def biases(h):
                    if h >= 4:
                        sp.wait_ge(s_biased, 2 * NB * (h // 2 - 1))
                    sp.dma_start(bias[:, h % 4], A["bias"][h]).then_inc(bias_loaded[h % 4], 16)
                heads(0)
                biases(0)
                biases(1)
                for n in range(2, len(V_ROWS)):
                    load_v(sp, n)
                for t in range(1, 4):
                    heads(t)
                for h in range(2, HEADS):
                    biases(h)

            @block.tensor
            def _(pe):
                def scores(i):
                    h, b, s, j = unit(i)
                    t0, qr, kr, rows, _, _ = ROW_SETS[s]
                    if b == 0 and h % 2 == 0:
                        pe.wait_ge(qk_loaded[h // 2], 32)
                    if i >= 3:
                        pe.wait_ge(s_biased, i - 2)
                    lo = DH * (h % 2)
                    at = t0 + qr * GRID_W + j * P
                    q = qk[lo:lo + DH, h // 2, at:at + P]
                    k = qk[lo:lo + DH, 4 + h // 2, t0 + kr * GRID_W:t0 + (kr + rows) * GRID_W].rearrange(
                        "p (r c) -> p r c", c=GRID_W)[:, :, KEY_COL0[j]:KEY_COL0[j] + K_COLS]
                    pe.matmul(psS[:, i % 3, 0:rows * K_COLS], q, k, start=True, stop=True).then_inc(s_done, 1)

                def turn(i):
                    pe.wait_ge(p_scaled, i + 1)
                    if i >= 2:
                        pe.wait_ge(pT_out, i - 1)
                    for m in range(ROW_SETS[unit(i)[2]][3] // 4):
                        mm = pe.transpose(psT[:, i % 2, m * P:(m + 1) * P], pr[:, i % 3, m * P:(m + 1) * P], ident[:, :])
                    mm.then_inc(pT_done, 1)

                def pv(u):
                    h, b, s, j = unit(2 * u)
                    t0, qr, kr, rows, _, _ = ROW_SETS[s]
                    first = V_ROWS.index((t0, kr))
                    pe.wait_ge(pT_out, 2 * u + 2)
                    if h == 0 and j == 0:
                        for m in range(rows // 4):
                            pe.wait_ge(v_loaded[first + m], 16 * 4 * COL_BLOCKS)
                    if u >= 3:
                        pe.wait_ge(o_out, u - 2)
                    for m in range(rows // 4):
                        mm = pe.matmul(psO[:, u % 3, 0:2 * P], v[:, (first + m) * COL_BLOCKS + j, h * DH:(h + 2) * DH],
                                       pT[:, u % 2, m, :, :].rearrange("p w q -> p (w q)"),
                                       start=(m == 0), stop=(m == rows // 4 - 1))
                    mm.then_inc(o_done, 1)

                for i in range(UNITS + 4):
                    if i < UNITS:
                        scores(i)
                    if 3 <= i < UNITS + 3:
                        turn(i - 3)
                    if i >= 5 and i % 2:
                        pv((i - 5) // 2)

            @block.vector
            def _(dve):
                for i in range(UNITS + 5):
                    if i < UNITS:
                        h, b, s, j = unit(i)
                        w = ROW_SETS[s][3] * K_COLS
                        at = ROW_SETS[s][5]
                        if b == 0:
                            dve.wait_ge(bias_loaded[h % 4], 16 * (h // 4 + 1))
                        dve.wait_ge(s_done, i + 1)
                        if i >= 2:
                            dve.wait_ge(p_ready, i - 1)
                        dve.tensor_tensor_reduce(out=sc[:, i % 2, 0:w], in0=psS[:, i % 3, 0:w],
                                                 in1=bias[:, h % 4, PATTERN[j], at:at + w], scale=1.0, scalar=-3e38,
                                                 op0=ALU.add, op1=ALU.max, accum_out=mx[:, i % 4:i % 4 + 1]).then_inc(s_biased, 1)
                        dve.wait_ge(s_biased, i + 1)
                        dve.tensor_scalar(nm[:, i % 4:i % 4 + 1], mx[:, i % 4:i % 4 + 1], -1.0, None,
                                          ALU.mult).then_inc(m_neg, 1)
                    if 1 <= i < UNITS + 1:
                        e = i - 1
                        w = ROW_SETS[unit(e)[2]][3] * K_COLS
                        one = slice(e % 4, e % 4 + 1)
                        dve.wait_ge(p_ready, e + 1)
                        dve.reciprocal(rs[:, one], sm[:, one]).then_inc(r_ready, 1)
                        dve.wait_ge(r_ready, e + 1)
                        dve.tensor_scalar(pr[:, e % 3, 0:w], pr[:, e % 3, 0:w], rs[:, one], None, ALU.mult).then_inc(p_scaled, 1)
                    if i >= 6 and i % 2 == 0:
                        u = (i - 6) // 2
                        h, b, s, j = unit(2 * u)
                        t0, qr = ROW_SETS[s][:2]
                        dve.wait_ge(o_done, u + 1)
                        for w in range(2):
                            rows = slice(w * DH, (w + 1) * DH)
                            out = attn[rows, h // 2, t0 + qr * GRID_W:t0 + (qr + 8) * GRID_W].rearrange(
                                "p (r c) -> p r c", c=GRID_W)[:, :, j * Q_COLS:(j + 1) * Q_COLS]
                            m = dve.tensor_copy(out, psO[rows, u % 3, w * P:(w + 1) * P].rearrange("p (r c) -> p r c", c=Q_COLS))
                        m.then_inc(o_out, 1)

            @block.scalar
            def _(act):
                load_v(act, 0)
                load_v(act, 1)
                for i in range(UNITS + 2):
                    if i < UNITS:
                        w = ROW_SETS[unit(i)[2]][3] * K_COLS
                        act.wait_ge(m_neg, i + 1)
                        if i >= 3:
                            act.wait_ge(pT_done, i - 2)
                        if i >= 4:
                            act.wait_ge(r_ready, i - 3)
                        act.activation(pr[:, i % 3, 0:w], sc[:, i % 2, 0:w], ACT.Exp, bias=nm[:, i % 4:i % 4 + 1],
                                       accum_out=sm[:, i % 4:i % 4 + 1]).then_inc(p_ready, 1)
                    if i >= 2:
                        e = i - 2
                        n = ROW_SETS[unit(e)[2]][3] // 4
                        act.wait_ge(pT_done, e + 1)
                        if e >= 4:
                            act.wait_ge(o_done, e // 2 - 1)
                        act.activation(pT[:, (e // 2) % 2, 0:n, e % 2, :],
                                       psT[:, e % 2, 0:n * P].rearrange("p (m q) -> p m q", q=P), ACT.Copy).then_inc(pT_out, 1)


def mix(nc, A, sem, sb, ps, rows_of, x_d, y_d, ada_d, conv_d, xhat_d, ident, eps_col, modv, a2, affT, attn):
    XR = 3
    conv_loaded = [sem(f"conv_loaded{i}") for i in range(NCH)]
    gate_loaded = sem("gate1_loaded")
    w_loaded = [sem(f"w_out_loaded{i}") for i in range(KD)]
    w_hi_ready, w_lo_ready = sem("w_out_hi"), sem("w_out_lo")
    m_hi, m_lo, mixed = sem("mix_hi"), sem("mix_lo"), sem("mixed")
    x_loaded = [sem(f"x3_loaded{i}") for i in range(XR)]
    gated, x1_ready, sq_done, ms_done, rt_done, r_done, xh_ready = (
        sem("gated"), sem("x1_ready"), sem("x1_sq"), sem("x1_ms"), sem("x1_rt"), sem("x1_rstd"), sem("xh_ready"))
    x1_stored = [sem(f"x1_stored{i}") for i in range(XR)]
    xh_stored = [sem(f"xh_stored{i}") for i in range(2)]
    xhT_done, h2_ready, logit_done, l_max, l_neg, l_exp, l_rec, aff_ready, aff_t, aff_out, wr_loaded, aff_zero = (
        sem("xhT_done"), sem("h2_ready"), sem("logit_done"), sem("l_max"), sem("l_neg"), sem("l_exp"), sem("l_rec"),
        sem("aff_ready"), sem("aff_turned"), sem("aff_out"), sem("w_router_loaded"), sem("aff_zero"))
    with ExitStack() as c:
        conv = sb(c, "conv3", [P, 4, TOKENS])
        w_hi = sb(c, "wo_hi", [P, KD, D], F32R)
        w_lo = sb(c, "wo_lo", [P, KD, D], F32R)
        mh = sb(c, "mh", [P, 2, KD, P], F32R)
        ml = sb(c, "ml", [P, 2, KD, P], F32R)
        gate1 = sb(c, "gate1", [P, 2, D])
        w_raw = sb(c, "wo_raw", [P, KD, D])
        xt, tg, xh = w_raw[:, 0:XR, :], w_raw[:, XR, :], w_raw[:, XR + 1:XR + 3, :]
        h2 = w_raw[:, XR + 3:XR + 5, :].rearrange("p a (k t) -> p a k t", k=KD)
        wr = sb(c, "wr", [P, KD, EXPERTS])
        st = sb(c, "st3", [P, 4, TILES])
        lg = sb(c, "lg", [P, 4, 2])
        ex = sb(c, "ex", [P, 2, EXPERTS])
        af = sb(c, "af", [P, 2, 48])
        psO = ps(c, "psMix", [P, 4, 512])
        psT = ps(c, "psXT", [P, 2, 512])
        psL = ps(c, "psLog", [P, 2, 512])

        with nc.Block() as block:
            @block.sync
            def _(sp):
                def load_conv(n):
                    sp.dma_start(conv[:, :, n * 512:(n + 1) * 512],
                                 conv_d.rearrange("j p t -> p j t")[:, :, n * 512:(n + 1) * 512]).then_inc(conv_loaded[n], 16)
                load_conv(0)
                for k in range(KD):
                    sp.dma_start(w_raw[:, k, :], A["w_out"][k * P:(k + 1) * P, :]).then_inc(w_loaded[k], 16)
                for grp in range(2):
                    sp.dma_start(gate1[:, grp, :], ada_d[grp:grp + 1, 2 * D:3 * D].to_broadcast([P, D])).then_inc(gate_loaded, 16)
                sp.dma_start(wr[:, :, :], A["w_router"].rearrange("(p k) n -> p k n", k=KD)).then_inc(wr_loaded, 16)
                sp.wait_ge(w_lo_ready, KD)
                for s in range(TILES + 2):
                    if s == 1:
                        for n in range(1, NCH):
                            load_conv(n)
                    if s < TILES:
                        if s >= XR:
                            sp.wait_ge(x1_stored[s % XR], 16 * (s // XR))
                            sp.wait_ge(xh_ready, s - XR + 1)
                        sp.dma_start(xt[:, s % XR, :], rows_of(x_d, s)).then_inc(x_loaded[s % XR], 16)
                    if s >= 2:
                        t = s - 2
                        sp.wait_ge(x1_ready, t + 1)
                        sp.dma_start(rows_of(y_d, t), xt[:, t % XR, :]).then_inc(x1_stored[t % XR], 16)
                        sp.wait_ge(xh_ready, t + 1)
                        sp.dma_start(xhat_d[t * P:(t + 1) * P, :], xh[:, t % 2, :]).then_inc(xh_stored[t % 2], 16)
                for i in range(XR):
                    sp.wait_ge(x1_stored[i], 16 * (TILES // XR))
                for i in range(2):
                    sp.wait_ge(xh_stored[i], 16 * (TILES // 2))

            @block.gpsimd
            def _(pool):
                pool.memset(af[:, :, :], 0.0).then_inc(aff_zero, 1)
                pool.memset(affT[:, :], -1.0).then_inc(aff_zero, 1)

            @block.tensor
            def _(pe):
                for s in range(TILES + 3):
                    if s < TILES:
                        pe.wait_ge(m_lo, s + 1)
                        if s >= 2:
                            pe.wait_ge(gated, s - 1)
                        for n in range(2):
                            for k in range(KD):
                                if s == 0 and n == 0:
                                    pe.wait_ge(w_lo_ready, k + 1)
                                for i, (m, w) in enumerate(((mh, w_hi), (mh, w_lo), (ml, w_hi))):
                                    mm = pe.matmul(psO[:, 2 * (s % 2) + n, :], m[:, s % 2, k, :],
                                                   w[:, k, n * 512:(n + 1) * 512], start=(k == 0 and i == 0),
                                                   stop=(k == KD - 1 and i == 2))
                        mm.then_inc(mixed, 1)
                    if 1 <= s < TILES + 1:
                        t = s - 1
                        pe.wait_ge(xh_ready, t + 1)
                        if t >= 1:
                            pe.wait_ge(h2_ready, t)
                        xk = xh[:, t % 2, :].rearrange("p (d k) -> p k d", k=KD)
                        for k in range(KD):
                            mm = pe.transpose(psT[:, k // 4, (k % 4) * P:(k % 4 + 1) * P], xk[:, k, :], ident[:, :])
                        mm.then_inc(xhT_done, 1)
                    if 2 <= s < TILES + 2:
                        t = s - 2
                        pe.wait_ge(h2_ready, t + 1)
                        if t >= 1:
                            pe.wait_ge(l_exp, t)
                        for k in range(KD):
                            mm = pe.matmul(psL[:, 0, 0:EXPERTS], h2[:, t % 2, k, :], wr[:, k, :], start=(k == 0), stop=(k == KD - 1))
                        mm.then_inc(logit_done, 1)
                    if s >= 3:
                        t = s - 3
                        pe.wait_ge(aff_ready, t + 1)
                        if t >= 1:
                            pe.wait_ge(aff_out, t)
                        pe.transpose(psL[0:48, 1, 0:P], af[:, t % 2, :], ident[:, :]).then_inc(aff_t, 1)

            @block.scalar
            def _(act):

                def split(t):
                    if t >= 2:
                        act.wait_ge(mixed, t - 1)
                    if t % 4 == 0:
                        act.wait_ge(conv_loaded[t // 4], 16)
                    act.activation(mh[:, t % 2, 0:4], attn[:, :, t * P:(t + 1) * P], ACT.Copy)
                    act.activation(mh[:, t % 2, 4:8], conv[:, :, t * P:(t + 1) * P], ACT.Copy).then_inc(m_hi, 1)
                split(0)
                for k in range(KD):
                    act.wait_ge(w_loaded[k], 16)
                    act.activation(w_hi[:, k, :], w_raw[:, k, :], ACT.Copy).then_inc(w_hi_ready, 1)
                for s in range(TILES + 2):
                    if s + 1 < TILES:
                        split(s + 1)
                    if 1 <= s < TILES + 1:
                        t = s - 1
                        act.wait_ge(x1_ready, t + 1)
                        act.activation(tg, xt[:, t % XR, :], ACT.Square,
                                       accum_out=st[:, 0, t:t + 1]).then_inc(sq_done, 1)
                        act.wait_ge(ms_done, t + 1)
                        act.activation(st[:, 2, t:t + 1], st[:, 1, t:t + 1], ACT.Sqrt).then_inc(rt_done, 1)
                        act.wait_ge(xhT_done, t + 1)
                        if t >= 2:
                            act.wait_ge(logit_done, t - 1)
                        for k in range(KD):
                            m = act.activation(h2[:, t % 2, k, :], psT[:, k // 4, (k % 4) * P:(k % 4 + 1) * P], ACT.Identity,
                                               bias=modv[:, group(t), 2, k:k + 1], scale=a2[:, group(t), k:k + 1])
                        m.then_inc(h2_ready, 1)
                    if s >= 2:
                        t = s - 2
                        act.wait_ge(l_neg, t + 1)
                        if t >= 2:
                            act.wait_ge(aff_ready, t - 1)
                        act.activation(ex[:, t % 2, :], psL[:, 0, 0:EXPERTS], ACT.Exp, bias=lg[:, 1, t % 2:t % 2 + 1],
                                       accum_out=lg[:, 2, t % 2:t % 2 + 1]).then_inc(l_exp, 1)

            @block.vector
            def _(dve):
                def split(t):
                    dve.wait_ge(m_hi, t + 1)
                    dve.tensor_tensor(ml[:, t % 2, 0:4], attn[:, :, t * P:(t + 1) * P], mh[:, t % 2, 0:4].bitcast(F32),
                                      ALU.subtract)
                    dve.tensor_tensor(ml[:, t % 2, 4:8], conv[:, :, t * P:(t + 1) * P], mh[:, t % 2, 4:8].bitcast(F32),
                                      ALU.subtract).then_inc(m_lo, 1)
                split(0)
                for k in range(KD):
                    dve.wait_ge(w_hi_ready, k + 1)
                    dve.tensor_tensor(w_lo[:, k, :], w_raw[:, k, :], w_hi[:, k, :].bitcast(F32),
                                      ALU.subtract).then_inc(w_lo_ready, 1)
                dve.wait_ge(gate_loaded, 32)
                dve.wait_ge(aff_zero, 2)
                for s in range(TILES + 3):
                    if s + 1 < TILES:
                        split(s + 1)
                    if 1 <= s < TILES + 1:
                        t = s - 1
                        dve.wait_ge(mixed, t + 1)
                        dve.wait_ge(x_loaded[t % XR], 16 * (t // XR + 1))
                        if t >= 1:
                            dve.wait_ge(sq_done, t)
                        dve.tensor_tensor(tg, psO[:, 2 * (t % 2):2 * (t % 2) + 2, :].rearrange("p a b -> p (a b)"),
                                          gate1[:, group(t), :], ALU.mult).then_inc(gated, 1)
                        dve.wait_ge(gated, t + 1)
                        dve.tensor_tensor(xt[:, t % XR, :], xt[:, t % XR, :], tg, ALU.add).then_inc(x1_ready, 1)
                        dve.wait_ge(sq_done, t + 1)
                        dve.tensor_scalar(st[:, 1, t:t + 1], st[:, 0, t:t + 1], 1.0 / D, EPS, ALU.mult, ALU.add).then_inc(ms_done, 1)
                        dve.wait_ge(rt_done, t + 1)
                        dve.reciprocal(st[:, 3, t:t + 1], st[:, 2, t:t + 1]).then_inc(r_done, 1)
                        dve.wait_ge(r_done, t + 1)
                        if t >= 2:
                            dve.wait_ge(xhT_done, t - 1)
                            dve.wait_ge(xh_stored[t % 2], 16 * (t // 2))
                        dve.tensor_scalar(xh[:, t % 2, :], xt[:, t % XR, :], st[:, 3, t:t + 1], None, ALU.mult).then_inc(xh_ready, 1)
                    if 2 <= s < TILES + 2:
                        t = s - 2
                        dve.wait_ge(logit_done, t + 1)
                        dve.reduce_max(lg[:, 0, t % 2:t % 2 + 1], psL[:, 0, 0:EXPERTS], AX.X).then_inc(l_max, 1)
                        dve.wait_ge(l_max, t + 1)
                        dve.tensor_scalar(lg[:, 1, t % 2:t % 2 + 1], lg[:, 0, t % 2:t % 2 + 1], -1.0, None, ALU.mult).then_inc(l_neg, 1)
                        dve.wait_ge(l_exp, t + 1)
                        dve.reciprocal(lg[:, 3, t % 2:t % 2 + 1], lg[:, 2, t % 2:t % 2 + 1]).then_inc(l_rec, 1)
                        dve.wait_ge(l_rec, t + 1)
                        at = 32 * group(t)
                        if t >= 2:
                            dve.wait_ge(aff_t, t - 1)
                        if t == 4 or t == 5:
                            dve.memset(af[:, t % 2, 0:EXPERTS], 0.0)
                        dve.tensor_scalar(af[:, t % 2, at:at + EXPERTS], ex[:, t % 2, :], lg[:, 3, t % 2:t % 2 + 1], None,
                                          ALU.mult).then_inc(aff_ready, 1)
                    if s >= 3:
                        t = s - 3
                        grp = group(t)
                        dve.wait_ge(aff_t, t + 1)
                        col = t * P - (PROMPT if grp else 0)
                        dve.tensor_copy(affT[32 * grp:32 * grp + EXPERTS, col:col + P],
                                        psL[32 * grp:32 * grp + EXPERTS, 1, 0:P]).then_inc(aff_out, 1)


def experts(nc, A, sem, sb, ps, y_d, ada_d, xhat_d, ident, modv, a2, affT):
    RING_GU, RING_DN = 3, 3
    HS = 3
    ROUNDS = CAP_S // 8
    AHEAD, BEHIND = 2, 2
    top_v, top_i, top_d = sem("top_vals"), sem("top_idx"), sem("top_drop")
    idx_f, tT_done, sel_ready = sem("idx_float"), sem("top_turned"), sem("sel_ready")
    gate_loaded = sem("gate2_loaded")
    gu_loaded = [sem(f"w_gu_loaded{i}") for i in range(RING_GU)]
    dn_loaded = [sem(f"w_dn_loaded{i}") for i in range(RING_DN)]
    gu_hi, gu_lo = sem("w_gu_hi"), sem("w_gu_lo")
    dn_hi, dn_lo = sem("w_dn_hi"), sem("w_dn_lo")
    gu_done, dn_done = sem("gate_up_done"), sem("down_done")
    gu_low, gu_sum = sem("gate_up_low"), sem("gate_up_summed")
    silu_done, hid_done, hid_hi, hid_lo = sem("silu_done"), sem("hid_done"), sem("hid_hi"), sem("hid_lo")
    pool_steps = sem("pool_steps")
    idx_now, g_loaded_p, g_loaded_s = sem("idx_now"), sem("gathered_p"), sem("gathered_s")
    x_turned, xs_ready, x_hi, x_lo = sem("x_turned"), sem("xe_staged"), sem("xe_hi"), sem("xe_lo")
    y_half, y_sent_s, y_sent_p, y_scaled = sem("y_half"), sem("scattered_s"), sem("scattered_p"), sem("y_scaled")

    def last_user(j, ring, count):
        return j - ring if j >= ring else max(range(j % ring, count, ring)) - count

    def turned_in(i):
        return (i - 6) // 2 if i % 2 == 0 and 6 <= i < 6 + 2 * KD else None

    with ExitStack() as c:
        raw_gu = sb(c, "raw_gu", [P, RING_GU, 2, 2, KD * P])
        raw_dn = sb(c, "raw_dn", [P, RING_DN, 2, D])
        w_hi = sb(c, "w_gu_hi_part", [P, 2, 2, KD * P], F32R)
        w_lo = sb(c, "w_gu_lo_part", [P, 2, 2, KD * P], F32R)
        d_hi = sb(c, "w_dn_hi_part", [P, 2, D], F32R)
        d_lo = sb(c, "w_dn_lo_part", [P, 2, D], F32R)
        xg_s = sb(c, "xg_s", [P, D])
        xg_p = sb(c, "xg_p", [CAP_P, D])
        xst = sb(c, "xst", [P, KD, CAP])
        xe = sb(c, "xe", [P, KD, 2, CAP], F32R)
        low = sb(c, "low", [P, 2, 2, CAP])
        gu = sb(c, "gu", [P, 2, 2, CAP])
        sl = sb(c, "sl", [P, 2, CAP])
        hid = sb(c, "hid", [P, 2, CAP])
        hs = sb(c, "hs", [P, HS, 2 * CAP], F32R)
        ye = sb(c, "ye", [P, D])
        yp = sb(c, "yp", [CAP_P, D])
        gate2 = sb(c, "gate2", [P, 2, D])
        vals = sb(c, "vals", [48, CAP_S])
        idxu = sb(c, "idxu", [48, CAP_S], U32)
        idxf = sb(c, "idxf", [48, CAP_S])
        gsel = sb(c, "gsel", [P, 48])
        isel = sb(c, "isel", [P, 48], U32)
        iall = sb(c, "iall", [P, EXPERTS], U32)
        gnow = sb(c, "gnow", [P, 2])
        inow = sb(c, "inow", [P, 2, 4], U32)
        psG = ps(c, "psG", [P, 4, 512])
        psY = ps(c, "psY", [P, 4, 512])

        def e_at(ap, e):
            return ap[bass.ds(e, 1)]

        w_gu = A["w_gu"]
        w_dn = A["w_down"].rearrange("e (c t p) d -> e c p t d", c=CHUNKS, t=2)

        with nc.Block() as block:
            @block.sync
            def _(sp):
                for grp in range(2):
                    sp.dma_start(gate2[:, grp, :], ada_d[grp:grp + 1, 5 * D:6 * D].to_broadcast([P, D])).then_inc(gate_loaded, 16)

                def load_gu(e, ci, first):
                    back = last_user(ci, RING_GU, CHUNKS)
                    if not (first and back < 0):
                        sp.wait_ge(gu_lo, (e * CHUNKS + back + 1) * 4)
                    s = ci % RING_GU
                    sp.dma_start(raw_gu[:, s], e_at(w_gu, e)[0, ci]).then_inc(gu_loaded[s], 16)

                def load_dn(e, ci, first):
                    back = last_user(ci, RING_DN, CHUNKS)
                    if not (first and back < 0):
                        sp.wait_ge(dn_lo, (e * CHUNKS + back + 1) * 2)
                    s = ci % RING_DN
                    sp.dma_start(raw_dn[:, s], e_at(w_dn, e)[0, ci]).then_inc(dn_loaded[s], 16)

                def loads(e, first):
                    for ci in range(CHUNKS):
                        load_gu(e, ci, first)
                        if ci >= 1:
                            load_dn(e, ci - 1, first)
                    load_dn(e, CHUNKS - 1, first)
                loads(0, True)
                with sp.Fori(1, EXPERTS) as e:
                    loads(e, False)

            @block.tensor
            def _(pe):
                pe.wait_ge(top_v, ROUNDS)
                pe.transpose(psG[:, 0, 0:48], vals[:, :], ident[0:48, 0:48]).then_inc(tT_done, 1)
                pe.wait_ge(idx_f, 1)
                pe.transpose(psG[:, 1, 0:48], idxf[:, :], ident[0:48, 0:48]).then_inc(tT_done, 1)

                def turn(k, bank):
                    pe.transpose(psG[:, bank, 2 * CAP:2 * CAP + P], xg_s[:, :].rearrange("p (d k) -> p k d", k=KD)[:, k, :], ident[:, :])
                    pe.transpose(psG[:, bank + 1, 2 * CAP:2 * CAP + CAP_P], xg_p[:, :].rearrange("p (d k) -> p k d", k=KD)[:, k, :],
                                 ident[0:CAP_P, 0:CAP_P]).then_inc(x_turned, 1)

                pe.wait_ge(sel_ready, 1)
                pe.wait_ge(g_loaded_s, 16)
                pe.wait_ge(g_loaded_p, 16)
                for k in range(KD):
                    if k >= 2:
                        pe.wait_ge(xs_ready, k - 1)
                    turn(k, 2 * (k % 2))

                def gate_up(e, i, first):
                    a = i % 2
                    n = e * FT + i
                    if i == 0:
                        pe.wait_ge(x_lo, e + 1)
                    if not (first and i < 2):
                        pe.wait_ge(gu_sum, n - 1)
                    if turned_in(i) is not None:
                        k = turned_in(i)
                        if k == 0:
                            pe.wait_ge(g_loaded_s, 16 * (e + 2))
                            pe.wait_ge(g_loaded_p, 16 * (e + 2))
                        pe.wait_ge(xs_ready, KD * (e + 1) + k)
                        turn(k, 2 * a)
                    for m in range(2):
                        pe.wait_ge(gu_lo, 2 * n + m + 1)
                        bank = psG[:, 2 * a + m]
                        for k in range(KD):
                            wh, wl = (w[:, a, m, k * P:(k + 1) * P] for w in (w_hi, w_lo))
                            pe.matmul(bank[:, 0:2 * CAP], wh, xe[:, k, :, :].rearrange("p a b -> p (a b)"), start=(k == 0), stop=False,
                                      skip_group_check=True)
                            mm = pe.matmul(bank[:, 0:CAP], wl, xe[:, k, 0, :], start=False, stop=(k == KD - 1),
                                           skip_group_check=True)
                    mm.then_inc(gu_done, 1)

                def down(e, i, first):
                    a = i % 2
                    n = e * FT + i
                    pe.wait_ge(dn_lo, n + 1)
                    pe.wait_ge(hid_lo, n + 1)
                    if i == 0 and not first:
                        pe.wait_ge(y_scaled, 3 * e)
                    st, en = i == 0, i == FT - 1
                    s_hi, pp, s_lo = (hs[:, i % HS, at * P:(at + 1) * P] for at in range(3))
                    for h in range(2):
                        wh, wl = (w[:, a, h * 512:(h + 1) * 512] for w in (d_hi, d_lo))
                        pe.matmul(psY[:, h, :], s_hi, wh, start=st, stop=False)
                        pe.matmul(psY[:, h, :], s_hi, wl, start=False, stop=False)
                        pe.matmul(psY[:, h, :], s_lo, wh, start=False, stop=en)
                        pe.matmul(psY[:, 2 + h, :], pp, wh, start=st, stop=False)
                        mm = pe.matmul(psY[:, 2 + h, :], pp, wl, start=False, stop=en)
                    mm.then_inc(dn_done, 1)

                def expert(e, first):
                    for i in range(FT + BEHIND):
                        if i < FT:
                            gate_up(e, i, first)
                        if i >= BEHIND:
                            down(e, i - BEHIND, first)
                expert(0, True)
                with pe.Fori(1, EXPERTS) as e:
                    expert(e, False)

            @block.gpsimd
            def _(pool):
                def gather(e_next):
                    pool.indirect_dma_start(out=xg_p[:, :], out_offset=None, in_=xhat_d,
                                            in_offset=bass.IndirectOffsetOnAxis(ap=inow[0:CAP_P, 1, 0:1], axis=0)).then_inc(g_loaded_p, 16)
                    pool.indirect_dma_start(out=xg_s[:, :], out_offset=None, in_=xhat_d,
                                            in_offset=bass.IndirectOffsetOnAxis(ap=inow[:, 1, 1:2], axis=0)).then_inc(g_loaded_s, 16)

                def lists(e, slot):
                    pool.tensor_copy(inow[:, slot, 0:1], isel[:, bass.ds(e, 1)])
                    pool.tensor_copy(inow[:, slot, 2:3], isel[:, bass.ds(e, 1)])
                    pool.tensor_copy(inow[:, slot, 3:4], isel[:, bass.ds(e + 32, 1)])
                    pool.tensor_copy(inow[:, slot, 1:2], iall[:, bass.ds(e, 1)]).then_inc(idx_now, 1)

                def scatter(e):
                    pool.wait_ge(y_scaled, 3 * e + 3)
                    pool.sem_inc(pool_steps)
                    pool.indirect_dma_start(out=y_d[1], out_offset=bass.IndirectOffsetOnAxis(ap=inow[:, 0, 3:4], axis=0),
                                            in_=ye[:, :], in_offset=None, compute_op=ALU.add).then_inc(y_sent_s, 16)
                    pool.indirect_dma_start(out=y_d[0], out_offset=bass.IndirectOffsetOnAxis(ap=inow[0:CAP_P, 0, 2:3], axis=0),
                                            in_=yp[:, :], in_offset=None, compute_op=ALU.add).then_inc(y_sent_p, 16)
                    pool.wait_ge(y_sent_s, 16 * (e + 1))
                    pool.wait_ge(y_sent_p, 16 * (e + 1))

                pool.wait_ge(sel_ready, 1)
                lists(0, 1)
                pool.wait_ge(idx_now, 1)
                gather(0)

                def expert(e, nxt):
                    pool.wait_ge(g_loaded_s, 16 * (e + 1))
                    pool.wait_ge(g_loaded_p, 16 * (e + 1))
                    pool.wait_ge(x_turned, KD * (e + 1))
                    lists(e, 0)
                    lists(nxt, 1)
                    pool.wait_ge(idx_now, 2 * e + 3)
                    pool.sem_inc(pool_steps)
                    gather(e + 1)
                    scatter(e)
                with pool.Fori(0, EXPERTS - 1) as e:
                    expert(e, e + 1)
                expert(EXPERTS - 1, 0)
                pool.wait_ge(g_loaded_s, 16 * (EXPERTS + 1))
                pool.wait_ge(g_loaded_p, 16 * (EXPERTS + 1))

            def splits(e, i, last):
                if i + AHEAD < FT:
                    return e, i + AHEAD
                return None if last else (e + 1, i + AHEAD - FT)

            @block.scalar
            def _(act):
                def stage(k, bank):
                    for grp, b, cols in ((1, bank, slice(0, P)), (0, bank + 1, slice(P, CAP))):
                        m = act.activation(xst[:, k, cols], psG[:, b, 2 * CAP:2 * CAP + cols.stop - cols.start], ACT.Identity,
                                           bias=modv[:, grp, 2, k:k + 1], scale=a2[:, grp, k:k + 1])
                    m.then_inc(xs_ready, 1)

                def hi(e, i, m):
                    ci = i // 2
                    s = ci % RING_GU
                    per = len(range(s, CHUNKS, RING_GU))
                    if m == 0 and i % 2 == 0:
                        act.wait_ge(gu_loaded[s], (e * per + ci // RING_GU + 1) * 16)
                    act.activation(w_hi[:, i % 2, m], raw_gu[:, s, m, i % 2], ACT.Copy).then_inc(gu_hi, 1)

                def hi_down(e, i, first):
                    ci = i // 2
                    s = ci % RING_DN
                    per = len(range(s, CHUNKS, RING_DN))
                    if i % 2 == 0:
                        act.wait_ge(dn_loaded[s], (e * per + ci // RING_DN + 1) * 16)
                    if not (first and i < 2):
                        act.wait_ge(dn_done, e * FT + i - 1)
                    act.activation(d_hi[:, i % 2], raw_dn[:, s, i % 2], ACT.Copy).then_inc(dn_hi, 1)

                def xsplit(e):
                    act.wait_ge(xs_ready, KD * (e + 1))
                    act.activation(xe[:, :, 0, :], xst[:, :, :], ACT.Copy).then_inc(x_hi, 1)

                def yhalf(e):
                    act.wait_ge(pool_steps, 2 * e + 1)
                    act.wait_ge(dn_done, (e + 1) * FT)
                    act.activation(yp[:, :], psY[CAP_P:P, 2:4, :].rearrange("p a b -> p (a b)"), ACT.Copy).then_inc(y_half, 1)

                def step(e, i, first, last):
                    a = i % 2
                    n = e * FT + i
                    nxt = splits(e, i, last)
                    act.wait_ge(gu_done, n + 1)
                    if turned_in(i) is not None:
                        stage(turned_in(i), 2 * a)
                    act.activation(low[:, a], psG[:, 2 * a:2 * a + 2, CAP:2 * CAP], ACT.Copy).then_inc(gu_low, 1)
                    if nxt and i < FT - 1:
                        hi(*nxt, 0)
                    act.wait_ge(gu_sum, n + 1)
                    act.activation(sl[:, a, :], gu[:, a, 0, :], ACT.Silu).then_inc(silu_done, 1)
                    if nxt and i < FT - 1:
                        hi(*nxt, 1)
                    back = last_user(i, HS, FT)
                    if not (first and back < 0):
                        act.wait_ge(dn_done, e * FT + back + 1)
                    act.wait_ge(hid_done, n + 1)
                    act.activation(hs[:, i % HS, 0:CAP], hid[:, a, :], ACT.Copy).then_inc(hid_hi, 1)
                    hi_down(e, i, first)
                    if nxt and i == FT - 1:
                        xsplit(e + 1)
                        hi(*nxt, 0)
                        hi(*nxt, 1)

                def expert(e, first, last):
                    for i in range(FT):
                        if i == 0 and not first:
                            yhalf(e - 1)
                        step(e, i, first, last)

                for i in range(AHEAD):
                    for m in range(2):
                        hi(0, i, m)
                for k in range(KD):
                    act.wait_ge(x_turned, k + 1)
                    stage(k, 2 * (k % 2))
                xsplit(0)
                expert(0, True, False)
                with act.Fori(1, EXPERTS - 1) as e:
                    expert(e, False, False)
                expert(EXPERTS - 1, False, True)
                yhalf(EXPERTS - 1)

            @block.vector
            def _(dve):
                for r in range(ROUNDS):
                    sl8 = slice(8 * r, 8 * r + 8)
                    if r:
                        dve.wait_ge(top_d, r)
                    dve.max(vals[:, sl8], affT[:, :]).then_inc(top_v, 1)
                    dve.wait_ge(top_v, r + 1)
                    dve.max_index(idxu[:, sl8], vals[:, sl8], affT[:, :]).then_inc(top_i, 1)
                    dve.wait_ge(top_i, r + 1)
                    dve.match_replace(affT[:, :], vals[:, sl8], affT[:, :], -2.0).then_inc(top_d, 1)
                dve.tensor_copy(idxf[:, :], idxu[:, :]).then_inc(idx_f, 1)
                dve.wait_ge(tT_done, 2)
                dve.tensor_copy(gsel[:, :], psG[:, 0, 0:48])
                dve.tensor_scalar(iall[:, :], psG[:, 1, 32:48], float(PROMPT), None, ALU.add)
                dve.tensor_copy(isel[:, :], psG[:, 1, 0:48]).then_inc(sel_ready, 1)

                def lo(e, i, m):
                    dve.wait_ge(gu_hi, 2 * (e * FT + i) + m + 1)
                    dve.tensor_tensor(w_lo[:, i % 2, m], raw_gu[:, (i // 2) % RING_GU, m, i % 2],
                                      w_hi[:, i % 2, m].bitcast(F32), ALU.subtract).then_inc(gu_lo, 1)

                def lo_down(e, i):
                    dve.wait_ge(dn_hi, e * FT + i + 1)
                    dve.tensor_tensor(d_lo[:, i % 2], raw_dn[:, (i // 2) % RING_DN, i % 2],
                                      d_hi[:, i % 2].bitcast(F32), ALU.subtract).then_inc(dn_lo, 1)

                def xsplit(e):
                    dve.wait_ge(x_hi, e + 1)
                    dve.tensor_tensor(xe[:, :, 1, :], xst[:, :, :], xe[:, :, 0, :].bitcast(F32), ALU.subtract).then_inc(x_lo, 1)

                def y_out(e):
                    dve.wait_ge(pool_steps, 2 * e + 1)
                    dve.tensor_copy(gnow[:, 0:1], gsel[:, bass.ds(e, 1)])
                    dve.tensor_copy(gnow[:, 1:2], gsel[:, bass.ds(e + 32, 1)]).then_inc(y_scaled, 1)
                    dve.wait_ge(y_scaled, 3 * e + 1)
                    dve.wait_ge(dn_done, (e + 1) * FT)
                    dve.scalar_tensor_tensor(out=ye[:, :], in0=psY[:, 0:2, :].rearrange("p a b -> p (a b)"), scalar=gnow[:, 1:2],
                                             in1=gate2[:, 1, :], op0=ALU.mult, op1=ALU.mult)
                    dve.wait_ge(y_half, e + 1)
                    dve.tensor_tensor(yp[:, :], psY[0:CAP_P, 2:4, :].rearrange("p a b -> p (a b)"), yp[:, :], ALU.add).then_inc(y_scaled, 1)
                    dve.wait_ge(y_scaled, 3 * e + 2)
                    dve.scalar_tensor_tensor(out=yp[:, :], in0=yp[:, :], scalar=gnow[0:CAP_P, 0:1],
                                             in1=gate2[0:CAP_P, 0, :], op0=ALU.mult, op1=ALU.mult).then_inc(y_scaled, 1)

                def step(e, i, first, last):
                    a = i % 2
                    n = e * FT + i
                    nxt = splits(e, i, last)
                    dve.wait_ge(gu_low, n + 1)
                    if not (first and i < 2):
                        dve.wait_ge(hid_lo, n - 1)
                    dve.tensor_tensor(gu[:, a], psG[:, 2 * a:2 * a + 2, 0:CAP], low[:, a], ALU.add).then_inc(gu_sum, 1)
                    if nxt and i < FT - 1:
                        lo(*nxt, 0)
                    dve.wait_ge(gu_sum, n + 1)
                    dve.wait_ge(silu_done, n + 1)
                    dve.tensor_tensor(hid[:, a, :], sl[:, a, :], gu[:, a, 1, :], ALU.mult).then_inc(hid_done, 1)
                    if nxt and i < FT - 1:
                        lo(*nxt, 1)
                    dve.wait_ge(hid_hi, n + 1)
                    part = hs[:, i % HS]
                    dve.tensor_tensor(part[:, CAP:CAP + CAP_P], hid[:, a, P:CAP], part[:, P:CAP].bitcast(F32), ALU.subtract)
                    dve.tensor_tensor(part[:, CAP + CAP_P:2 * CAP], hid[:, a, 0:P], part[:, 0:P].bitcast(F32),
                                      ALU.subtract).then_inc(hid_lo, 1)
                    lo_down(e, i)
                    if nxt and i == FT - 1:
                        xsplit(e + 1)
                        lo(*nxt, 0)
                        lo(*nxt, 1)

                def expert(e, first, last):
                    for i in range(FT):
                        if i == 0 and not first:
                            y_out(e - 1)
                        step(e, i, first, last)

                dve.wait_ge(sel_ready, 1)
                dve.wait_ge(gate_loaded, 32)
                for i in range(AHEAD):
                    for m in range(2):
                        lo(0, i, m)
                xsplit(0)
                expert(0, True, False)
                with dve.Fori(1, EXPERTS - 1) as e:
                    expert(e, False, False)
                expert(EXPERTS - 1, False, True)
                y_out(EXPERTS - 1)


_OUTS = [((1, PROMPT, D), "float32"), ((1, SAMPLE, D), "float32")]


def bias_layout(rpb):
    padded = np.concatenate([rpb.reshape(HEADS, -1), np.full((HEADS, 1), NEG, rpb.dtype)], axis=1)
    off = rpb.shape[1] * rpb.shape[2]
    where = np.full((P, 3, BIAS_COLS), off, np.int64)
    for t0, qr0, kr0, rows, grid_rows, at in ROW_SETS:
        for j in (0, 1, 3):
            for q in range(P):
                r, cq = qr0 + q // Q_COLS, j * Q_COLS + q % Q_COLS
                rs = min(max(r - WIN_ROWS // 2, 0), grid_rows - WIN_ROWS)
                cs = min(max(cq - WIN_COLS // 2, 0), GRID_W - WIN_COLS)
                for kr in range(rs, rs + WIN_ROWS):
                    a = (kr - r + WIN_ROWS - 1) * (2 * WIN_COLS - 1) + (cs - cq + WIN_COLS - 1)
                    b = at + (kr - kr0) * K_COLS + cs - KEY_COL0[j]
                    where[q, PATTERN[j], b:b + WIN_COLS] = np.arange(a, a + WIN_COLS)
    return np.ascontiguousarray(padded[:, where])


def lay_out(inputs):
    a = {n: np.ascontiguousarray(inputs[n]) for n in (
        "x_prompt", "x_sample", "c_prompt", "c_sample", "ada_w", "ada_b", "norm1_g", "w_in", "w_out", "norm2_g",
        "w_router", "w_down")}
    a["ident"] = np.eye(P, dtype=np.float32)
    a["ones64"] = np.kron(np.eye(P // DH), np.full((DH, DH), 1.0 / DH)).astype(np.float32)
    a["qk_gain"] = np.stack([np.tile(np.asarray(inputs[n]), P // DH) for n in ("q_norm_g", "k_norm_g")], axis=1)
    per = np.concatenate([np.asarray(inputs["conv_w"])] + [np.asarray(inputs[n])[None] for n in
                         ("conv_b", "conv_ln_g", "conv_ln_b")], axis=0)
    a["conv_pack"] = np.ascontiguousarray(per.reshape(CONV_K + 3, 4, P).transpose(2, 1, 0))
    a["bias"] = bias_layout(np.asarray(inputs["rpb"]))
    gu = np.empty((EXPERTS, CHUNKS, P, 2, 2, KD, P), np.float32)
    for m, n in enumerate(("w_gate", "w_up")):
        w = np.asarray(inputs[n]).reshape(EXPERTS, P, KD, CHUNKS, 2, P)
        gu[:, :, :, m] = w.transpose(0, 3, 1, 4, 2, 5)
    a["w_gu"] = gu.reshape(EXPERTS, CHUNKS, P, 2, 2, KD * P)
    return a


def kernel(**inputs):
    import concourse.bacc as _bacc
    from concourse.bass_utils import run_bass_kernel_spmd as _run

    nc = _bacc.Bacc("TRN2", target_bir_lowering=False, num_devices=1)
    arrays, aps = {}, {}
    for name, a in lay_out(inputs).items():
        arrays[f"in_{name}"] = a
        aps[name] = nc.dram_tensor(f"in_{name}", a.shape, mybir.dt.from_np(a.dtype), kind="ExternalInput").ap()
    outs = [nc.dram_tensor(f"out_{i}", s, mybir.dt.from_np(np.dtype(d)), kind="ExternalOutput").ap()
            for i, (s, d) in enumerate(_OUTS)]
    program(nc, aps, outs)
    r = _run(nc, [arrays], core_ids=[0])
    return tuple(r.results[0][f"out_{i}"] for i in range(len(_OUTS)))
```
